# Optimizing a Trainium2 kernel written in Bass

```python
import jax, jax.numpy as jnp
from jax import lax
import numpy as np

D_MODEL = 1024
BATCH = 1
SEQ = 256
DEPTH = 2

GRID_W = 64
CTX_LEN = 256

MIX_HALF = D_MODEL // 2
RET_HEADS = 4
RET_DV = MIX_HALF // RET_HEADS
RET_DK = RET_DV // 2
RET_DECAY_BASE = 5
GLA_HEADS = 4
GLA_DV = MIX_HALF // GLA_HEADS
GLA_DK = GLA_DV // 2
GLA_GATE_RANK = 16
GLA_GATE_TAU = 16.0
SCAN_CHUNK = 64
RET_QK = RET_HEADS * RET_DK
RET_V = RET_HEADS * RET_DV
GLA_QK = GLA_HEADS * GLA_DK
GLA_V = GLA_HEADS * GLA_DV
EVEN_SPLITS = (RET_QK, RET_QK, RET_V, RET_V, GLA_QK, GLA_QK, GLA_V, GLA_V, 2 * GLA_GATE_RANK)
EVEN_PROJ = 2 * RET_QK + 2 * RET_V + 2 * GLA_QK + 2 * GLA_V + 2 * GLA_GATE_RANK

ATT_HEAD_DIM = 64
ATT_Q_HEADS = D_MODEL // ATT_HEAD_DIM
ATT_GROUP = 4
ATT_KV_HEADS = ATT_Q_HEADS // ATT_GROUP
WINDOW = 128
ATT_BLOCK = 128
ATT_QW = ATT_Q_HEADS * ATT_HEAD_DIM
ATT_KVW = ATT_KV_HEADS * ATT_HEAD_DIM
ATT_PROJ = ATT_QW + 2 * ATT_KVW
ROPE_BASE = 10000.0

D_FF = 4 * D_MODEL
DEEPNORM_ALPHA = (2.0 * DEPTH) ** 0.25
DEEPNORM_BETA = (8.0 * DEPTH) ** -0.25
LN_EPS = 1e-5
RMS_EPS = 1e-6
N_EVEN = (DEPTH + 1) // 2
N_ODD = DEPTH // 2


def layer_norm(x, g, b):
    xf = x.astype(jnp.float32)
    mu = jnp.mean(xf, axis=-1, keepdims=True)
    var = jnp.mean(jnp.square(xf - mu), axis=-1, keepdims=True)
    return ((xf - mu) * lax.rsqrt(var + LN_EPS) * g + b).astype(x.dtype)

def rms_norm(x, g=None):
    xf = x.astype(jnp.float32)
    y = xf * lax.rsqrt(jnp.mean(jnp.square(xf), axis=-1, keepdims=True) + RMS_EPS)
    if g is not None:
        y = y * g
    return y.astype(x.dtype)

def modulation(cvec, w, b):
    m = jax.nn.silu(cvec) @ w + b
    return jnp.split(m[..., None, :], 6, axis=-1)

def sublayer_residual(x, y, gate, g, b):
    return layer_norm(DEEPNORM_ALPHA * x + gate * y, g, b)

def split_cols(t, sizes):
    idx = np.cumsum(sizes)[:-1].tolist()
    return jnp.split(t, idx, axis=-1)

def split_heads(t, h):
    b, n, _ = t.shape
    return t.reshape(b, n, h, -1).transpose(0, 2, 1, 3)

def merge_heads(t):
    b, h, n, d = t.shape
    return t.transpose(0, 2, 1, 3).reshape(b, n, h * d)

def sq_relu_mlp(h, w1, w2):
    return jnp.square(jax.nn.relu(h @ w1)) @ w2

def chunk_gated_scan(q, k, v, log_a, s0, strict):
    f32 = jnp.float32
    B, H, T, dk = q.shape
    dv = v.shape[-1]
    n = T // SCAN_CHUNK
    qc = q.astype(f32).reshape(B, H, n, SCAN_CHUNK, dk)
    kc = k.astype(f32).reshape(B, H, n, SCAN_CHUNK, dk)
    vc = v.astype(f32).reshape(B, H, n, SCAN_CHUNK, dv)
    bcum = jnp.cumsum(log_a.astype(f32).reshape(B, H, n, SCAN_CHUNK, dk), axis=3)
    b_last = bcum[:, :, :, -1:, :]
    q_dec = qc * jnp.exp(bcum)
    k_inv = kc * jnp.exp(-bcum)
    k_end = kc * jnp.exp(b_last - bcum)
    mask = jnp.tril(jnp.ones((SCAN_CHUNK, SCAN_CHUNK), bool), k=-1 if strict else 0)
    scores = jnp.einsum('bhncd,bhnsd->bhncs', q_dec, k_inv)
    o_intra = jnp.einsum('bhncs,bhnse->bhnce', jnp.where(mask, scores, 0.0), vc)
    kv = jnp.einsum('bhnsd,bhnse->bhnde', k_end, vc)
    chunk_decay = jnp.exp(b_last[:, :, :, 0, :])

    def step(s, inp):
        kv_n, dec_n = inp
        return dec_n[..., None] * s + kv_n, s

    s_final, s_prev = lax.scan(step, s0.astype(f32),
                               (jnp.moveaxis(kv, 2, 0), jnp.moveaxis(chunk_decay, 2, 0)))
    s_prev = jnp.moveaxis(s_prev, 0, 2)
    o_inter = jnp.einsum('bhncd,bhnde->bhnce', q_dec, s_prev)
    o = (o_intra + o_inter).reshape(B, H, T, dv)
    return o.astype(v.dtype), s_final

def bidir_scan(q, k, v, log_a_f, log_a_b, s0_f, s0_b):
    flip = lambda t: jnp.flip(t, axis=2)
    o_f, s_f = chunk_gated_scan(q, k, v, log_a_f, s0_f, strict=False)
    o_b, s_b = chunk_gated_scan(flip(q), flip(k), flip(v), flip(log_a_b), s0_b, strict=True)
    return o_f + flip(o_b), s_f, s_b

def retention_gla_mixer(h, w_in, ret_theta, gla_gk_w, gla_gk_b, gla_norm_g, s0):
    f32 = jnp.float32
    qa, ka, va, ga, qb, kb, vb, gb, lr = split_cols(h @ w_in, EVEN_SPLITS)
    qa = split_heads(qa, RET_HEADS)
    ka = split_heads(ka, RET_HEADS) * RET_DK ** -0.5
    va = split_heads(va, RET_HEADS)
    log_gamma = jnp.log1p(-jnp.exp(ret_theta.astype(f32)))
    la_f = jnp.broadcast_to(log_gamma[0][None, :, None, None], qa.shape)
    la_b = jnp.broadcast_to(log_gamma[1][None, :, None, None], qa.shape)
    o_a, ra_f, ra_b = bidir_scan(qa, ka, va, la_f, la_b, s0[0], s0[1])
    y_a = jax.nn.silu(ga) * merge_heads(rms_norm(o_a))
    qb = split_heads(qb, GLA_HEADS) * GLA_DK ** -0.5
    kb = split_heads(kb, GLA_HEADS)
    vb = split_heads(vb, GLA_HEADS)
    lr_f, lr_b = jnp.split(lr, 2, axis=-1)

    def gate(u, w, b):
        z = (u @ w + b).astype(f32)
        return split_heads(jax.nn.log_sigmoid(z) / GLA_GATE_TAU, GLA_HEADS)

    o_b, sb_f, sb_b = bidir_scan(qb, kb, vb, gate(lr_f, gla_gk_w[0], gla_gk_b[0]),
                                 gate(lr_b, gla_gk_w[1], gla_gk_b[1]), s0[2], s0[3])
    y_b = jax.nn.silu(gb) * merge_heads(rms_norm(o_b, gla_norm_g))
    return jnp.concatenate([y_a, y_b], axis=-1), (ra_f, ra_b, sb_f, sb_b)

def axial_rope(t, row, col):
    f32 = jnp.float32
    half = ATT_HEAD_DIM // 2
    inv_freq = ROPE_BASE ** (-jnp.arange(0, half, 2, dtype=f32) / half)

    def rot(u, p):
        ang = p.astype(f32)[:, None] * inv_freq[None, :]
        cos, sin = jnp.cos(ang), jnp.sin(ang)
        u1, u2 = u[..., :half // 2], u[..., half // 2:]
        return jnp.concatenate([u1 * cos - u2 * sin, u1 * sin + u2 * cos], axis=-1)

    return jnp.concatenate([rot(t[..., :half], row), rot(t[..., half:], col)], axis=-1).astype(t.dtype)

def window_attention(q, k, v, k_c, v_c, sink):
    f32 = jnp.float32
    B, Hq, T, dh = q.shape
    nb = T // ATT_BLOCK
    scale = dh ** -0.5
    qb = q.reshape(B, ATT_KV_HEADS, ATT_GROUP, nb, ATT_BLOCK, dh)
    pad = ((0, 0), (0, 0), (ATT_BLOCK, ATT_BLOCK), (0, 0))
    kp = jnp.pad(k, pad).reshape(B, ATT_KV_HEADS, nb + 2, ATT_BLOCK, dh)
    vp = jnp.pad(v, pad).reshape(B, ATT_KV_HEADS, nb + 2, ATT_BLOCK, dh)
    kb = jnp.concatenate([kp[:, :, 0:nb], kp[:, :, 1:nb + 1], kp[:, :, 2:nb + 2]], axis=3)
    vb = jnp.concatenate([vp[:, :, 0:nb], vp[:, :, 1:nb + 1], vp[:, :, 2:nb + 2]], axis=3)
    qi = jnp.arange(ATT_BLOCK)[:, None]
    kj = jnp.arange(3 * ATT_BLOCK)[None, :]
    in_window = jnp.abs(kj - ATT_BLOCK - qi) <= WINDOW
    kpos = (jnp.arange(nb)[:, None] - 1) * ATT_BLOCK + jnp.arange(3 * ATT_BLOCK)[None, :]
    in_range = (kpos >= 0) & (kpos < T)
    valid = in_window[None] & in_range[:, None, :]
    s_loc = jnp.einsum('bkgnqd,bkncd->bkgnqc', qb, kb).astype(f32) * scale
    s_loc = jnp.where(valid, s_loc, -jnp.inf)
    s_ctx = jnp.einsum('bkgnqd,bkld->bkgnql', qb, k_c).astype(f32) * scale
    s_sink = sink.astype(f32).reshape(1, ATT_KV_HEADS, ATT_GROUP, 1, 1, 1)
    m = jnp.maximum(jnp.maximum(jnp.max(s_loc, -1, keepdims=True), jnp.max(s_ctx, -1, keepdims=True)), s_sink)
    e_loc = jnp.exp(s_loc - m)
    e_ctx = jnp.exp(s_ctx - m)
    denom = jnp.sum(e_loc, -1, keepdims=True) + jnp.sum(e_ctx, -1, keepdims=True) + jnp.exp(s_sink - m)
    o = (jnp.einsum('bkgnqc,bkncd->bkgnqd', e_loc, vb.astype(f32))
         + jnp.einsum('bkgnql,bkld->bkgnqd', e_ctx, v_c.astype(f32))) / denom
    return o.reshape(B, Hq, T, dh).astype(q.dtype)

def context_attention(q_c, k_c, v_c, sink):
    f32 = jnp.float32
    B, Hq, L, dh = q_c.shape
    qg = q_c.reshape(B, ATT_KV_HEADS, ATT_GROUP, L, dh)
    s = jnp.einsum('bkgqd,bkld->bkgql', qg, k_c).astype(f32) * dh ** -0.5
    s_sink = jnp.broadcast_to(sink.astype(f32).reshape(1, ATT_KV_HEADS, ATT_GROUP, 1, 1), s.shape[:-1] + (1,))
    p = jax.nn.softmax(jnp.concatenate([s, s_sink], axis=-1), axis=-1)[..., :L]
    return jnp.einsum('bkgql,bkld->bkgqd', p, v_c.astype(f32)).reshape(B, Hq, L, dh).astype(q_c.dtype)

def first_inputs(seed: int = 0) -> dict:
    key = jax.random.key(seed)
    ks = jax.random.split(key, 19)
    f32 = jnp.float32
    D = D_MODEL

    def nrm(k, shape, fan_in, scale=1.0):
        return jax.random.normal(k, shape, f32) * (scale * fan_in ** -0.5)

    ret_init = -(RET_DECAY_BASE + jnp.arange(RET_HEADS, dtype=f32)) * jnp.log(2.0)
    return {
        'x': jax.random.normal(ks[0], (BATCH, SEQ, D), f32),
        'c': jax.random.normal(ks[1], (BATCH, D), f32),
        'ctx': jax.random.normal(ks[2], (BATCH, CTX_LEN, D), f32),
        'c_ctx': jax.random.normal(ks[3], (D,), f32),
        'w_mod': nrm(ks[4], (DEPTH, D, 6 * D), D),
        'b_mod': 0.02 * jax.random.normal(ks[5], (DEPTH, 6 * D), f32),
        'ln_g': 1.0 + 0.02 * jax.random.normal(ks[6], (DEPTH, 2, D), f32),
        'ln_b': 0.02 * jax.random.normal(ks[7], (DEPTH, 2, D), f32),
        'mlp_w1': nrm(ks[8], (DEPTH, D, D_FF), D),
        'mlp_w2': nrm(ks[9], (DEPTH, D_FF, D), D_FF, DEEPNORM_BETA),
        'ev_w_in': nrm(ks[10], (N_EVEN, D, EVEN_PROJ), D),
        'ev_ret_theta': ret_init + 0.05 * jax.random.normal(ks[11], (N_EVEN, 2, RET_HEADS), f32),
        'ev_gla_gk_w': nrm(ks[12], (N_EVEN, 2, GLA_GATE_RANK, GLA_QK), GLA_GATE_RANK),
        'ev_gla_gk_b': 0.02 * jax.random.normal(ks[13], (N_EVEN, 2, GLA_QK), f32),
        'ev_gla_norm_g': 1.0 + 0.02 * jax.random.normal(ks[14], (N_EVEN, GLA_DV), f32),
        'ev_w_out': nrm(ks[15], (N_EVEN, D, D), D, DEEPNORM_BETA),
        'od_w_qkv': nrm(ks[16], (N_ODD, D, ATT_PROJ), D),
        'od_sink': 0.5 * jax.random.normal(ks[17], (N_ODD, ATT_Q_HEADS), f32),
        'od_w_out': nrm(ks[18], (N_ODD, D, D), D, DEEPNORM_BETA),
    }

def first_block(x, c, ctx, c_ctx, w_mod, b_mod, ln_g, ln_b, mlp_w1, mlp_w2,
              ev_w_in, ev_ret_theta, ev_gla_gk_w, ev_gla_gk_b, ev_gla_norm_g, ev_w_out,
              od_w_qkv, od_sink, od_w_out):
    B, T, _ = x.shape
    rows = T // GRID_W
    row = jnp.repeat(jnp.arange(rows), GRID_W)
    col = jnp.tile(jnp.arange(GRID_W), rows)
    xc = ctx
    for i in range(DEPTH):
        last = i == DEPTH - 1
        j = i // 2
        sh1, sc1, g1, sh2, sc2, g2 = modulation(c, w_mod[i], b_mod[i])
        csh1, csc1, cg1, csh2, csc2, cg2 = modulation(c_ctx, w_mod[i], b_mod[i])
        h = x * (1.0 + sc1) + sh1
        hc = xc * (1.0 + csc1) + csh1
        if i % 2 == 0:
            prm = (ev_w_in[j], ev_ret_theta[j], ev_gla_gk_w[j], ev_gla_gk_b[j], ev_gla_norm_g[j])
            s0 = (jnp.zeros((B, RET_HEADS, RET_DK, RET_DV), jnp.float32),
                  jnp.zeros((B, RET_HEADS, RET_DK, RET_DV), jnp.float32),
                  jnp.zeros((B, GLA_HEADS, GLA_DK, GLA_DV), jnp.float32),
                  jnp.zeros((B, GLA_HEADS, GLA_DK, GLA_DV), jnp.float32))
            yc, ctx_states = retention_gla_mixer(hc, *prm, s0)
            y, _ = retention_gla_mixer(h, *prm, ctx_states)
            y = y @ ev_w_out[j]
            if not last:
                yc = yc @ ev_w_out[j]
        else:
            w = od_w_qkv[j]
            q, k, v = split_cols(h @ w, (ATT_QW, ATT_KVW, ATT_KVW))
            q = axial_rope(split_heads(q, ATT_Q_HEADS), row, col)
            k = axial_rope(split_heads(k, ATT_KV_HEADS), row, col)
            v = split_heads(v, ATT_KV_HEADS)
            k_c, v_c = split_cols(hc @ w[:, ATT_QW:], (ATT_KVW, ATT_KVW))
            k_c = split_heads(k_c, ATT_KV_HEADS)
            v_c = split_heads(v_c, ATT_KV_HEADS)
            y = merge_heads(window_attention(q, k, v, k_c, v_c, od_sink[j])) @ od_w_out[j]
            if not last:
                q_c = split_heads(hc @ w[:, :ATT_QW], ATT_Q_HEADS)
                yc = merge_heads(context_attention(q_c, k_c, v_c, od_sink[j])) @ od_w_out[j]
        x = sublayer_residual(x, y, g1, ln_g[i, 0], ln_b[i, 0])
        x = sublayer_residual(x, sq_relu_mlp(x * (1.0 + sc2) + sh2, mlp_w1[i], mlp_w2[i]), g2, ln_g[i, 1], ln_b[i, 1])
        if not last:
            xc = sublayer_residual(xc, yc, cg1, ln_g[i, 0], ln_b[i, 0])
            xc = sublayer_residual(xc, sq_relu_mlp(xc * (1.0 + csc2) + csh2, mlp_w1[i], mlp_w2[i]), cg2, ln_g[i, 1], ln_b[i, 1])
    return x


DEPTH_2 = 1

CHUNK = 64
QBLK = 128
EPS = 1e-6

REC_HEADS = 4
REC_DK = 128
REC_DV = 128
REC_W = REC_HEADS * REC_DV
ATT_HEADS = 8
ATT_DH = 64
ATT_W = ATT_HEADS * ATT_DH
IDX_HEADS = 8
IDX_DIM = 64
TOPK_MAX = 256
NUM_BUCKETS = 32
MAX_DISTANCE = 128
N_GROUPS = 4
EXPERTS_PER_GROUP = 4
N_EXPERTS = N_GROUPS * EXPERTS_PER_GROUP
TOP_K_EXPERTS = 2
D_EXPERT = 512

MIX_W = REC_W + ATT_W
IN_SIZES = (REC_HEADS * REC_DK,
            REC_HEADS * REC_DK,
            REC_W,
            REC_W,
            ATT_W, ATT_W, ATT_W,
            IDX_HEADS * IDX_DIM,
            IDX_DIM,
            IDX_HEADS)
D_IN = int(sum(IN_SIZES))
IN_OFFSETS = tuple(int(o) for o in np.cumsum(IN_SIZES)[:-1])


def _rms(x, g):
    xf = x.astype(jnp.float32)
    y = xf * lax.rsqrt(jnp.mean(xf * xf, axis=-1, keepdims=True) + EPS)
    return (y * g.astype(jnp.float32)).astype(x.dtype)

def _layernorm(x, g, b):
    xf = x.astype(jnp.float32)
    mu = jnp.mean(xf, axis=-1, keepdims=True)
    var = jnp.mean(jnp.square(xf - mu), axis=-1, keepdims=True)
    y = (xf - mu) * lax.rsqrt(var + EPS)
    return (y * g.astype(jnp.float32) + b.astype(jnp.float32)).astype(x.dtype)

def _t5_bucket(rel):
    nb = NUM_BUCKETS // 2
    max_exact = nb // 2
    ret = jnp.where(rel > 0, nb, 0)
    n = jnp.abs(rel)
    nf = jnp.maximum(n, 1).astype(jnp.float32)
    large = max_exact + (jnp.log(nf / max_exact) / np.log(MAX_DISTANCE / max_exact)
                         * (nb - max_exact)).astype(jnp.int32)
    large = jnp.minimum(large, nb - 1)
    return ret + jnp.where(n < max_exact, n, large)

def _hgrn2(q_raw, f_raw, i_raw, g_raw, lb, out_g):
    B, S, _ = q_raw.shape
    nc = S // CHUNK
    f32 = jnp.float32
    q = jax.nn.silu(q_raw.astype(f32))
    f = lb + (1.0 - lb) * jax.nn.sigmoid(f_raw.astype(f32))
    k = 1.0 - f
    lf = jnp.log(f)
    v = i_raw.astype(f32)

    def to_chunks(a, d):
        return a.reshape(B, nc, CHUNK, REC_HEADS, d).transpose(1, 0, 3, 2, 4)

    tril = jnp.tril(jnp.ones((CHUNK, CHUNK), bool))[:, :, None]

    def step(state, inp):
        qc, kc, vc, lfc = inp
        b = jnp.cumsum(lfc, axis=2)
        diff = b[:, :, :, None, :] - b[:, :, None, :, :]
        decay = jnp.where(tril, jnp.exp(jnp.where(tril, diff, 0.0)), 0.0)
        attn = jnp.einsum('bhtk,bhsk,bhtsk->bhts', qc, kc, decay)
        o = (jnp.einsum('bhts,bhsv->bhtv', attn, vc)
             + jnp.einsum('bhtk,bhkv->bhtv', qc * jnp.exp(b), state))
        b_end = b[:, :, -1:, :]
        state = (jnp.exp(b_end[:, :, 0, :])[..., None] * state
                 + jnp.einsum('bhsk,bhsv->bhkv', kc * jnp.exp(b_end - b), vc))
        return state, o

    s0 = jnp.zeros((B, REC_HEADS, REC_DK, REC_DV), f32)
    _, o = lax.scan(step, s0, (to_chunks(q, REC_DK), to_chunks(k, REC_DK),
                               to_chunks(v, REC_DV), to_chunks(lf, REC_DK)))
    o = o.transpose(1, 0, 3, 2, 4).reshape(B, S, REC_HEADS, REC_DV)
    o = _rms(o, out_g.reshape(REC_HEADS, REC_DV))
    gate = jax.nn.silu(g_raw.astype(f32)).reshape(B, S, REC_HEADS, REC_DV)
    return (o * gate).reshape(B, S, REC_W).astype(q_raw.dtype)

def _dsa_attention(q, k, v, iq, ik, iw, rel_bias):
    B, S = q.shape[0], q.shape[1]
    nb = S // QBLK
    k_sel = min(TOPK_MAX, S // 4)
    key_chunk = jnp.arange(S) // CHUNK
    ikf = ik.astype(jnp.float32)

    def blocks(a):
        return a.reshape((B, nb, QBLK) + a.shape[2:]).swapaxes(0, 1)

    def one_block(args):
        bi, qb, iqb, iwb = args
        t = bi * QBLK + jnp.arange(QBLK)
        t_chunk = t // CHUNK
        sc = jnp.einsum('bqhd,bsd->bqhs', iqb.astype(jnp.float32), ikf) * IDX_DIM ** -0.5
        score = jnp.einsum('bqhs,bqh->bqs', jax.nn.relu(sc), iwb.astype(jnp.float32))
        adm = key_chunk[None, :] <= t_chunk[:, None]
        score = jnp.where(adm[None], score, -jnp.inf)
        _, idx = lax.top_k(score, k_sel)
        valid = (idx // CHUNK) <= t_chunk[None, :, None]
        kg = jax.vmap(lambda a, j: a[j])(k, idx)
        vg = jax.vmap(lambda a, j: a[j])(v, idx)
        logits = jnp.einsum('bqhd,bqkhd->bqhk', qb, kg).astype(jnp.float32) * ATT_DH ** -0.5
        bias = rel_bias[_t5_bucket(idx - t[None, :, None])]
        logits = logits + jnp.swapaxes(bias, 2, 3).astype(jnp.float32)
        logits = jnp.where(valid[:, :, None, :], logits, -jnp.inf)
        p = jax.nn.softmax(logits, axis=-1).astype(vg.dtype)
        return jnp.einsum('bqhk,bqkhd->bqhd', p, vg)

    out = lax.map(one_block, (jnp.arange(nb), blocks(q), blocks(iq), blocks(iw)))
    return out.swapaxes(0, 1).reshape(B, S, ATT_HEADS, ATT_DH)

def _hier_moe(h, w_rg, b_rg, w_re, b_re, w1, w3, w2):
    B, S, D = h.shape
    hf = h.reshape(B * S, D)
    g_logits = (hf @ w_rg + b_rg).astype(jnp.float32)
    p_group = jax.nn.softmax(g_logits, axis=-1)
    g_top = jnp.argmax(g_logits, axis=-1)
    gate_g = jnp.take_along_axis(p_group, g_top[:, None], axis=-1)
    e_logits = (hf @ w_re + b_re).astype(jnp.float32).reshape(-1, N_GROUPS, EXPERTS_PER_GROUP)
    e_in = jnp.take_along_axis(e_logits, g_top[:, None, None], axis=1)[:, 0]
    top_v, top_j = lax.top_k(e_in, TOP_K_EXPERTS)
    w_sel = jax.nn.softmax(top_v, axis=-1) * gate_g
    e_id = g_top[:, None] * EXPERTS_PER_GROUP + top_j
    combine = jnp.einsum('nk,nke->ne', w_sel,
                         jax.nn.one_hot(e_id, N_EXPERTS, dtype=jnp.float32)).astype(h.dtype)
    y = jnp.zeros_like(hf)
    for e in range(N_EXPERTS):
        he = jax.nn.silu(hf @ w1[e]) * (hf @ w3[e])
        y = y + combine[:, e:e + 1] * (he @ w2[e])
    return y.reshape(B, S, D)

def second_inputs(seed: int = 0) -> dict:
    key = jax.random.key(seed)
    ks = jax.random.split(key, 24)
    f32 = jnp.float32

    def nrm(k, shape, s):
        return jax.random.normal(k, shape, f32) * s

    D = D_MODEL
    return {
        'x': nrm(ks[0], (BATCH, SEQ, D), 1.0),
        'c': nrm(ks[1], (BATCH, D), 1.0),
        'w_ada': nrm(ks[2], (DEPTH_2, D, 6 * D), 0.5 * D ** -0.5),
        'b_ada': nrm(ks[3], (DEPTH_2, 6 * D), 0.02),
        'norm1_g': 1.0 + nrm(ks[4], (DEPTH_2, D), 0.02),
        'norm2_g': 1.0 + nrm(ks[5], (DEPTH_2, D), 0.02),
        'w_in': nrm(ks[6], (DEPTH_2, D, D_IN), D ** -0.5),
        'lb_logits': nrm(ks[7], (DEPTH_2 + 1, REC_HEADS * REC_DK), 0.5),
        'rec_out_g': 1.0 + nrm(ks[8], (DEPTH_2, REC_W), 0.02),
        'q_norm_g': 1.0 + nrm(ks[9], (DEPTH_2, ATT_DH), 0.02),
        'k_norm_g': 1.0 + nrm(ks[10], (DEPTH_2, ATT_DH), 0.02),
        'idx_k_norm_g': 1.0 + nrm(ks[11], (DEPTH_2, IDX_DIM), 0.02),
        'idx_k_norm_b': nrm(ks[12], (DEPTH_2, IDX_DIM), 0.02),
        'attn_out_g': 1.0 + nrm(ks[13], (DEPTH_2, ATT_W), 0.02),
        'rel_bias': nrm(ks[14], (NUM_BUCKETS, ATT_HEADS), 0.5),
        'w_out': nrm(ks[15], (DEPTH_2, MIX_W, D), MIX_W ** -0.5),
        'w_rg': nrm(ks[16], (DEPTH_2, D, N_GROUPS), D ** -0.5),
        'b_rg': nrm(ks[17], (DEPTH_2, N_GROUPS), 0.01),
        'w_re': nrm(ks[18], (DEPTH_2, D, N_EXPERTS), D ** -0.5),
        'b_re': nrm(ks[19], (DEPTH_2, N_EXPERTS), 0.01),
        'w1': nrm(ks[20], (DEPTH_2, N_EXPERTS, D, D_EXPERT), D ** -0.5),
        'w3': nrm(ks[21], (DEPTH_2, N_EXPERTS, D, D_EXPERT), D ** -0.5),
        'w2': nrm(ks[22], (DEPTH_2, N_EXPERTS, D_EXPERT, D), D_EXPERT ** -0.5),
    }

def second_block(x, c, w_ada, b_ada, norm1_g, norm2_g, w_in, lb_logits, rec_out_g,
              q_norm_g, k_norm_g, idx_k_norm_g, idx_k_norm_b, attn_out_g, rel_bias,
              w_out, w_rg, b_rg, w_re, b_re, w1, w3, w2):
    B, S, D = x.shape
    lb_all = jnp.cumsum(jax.nn.softmax(lb_logits.astype(jnp.float32), axis=0), axis=0)
    for l in range(DEPTH_2):
        mod = jax.nn.silu(c) @ w_ada[l] + b_ada[l]
        sh1, sc1, g1, sh2, sc2, g2 = jnp.split(mod, 6, axis=-1)

        h = _rms(x, norm1_g[l]) * (1.0 + sc1[:, None, :]) + sh1[:, None, :]
        z = h @ w_in[l]
        rq, rf, ri, rg, aq, ak, av, iq, ik, iw = jnp.split(z, IN_OFFSETS, axis=-1)

        rec = _hgrn2(rq, rf, ri, rg, lb_all[l], rec_out_g[l])

        aq = _rms(aq.reshape(B, S, ATT_HEADS, ATT_DH), q_norm_g[l])
        ak = _rms(ak.reshape(B, S, ATT_HEADS, ATT_DH), k_norm_g[l])
        av = av.reshape(B, S, ATT_HEADS, ATT_DH)
        iq = iq.reshape(B, S, IDX_HEADS, IDX_DIM)
        ik = _layernorm(ik, idx_k_norm_g[l], idx_k_norm_b[l])
        iw = iw * IDX_HEADS ** -0.5
        att = _dsa_attention(aq, ak, av, iq, ik, iw, rel_bias)
        att = _rms(att, attn_out_g[l].reshape(ATT_HEADS, ATT_DH)).reshape(B, S, ATT_W)

        mix = jnp.concatenate([rec, att.astype(rec.dtype)], axis=-1) @ w_out[l]
        x = x + g1[:, None, :] * mix

        h2 = _rms(x, norm2_g[l]) * (1.0 + sc2[:, None, :]) + sh2[:, None, :]
        x = x + g2[:, None, :] * _hier_moe(h2, w_rg[l], b_rg[l], w_re[l], b_re[l],
                                           w1[l], w3[l], w2[l])
    return x


def setup_inputs(seed=0):
    out = dict(first_inputs(seed))
    for name, value in second_inputs(seed + 1).items():
        if name != "x":
            out[name + "_2"] = value
    return out


def reference(
    x, c, ctx, c_ctx, w_mod, b_mod, ln_g, ln_b, mlp_w1, mlp_w2, ev_w_in, ev_ret_theta,
    ev_gla_gk_w, ev_gla_gk_b, ev_gla_norm_g, ev_w_out, od_w_qkv, od_sink, od_w_out, c_2,
    w_ada_2, b_ada_2, norm1_g_2, norm2_g_2, w_in_2, lb_logits_2, rec_out_g_2, q_norm_g_2,
    k_norm_g_2, idx_k_norm_g_2, idx_k_norm_b_2, attn_out_g_2, rel_bias_2, w_out_2, w_rg_2,
    b_rg_2, w_re_2, b_re_2, w1_2, w3_2, w2_2,
):
    x = first_block(
        x, c, ctx, c_ctx, w_mod, b_mod, ln_g, ln_b, mlp_w1, mlp_w2, ev_w_in, ev_ret_theta,
        ev_gla_gk_w, ev_gla_gk_b, ev_gla_norm_g, ev_w_out, od_w_qkv, od_sink, od_w_out,
    )
    return second_block(
        x, c_2, w_ada_2, b_ada_2, norm1_g_2, norm2_g_2, w_in_2, lb_logits_2, rec_out_g_2,
        q_norm_g_2, k_norm_g_2, idx_k_norm_g_2, idx_k_norm_b_2, attn_out_g_2, rel_bias_2,
        w_out_2, w_rg_2, b_rg_2, w_re_2, b_re_2, w1_2, w3_2, w2_2,
    )


_drawn_inputs = setup_inputs


def setup_inputs(seed=0):
    import zlib

    import numpy as np

    out = dict(_drawn_inputs(seed))
    spreads = {}
    factors = {'ev_gla_gk_b': 8.0,
     'ev_gla_norm_g': 8.0,
     'od_sink': 8.0,
     'norm1_g_2': 4.004,
     'norm2_g_2': 7.382,
     'lb_logits_2': 7.178,
     'rec_out_g_2': 8.0,
     'q_norm_g_2': 8.0,
     'k_norm_g_2': 8.0,
     'idx_k_norm_g_2': 6.263,
     'idx_k_norm_b_2': 7.14,
     'attn_out_g_2': 8.0,
     'b_rg_2': 8.0,
     'b_re_2': 28.753}
    for name, (base, spread) in spreads.items():
        noise = np.random.default_rng([zlib.crc32(name.encode()), seed]).standard_normal(out[name].shape)
        drawn = base * np.exp(spread * noise) if base else spread * noise
        out[name] = __import__('jax').numpy.asarray(drawn.astype(out[name].dtype))
    for name, factor in factors.items():
        out[name] = (out[name] * factor).astype(out[name].dtype)
    return out
```

```python
from contextlib import ExitStack

import numpy as np

import concourse.bass as bass
from concourse import mybir

ALU = mybir.AluOpType
ACT = mybir.ActivationFunctionType
AX = mybir.AxisListType
F32 = mybir.dt.float32
I32 = mybir.dt.int32

P = 128
D = 1024
KC = D // P
T = 256
NT = 4
X0 = 2
DFF = 4 * D
ALPHA = 4.0 ** 0.25
LN_EPS = 1e-5
RMS_EPS = 1e-6
RING = 4
BANKS = 8
HD = 64
NEXP = 16
BODY = 4
NEG = -1.0e30
INADMISSIBLE = -2.0e38
TAKEN = -3.0e38
NBUCKET = 32
MIDREF = P // 2


CONST_COLS = {}


def _place(names):
    at = 0
    for name, width in names:
        CONST_COLS[name] = (at, at + width)
        at += width
    return at


CONST_W = _place([("ident", P), ("cum_f", P), ("cum_b", P), ("dec_f", 3), ("dec_b", 3), ("perm", P),
                  ("win0", P), ("win1", P), ("pick", 4),
                  ("ones", 1)])
LEVELS = [64, 32, 16, 8, 4, 2, 1]
LEVEL_W = P * len(LEVELS) + 4 * T


def shape_constants():
    c = np.zeros((P, CONST_W), np.float32)
    r, t = np.arange(P)[:, None], np.arange(P)[None, :]

    def put(name, value):
        a, b = CONST_COLS[name]
        c[:, a:b] = value

    put("ident", r == t)
    first_f, first_b = (r < MIDREF), (r >= MIDREF)
    put("cum_f", ((r <= t) * 1.0 - first_f) / 16.0)
    put("cum_b", ((r >= t) * 1.0 - first_b) / 16.0)
    put("dec_f", np.concatenate([first_f, ~first_f, np.ones((P, 1))], 1) / 16.0)
    put("dec_b", np.concatenate([first_b, ~first_b, np.ones((P, 1))], 1) / 16.0)
    d = np.arange(P) % 32
    perm = np.zeros((P, P))
    for m in range(P):
        if m % 32 < 16:
            perm[m + 16, m] = -1.0
        else:
            perm[m - 16, m] = 1.0
    put("perm", perm)
    inv = (10000.0 ** (-np.arange(0, 32, 2) / 32.0)).astype(np.float32)
    tok = np.arange(T)
    pos = np.where((np.arange(P)[:, None] % 64) < 32, tok[None, :] // 64, tok[None, :] % 64).astype(np.float32)
    ang = (pos * inv[d % 16][:, None]).astype(np.float32)
    rope = np.concatenate([np.cos(ang.astype(np.float64)), np.sin(ang.astype(np.float64))], 1).astype(np.float32)
    put("win0", np.where(t > r, NEG, 0.0))
    put("win1", np.where(r > t, NEG, 0.0))
    put("pick", np.array([[4.0, 3.0, 2.0, 1.0]]))
    put("ones", 1.0)
    lv = np.zeros((P, LEVEL_W), np.float32)
    for n, size in enumerate(LEVELS):
        same = (r // (2 * size)) == (t // (2 * size))
        lv[:, n * P:(n + 1) * P] = same & (r % (2 * size) < size) & (t % (2 * size) >= size)
    go = np.ones(4 * T)
    go[::P] = 0.0
    lv[:, len(LEVELS) * P:] = go
    rel = (T - 1) - np.arange(2 * T - 1)
    n = np.abs(rel)
    large = 8 + np.floor(np.log2(np.maximum(n, 1) / 8.0) * 2 + 1e-9).astype(int)
    bucket = np.where(rel > 0, 16, 0) + np.where(n < 8, n, np.minimum(large, 15))
    hot = (bucket[None, :] == np.arange(NBUCKET)[:, None]).astype(np.float32)
    return {"const_main": c, "const_rope": rope, "const_levels": lv, "const_buckets": hot}


def _deal(chunks, counts):
    chunks = list(chunks)
    return [[chunks.pop(0) for _ in range(n)] for n in counts]


BESIDE = {
    "ev_in": _deal([(0, c) for c in range(4, 12)], (1, 2, 1, 2, 1, 1, 0)),
    "up0": _deal([(1, c) for c in range(12)] + [(2, c) for c in range(4)], (3, 2, 2, 3, 2, 2, 2, 0)),
    "up1": _deal([(2, c) for c in range(4, 12)], (1, 1, 1, 1, 1, 1, 2, 0)),
}
SUMMED = [m for name in ("ev_in", "up0", "up1") for group in BESIDE[name] for m in group]


def vectors(l):
    return 2 if l < 2 else 1


def weight_stream():
    def part(name, lo, hi):
        return [(name, c) for c in range(lo, hi)]

    def with_mods(name, n):
        s = []
        for c in range(n):
            s += [(name, c)] + [(f"mod{l}", m) for l, m in BESIDE[name][c]]
        return s

    return (part("mod0", 0, 4) + with_mods("ev_in", 7) + part("out0", 0, 2)
            + with_mods("up0", 8) + part("down0", 0, 8) + part("od_qkv", 0, 3)
            + part("out1", 0, 2) + with_mods("up1", 8) + part("down1", 0, 8)
            + part("w_in", 0, 9) + part("out2", 0, 2))


def build(nc, I, out):
    STREAM = weight_stream()
    load_no = {key: n for n, key in enumerate(STREAM)}
    MOE_LOAD0 = len(STREAM)
    LOADS_PER_TURN = 3 * BODY
    TURNS = NEXP // BODY

    with ExitStack() as ctx:
        def sb(name, shape, dt=F32):
            return ctx.enter_context(nc.sbuf_tensor(name, shape, dt))

        def sem(name):
            return ctx.enter_context(nc.semaphore(name))

        psum = ctx.enter_context(nc.psum_tensor("psum", [P, BANKS, 512], F32))
        wring = sb("wring", [P, RING, KC, 512])
        xres = sb("xres", [P, NT, D])
        hT = sb("hT", [P, KC, 512])
        big = sb("big", [P, 16384])
        gate = sb("gate", [P, 2, D])
        lnb = sb("lnb", [P, 2, D])
        tmp = sb("tmp", [P, 22 * 256])
        const = sb("const", [P, CONST_W])
        cols = sb("cols", [P, 192])
        csilu = sb("csilu", [P, 24])
        modc = sb("modc", [P, 3, 6 * KC, 2])
        small = sb("small", [P, 576])

        def cst(name, rows=P):
            a, b = CONST_COLS[name]
            return const[0:rows, a:b]

        ident = cst("ident")

        def region(base, at, *shape):
            n = int(np.prod(shape))
            v = base[:, at:at + n]
            if len(shape) == 1:
                return v
            names = "abcd"[:len(shape)]
            return v.rearrange(f"p ({' '.join(names)}) -> p {' '.join(names)}",
                               **{names[i]: shape[i] for i in range(1, len(shape))})

        CARRY = {(0, 1): 0, (0, 2): 1, (0, 3): 2, (1, 0): 3, (1, 3): 4, (1, 2): 5}
        qkT = region(big, 0, 8, 512)
        vtok = region(big, 4096, NT, D)
        gtok = region(big, 8192, NT, D)
        qd = region(big, 12288, 8, 512)
        kd = hT
        yT = region(big, 0, KC, 512)
        h1T = region(big, 0, 32, 512)
        rows1 = region(big, 0, P)
        rows2 = region(big, P, P)
        exp_ret = region(tmp, 0, 2, 4, P)
        exp_gla = region(tmp, 1024, 2, 4, P)
        amask = region(tmp, 0, 8, P)
        sq = region(tmp, 1024, 4, P)
        sqb = region(tmp, 1536, 512)
        la = region(tmp, 2048, 512)
        modrow = region(tmp, 0, 4, 512)
        modsum = region(tmp, 2560, 2, 2, 512)
        carried = region(tmp, 2560, 6, 512)
        roll = {0: CARRY[(0, 3)], 1: CARRY[(1, 2)]}
        ktok = region(lnb[:, :, :].rearrange("p a b -> p (a b)"), 0, 8, P)
        zabs = region(lnb[:, :, :].rearrange("p a b -> p (a b)"), 1024, 512)
        zlog = zabs
        gkw = region(gate[:, :, :].rearrange("p a b -> p (a b)"), 0, 512)
        la_ret = region(gate[:, :, :].rearrange("p a b -> p (a b)"), 512, 512)
        normg = region(gate[:, :, :].rearrange("p a b -> p (a b)"), 1024, P)
        theta = region(gate[:, :, :].rearrange("p a b -> p (a b)"), 1152, 8)
        dec = region(gate[:, :, :].rearrange("p a b -> p (a b)"), 1160, NT, 2, 4, 3)
        lrT = region(gate[:, :, :].rearrange("p a b -> p (a b)"), 1280, 512)
        q_raw = region(big, 0, 8, T)
        k_raw = region(big, 2048, 2, T)
        qT = region(big, 2560, 8, T)
        kT = region(big, 4608, 2, 512)
        kTx = region(big, 14848, 2, 512)
        v1 = region(big, 5632, NT, T)
        rope = region(big, 14336, 2, T)
        e1 = region(big, 6656, 4, 512)
        rope_t = region(big, 6656, 512)
        eT1 = region(big, 8704, 4, 512)
        y1 = region(big, 12288, 2, D)
        yT1 = region(big, 0, KC, T)
        sinkb = region(small, 0, 16)
        mx1 = region(small, 16, 4)
        negm1 = region(small, 20, 4)
        den1 = region(small, 24, 32)
        sexp1 = region(small, 56, 4)
        lnstat = region(small, 64, 2, 6)
        lnagg = region(small, 76, 2)
        lnr = region(small, 78, 1)
        hsum = region(small, 80, 8)
        rqT = region(big, 0, 4, T)
        rkT = region(big, 1024, 4, T)
        rb = region(big, 2048, 4, T)
        rsig = region(big, 3072, 4, T)
        rv = region(big, 4096, 2, 512)
        rg = region(big, 5120, 2, 512)
        aq = region(big, 6144, 2, 512)
        ak = region(big, 7168, 2, 512)
        av = region(big, 8192, 2, 512)
        iqT = region(big, 9216, 4, T)
        aqT = region(big, 10240, 4, T)
        akT = region(big, 11264, 4, T)
        mix = region(big, 12288, 2, D)
        ikd = region(big, 14336, 2, P)
        ikT = region(big, 14592, T)
        score = region(big, 14848, 2, T)
        work = region(big, 15360, 2, T)
        ikn = region(big, 15872, P)
        qkg = region(big, 16000, P)
        iwt = region(big, 16128, 2, 8)
        levels = region(tmp, 0, LEVEL_W)
        sc_r = region(tmp, 1920, 2, T)
        edec = region(tmp, 2432, 4, T)
        ql = region(tmp, 3456, 4, T)
        kl = region(tmp, 4480, 4, T)
        amat = region(hT[:, :, :].rearrange("p a b -> p (a b)"), 0, 2, 4, P)
        across = region(hT[:, :, :].rearrange("p a b -> p (a b)"), 1024, 4, P)
        rowg = region(hT[:, :, :].rearrange("p a b -> p (a b)"), 1536, 2, 512)
        relE = region(hT[:, :, :].rearrange("p a b -> p (a b)"), 2560, 512)
        relb = region(small, 520, 8)
        hot = region(big, 14848, 2 * T - 1)
        biasT = region(tmp, 0, 8, T)
        logit = region(tmp, 2048, 8, T)
        eT2 = region(big, 2048, 4, 512)
        yT2 = region(big, 0, KC, T)
        negsel = work
        sq2 = region(tmp, 1920, 512)
        ubuf = region(tmp, 5120, 512)
        ubuf2 = region(tmp, 2048, 512)
        ubuf3 = region(big, 14848, 512)
        junk = region(small, 575, 1)
        half_neg = region(small, 528, 8)
        lbc = region(small, 96, 4)
        olb = region(small, 100, 4)
        mod3 = region(small, 104, 8)
        st8 = region(small, 112, 8)
        max8 = region(small, 120, 8)
        mx2 = region(small, 128, 8)
        neg2 = region(small, 136, 8)
        den2 = region(small, 144, 8)
        ik_st = region(small, 152, 6)
        ik_ag = region(small, 158, 2)
        xn = region(tmp, 0, 2, D)
        wr = region(small, 176, KC, 20)
        brr = region(small, 336, 20)
        lg = region(small, 356, 2, 20)
        comb = region(small, 396, 2, NEXP)
        rt_p = region(small, 428, 32)
        rt_g = region(small, 460, 2)
        rt_m = region(small, 462, 2)
        rt_1 = region(small, 464, 2)
        rt_2 = region(small, 466, 2)
        rt_hg = region(small, 468, 2, 4)
        rt_h1 = region(small, 476, 2, 4)
        rt_h2 = region(small, 484, 2, 4)
        rt_e = region(small, 492, 2, 4)
        rt_e2 = region(small, 500, 2, 4)
        rt_exp = region(small, 508, 10)
        sg = region(big, 2048, 2, 4, T)
        he = region(big, 4096, 2, 4, T)
        yacc = region(big, 8192, 2, D)

        rel_scratch = nc.dram_tensor("rel_scratch", [8, 2 * T - 1], F32, kind="Internal").ap()

        w_landed = [sem(f"w_landed{s}") for s in range(RING)]
        w_used = sem("w_used")
        bank_full = sem("bank_full")
        bank_freed = [sem(f"bank_freed{b}") for b in range(BANKS)]
        consts_in = sem("consts_in")
        rows_in = sem("rows_in")
        x_in = sem("x_in")
        mix0_in = sem("mix0_in")
        ln_in = sem("ln_in")
        sink_in = sem("sink_in")
        rope_in = sem("rope_in")
        rate_ready = sem("rate_ready")
        rate_done = sem("rate_done")
        bias_used = sem("bias_used")
        relu_ready = sem("relu_ready")
        l2_in = sem("l2_in")
        lev_in = sem("lev_in")
        rowg_in = sem("rowg_in")
        rel_out = sem("rel_out")
        rel_in = sem("rel_in")
        out_done = sem("out_done")
        act_step = sem("act_step")
        dve_step = sem("dve_step")
        pool_step = sem("pool_step")
        csilu_ready = sem("csilu_ready")
        modc_ready = sem("modc_ready")
        gkw_ready = sem("gkw_ready")
        laret_ready = sem("laret_ready")
        theta_exp = sem("theta_exp")
        zlog_ready = sem("zlog_ready")
        kd_ready = sem("kd_ready")
        carried_ready = sem("carried_ready")
        y_ready = sem("y_ready")
        mod_summed = sem("mod_summed")
        sq_ready = sem("sq_ready")
        x_ready = sem("x_ready")
        roped = sem("roped")
        negm_ready = sem("negm_ready")
        e_ready = sem("e_ready")
        xn_ready = sem("xn_ready")
        lf_ready = sem("lf_ready")
        aqk_ready = sem("aqk_ready")
        ik_ready = sem("ik_ready")
        diff_ready = sem("diff_ready")
        edec_ready = sem("edec_ready")
        ql_ready = sem("ql_ready")
        kl_ready = sem("kl_ready")
        neg2_ready = sem("neg2_ready")
        e2_ready = sem("e2_ready")
        mix_ready = sem("mix_ready")
        final_ready = sem("final_ready")
        amat_zero = sem("amat_zero")
        kln_ready = sem("kln_ready")
        rfs_ready = sem("rfs_ready")
        sexp_ready = sem("sexp_ready")
        sc_ready = sem("sc_ready")
        lbd_ready = sem("lbd_ready")
        lbs_ready = sem("lbs_ready")
        yacc_step = sem("yacc_step")
        sg_ready = sem("sg_ready")
        route_ready = sem("route_ready")
        route_exp = sem("route_exp")

        rates = []
        slot_free = {}
        ROWS_DMAS = 9
        L2_DMAS = 10
        bank_no = {}
        MOE_BANKS = 8 * BODY

        def full(name):
            return bank_no[name] + 1

        def bank(name):
            return psum[:, bank_no[name] % BANKS, :]

        def freed(name):
            return bank_freed[bank_no[name] % BANKS]

        def moved(name):
            return freed(name), bank_no[name] // BANKS + 1

        def bank_of(name, n):
            return bank(name).rearrange("p (a n) -> p a n", a=n)

        stages = ["mix0", "mlp0", "mix1", "mlp1", "mix2", "moe"]
        MODC_DONE = {"mix0": 1, "mlp0": 2, "mix1": 3, "mlp1": 3, "mix2": 4, "moe": 4}

        block = ctx.enter_context(nc.Block())

        @block.tensor
        def _(pe):
            count, uses = [0], [0]

            def claim(name):
                i = count[0]
                count[0] += 1
                assert name not in bank_no
                bank_no[name] = i
                if i >= BANKS:
                    pe.wait_ge(bank_freed[i % BANKS], i // BANKS)
                return psum[:, i % BANKS, :]

            def weights(key):
                i = load_no[key]
                pe.wait_ge(w_landed[i % RING], 16 * (i // RING + 1))
                return wring[:, i % RING, :, :]

            def mm(o, a, b, first=True, last=True):
                return nc.tensor.matmul(o, a, b, start=first, stop=last)

            def turn(o, a):
                n = a.shape[0]
                return nc.tensor.transpose(o, a, ident[0:n, 0:n])

            def mod_rows():
                vec = csilu[:, 0:16].rearrange("p (v k) -> p k v", v=2)
                for c in range(4):
                    w = weights(("mod0", c))
                    o = claim(f"modrow{c}")
                    for k in range(KC):
                        last = mm(o[0:2, :], vec[:, k, :], w[:, k, :], k == 0, k == KC - 1)
                    last.then_inc(bank_full, 1)
                    release(("mod0", c))
                for c in range(4):
                    pe.wait_ge(*moved(f"modrow{c}"))
                    o = claim(f"mod0_{c}")
                    for f in range(4):
                        last = turn(o[:, 2 * f:2 * f + 2], modrow[0:2, c, f * P:(f + 1) * P])
                    last.then_inc(bank_full, 1)

            def mod_sums(name, c):
                for l, m in BESIDE[name][c]:
                    V = vectors(l)
                    n = SUMMED.index((l, m))
                    done = sum(vectors(x) for x, _ in SUMMED[:n + 1])
                    slot_free[load_no[(f"mod{l}", m)]] = (mod_summed, done)
                    pe.wait_ge(mod_summed, done)
                    o = claim(f"mod{l}_{m}")
                    for f in range(4):
                        for v in range(V):
                            last = mm(o[:, f * V + v:f * V + v + 1], modsum[:, n % 2, v, f * P:(f + 1) * P], cst("ones"))
                    last.then_inc(bank_full, 1)

            def gate_rows(l, half):
                pe.wait_ge(modc_ready, l + 2)
                for c in range(2):
                    for v in ((0, 1) if l == 0 else (1,)):
                        o = claim(f"gate{l}{half}{c}{v}")
                        for j in range(4):
                            col = modc[:, l, 24 * half + 16 + 4 * c + j, 1 - v:2 - v]
                            last = mm(o[:, j * P:(j + 1) * P], col.to_broadcast([P, P]), ident)
                        last.then_inc(bank_full, 1)

            def release(key):
                slot_free[load_no[key]] = (bank_full, count[0])

            def release_on_use(key):
                uses[0] += 1
                slot_free[load_no[key]] = (w_used, uses[0])

            def turn_x(stage, src, tiles):
                n = len(tiles)
                per = 4 // n
                for b in range(KC // per):
                    o = claim(f"xT{stage}{b}")
                    for j in range(per):
                        k = b * per + j
                        for t in range(n):
                            last = turn(o[:, (j * n + t) * P:(j * n + t + 1) * P], src[:, tiles[t], k * P:(k + 1) * P])
                    last.then_inc(bank_full, 1)

            def wait_h(stage):
                for b in range(8 if stage in ("mix0", "mlp0", "mix1") else 4):
                    pe.wait_ge(*moved(f"xT{stage}{b}"))

            def features(name, w, f, lo, hi, o=None, close=True, cols=None):
                if o is None:
                    o = claim(name)
                for k in range(KC):
                    a = w[:, k, f * P:(f + 1) * P] if cols is None else cols(w, k)
                    last = mm(o[0:a.shape[-1] if cols is None else P, 0:hi - lo], a, hT[:, k, lo:hi], k == 0, k == KC - 1)
                if close:
                    last.then_inc(bank_full, 1)
                return last

            def tokens(name, w, t, width=512, at=0):
                o = claim(name)
                for k in range(KC):
                    last = mm(o[:, 0:width], hT[:, k, t * P:(t + 1) * P], w[:, k, at:at + width], k == 0, k == KC - 1)
                last.then_inc(bank_full, 1)

            def out_project(l, y, tiles):
                for n, t in enumerate(tiles):
                    pe.wait_ge(*moved(f"yT{l}{t if l < 2 else n}0"))
                    pe.wait_ge(*moved(f"yT{l}{t if l < 2 else n}1"))
                    for c in range(2):
                        w = weights((f"out{l}", c))
                        o = claim(f"out{l}{c}{t}")
                        for k in range(KC):
                            last = mm(o, y[:, k, n * P:(n + 1) * P], w[:, k, :], k == 0, k == KC - 1)
                        last.then_inc(bank_full, 1)
                        if t == tiles[-1]:
                            release((f"out{l}", c))

            def turn_y(l, src, t, n):
                for b in range(2):
                    o = claim(f"yT{l}{t}{b}")
                    for j in range(4):
                        k = 4 * b + j
                        last = turn(o[:, j * P:(j + 1) * P], src[:, n, k * P:(k + 1) * P])
                    last.then_inc(bank_full, 1)

            def mlp(l, tiles):
                lo = 0
                n = len(tiles) * P
                for c in range(8):
                    w = weights((f"up{l}", c))
                    for f in range(4):
                        features(f"up{l}{4 * c + f}", w, f, lo, lo + n)
                    release((f"up{l}", c))
                    if c > 0:
                        mod_sums(f"up{l}", c - 1)
                for half in range(2):
                    outs = [claim(f"down{l}{half}{t}") for t in tiles]
                    for g in range(4):
                        w = weights((f"down{l}", 4 * half + g))
                        if half == 0 and g == 0:
                            pe.wait_ge(*moved(f"up{l}31"))
                        for i, t in enumerate(tiles):
                            for c in range(KC):
                                last = mm(outs[i], h1T[:, g * KC + c, i * P:(i + 1) * P], w[:, c, :],
                                          g == 0 and c == 0, g == 3 and c == KC - 1)
                            if g == 3:
                                last.then_inc(bank_full, 1)
                        if g < 3:
                            last.then_inc(w_used, 1)
                            release_on_use((f"down{l}", 4 * half + g))
                    release((f"down{l}", 4 * half + 3))

            pe.wait_ge(consts_in, 16)
            pe.wait_ge(rows_in, ROWS_DMAS * 16)
            o = claim("cols")
            turn(o[:, 0:96], rows1[0:96, :])
            turn(o[:, 96:192], rows2[0:96, :]).then_inc(bank_full, 1)
            pe.wait_ge(csilu_ready, 1)

            mod_rows()
            pe.wait_ge(x_in, 32)
            turn_x("mix0", xres, range(4))
            wait_h("mix0")
            for c in range(7):
                w = weights(("ev_in", c))
                if c in (0, 3):
                    for f in range(4):
                        features(f"qk0{c}{f}", w, f, 0, 512)
                elif c < 6:
                    for t in range(NT):
                        tokens(f"vg0{c}{t}", w, t)
                else:
                    o = claim("lr0")
                    for k in range(KC):
                        last = mm(o[0:32, :], w[:, k, 0:32], hT[:, k, :], k == 0, k == KC - 1)
                    last.then_inc(bank_full, 1)
                release(("ev_in", c))
                if c > 0:
                    mod_sums("ev_in", c - 1)
            pe.wait_ge(laret_ready, 1)

            def decays(name, src):
                o = claim(f"cum{name}")
                for dr, (cum, dc) in enumerate((("cum_f", "dec_f"), ("cum_b", "dec_b"))):
                    for hp in range(2):
                        a = src[:, dr * 256 + hp * P:dr * 256 + (hp + 1) * P]
                        last = mm(o[:, (2 * dr + hp) * P:(2 * dr + hp + 1) * P], a, cst(cum))
                last.then_inc(bank_full, 1)
                o = claim(f"dec{name}")
                for dr, (cum, dc) in enumerate((("cum_f", "dec_f"), ("cum_b", "dec_b"))):
                    for hp in range(2):
                        a = src[:, dr * 256 + hp * P:dr * 256 + (hp + 1) * P]
                        last = mm(o[:, (2 * dr + hp) * 3:(2 * dr + hp + 1) * 3], a, cst(dc))
                last.then_inc(bank_full, 1)

            decays("ret", la_ret)
            pe.wait_ge(*moved("lr0"))
            pe.wait_ge(gkw_ready, 1)
            for t in range(NT):
                o = claim(f"z{t}")
                mm(o, lrT[0:33, t * P:(t + 1) * P], gkw[0:33, :]).then_inc(bank_full, 1)
                pe.wait_ge(*moved(f"z{t}"))
                decays(t, la)
                pe.wait_ge(kd_ready, t + 1)
                for dr in range(2):
                    o = claim(f"ktok{t}{dr}")
                    for hp in range(4):
                        last = turn(o[:, hp * P:(hp + 1) * P], kd[:, 4 * dr + hp, t * P:(t + 1) * P])
                    last.then_inc(bank_full, 1)
                pe.wait_ge(*moved(f"vg01{t}"))
                pe.wait_ge(*moved(f"vg04{t}"))
                for dr in range(2):
                    pe.wait_ge(*moved(f"ktok{t}{dr}"))
                for dr in range(2):
                    if (dr, t) in ((0, 3), (1, 2)):
                        continue
                    o = claim(f"kv{t}{dr}")
                    for hp in range(4):
                        for j in range(2):
                            last = mm(o[j * HD:(j + 1) * HD, hp * P:(hp + 1) * P],
                                      ktok[:, 4 * dr + hp, j * HD:(j + 1) * HD],
                                      vtok[:, t, (2 * hp + j) * P:(2 * hp + j + 1) * P])
                    last.then_inc(bank_full, 1)
            pe.wait_ge(carried_ready, 6)
            for t in range(NT):
                for half in range(2):
                    for dr in range(2):
                        o = claim(f"sc{t}{half}{dr}")
                        for hp in range(4):
                            h, j = hp, half
                            ks = kd[j * HD:(j + 1) * HD, 4 * dr + hp, t * P:(t + 1) * P]
                            qs = qd[j * HD:(j + 1) * HD, 4 * dr + hp, t * P:(t + 1) * P]
                            last = mm(o[:, h * P:(h + 1) * P], ks, qs)
                        last.then_inc(bank_full, 1)
                for half in range(2):
                    pe.wait_ge(*moved(f"sc{t}{half}1"))
                    o = claim(f"o{t}{half}")
                    for hp in range(4):
                        h, j = hp, half
                        oh = o[:, h * P:(h + 1) * P]
                        seeds = [s for s in (0, 1) if (s, t) != (0, 0) and (s, t) != (1, 1)]
                        mm(oh, amask[:, 4 * half + h, :], vtok[:, t, (2 * hp + j) * P:(2 * hp + j + 1) * P], True, False)
                        for s in seeds:
                            last = mm(oh, qd[j * HD:(j + 1) * HD, 4 * s + hp, t * P:(t + 1) * P],
                                      carried[j * HD:(j + 1) * HD, CARRY[(s, t)], hp * P:(hp + 1) * P],
                                      False, s == seeds[-1])
                    last.then_inc(bank_full, 1)
            for t in range(NT):
                pe.wait_ge(y_ready, 2 * (t + 1))
                turn_y(0, gtok, t, t)
            gate_rows(0, 0)
            out_project(0, yT, range(NT))
            pe.wait_ge(x_ready, 4)
            turn_x("mlp0", xres, range(4))
            gate_rows(0, 1)
            wait_h("mlp0")
            mlp(0, range(4))

            pe.wait_ge(x_ready, 8)
            turn_x("mix1", xres, range(4))
            wait_h("mix1")
            for p in range(2):
                w = weights(("od_qkv", p))
                for b in range(2):
                    o = claim(f"q1{p}{b}")
                    for j in range(2):
                        a = 2 * b + j
                        for k in range(KC):
                            last = mm(o[:, j * T:(j + 1) * T], w[:, k, a * P:(a + 1) * P], hT[:, k, T:2 * T], k == 0, k == KC - 1)
                    last.then_inc(bank_full, 1)
                release(("od_qkv", p))
            w = weights(("od_qkv", 2))
            for p in range(2):
                features(f"k1{p}", w, p, 0, 512)
            for t in range(NT):
                tokens(f"v1{t}", w, t, T, T)
            release(("od_qkv", 2))
            for b in range(5):
                for n in ([f"q1{b // 2}{b % 2}"] if b < 4 else ["k10", "k11"]):
                    pe.wait_ge(*moved(n))
                o = claim(f"rot{b}")
                src = q_raw[:, 2 * b:2 * b + 2, :] if b < 4 else k_raw
                mm(o, cst("perm"), src).then_inc(bank_full, 1)
            pe.wait_ge(roped, 7)
            for t in range(NT):
                pe.wait_ge(*moved(f"v1{t}"))
            for i in range(2):
                for g in range(4):
                    for a in range(4):
                        o = claim(f"lg1{i}{g}{a}")
                        j = a % 2
                        keys = kT if j == g % 2 else kTx
                        mm(o, qT[j * HD:(j + 1) * HD, 2 * g + a // 2, i * P:(i + 1) * P],
                           keys[j * HD:(j + 1) * HD, g // 2, :], True, False)
                        far = T + P * (1 - i)
                        mm(o[:, far:far + P], ident, cst(f"win{i}"), False, True).then_inc(bank_full, 1)
                    for a in range(4):
                        pe.wait_ge(e_ready, 16 * i + 4 * g + a + 1)
                        o = claim(f"eT1{i}{g}{a}")
                        for c in range(4):
                            last = turn(o[:, c * P:(c + 1) * P], e1[:, a, c * P:(c + 1) * P])
                        last.then_inc(bank_full, 1)
                    o1 = claim(f"o1{i}{g}")
                    for a in range(4):
                        pe.wait_ge(*moved(f"eT1{i}{g}{a}"))
                        for c in range(4):
                            last = mm(o1[:, a * HD:(a + 1) * HD], eT1[:, a, c * P:(c + 1) * P],
                                      v1[:, c, g * HD:(g + 1) * HD], c == 0, c == 3)
                    last.then_inc(bank_full, 1)
            for i in range(2):
                pe.wait_ge(*moved(f"o1{i}3"))
                turn_y(1, y1, X0 + i, i)
            gate_rows(1, 0)
            out_project(1, yT1, (2, 3))
            pe.wait_ge(x_ready, 10)
            turn_x("mlp1", xres, (2, 3))
            gate_rows(1, 1)
            wait_h("mlp1")
            mlp(1, (2, 3))

            pe.wait_ge(xn_ready, 2)
            turn_x("mix2", xn, (0, 1))
            wait_h("mix2")
            for c in range(9):
                w = weights(("w_in", c))
                if c in (0, 1, 7):
                    for b in range(2):
                        o = claim(f"f2{c}{b}")
                        for j in range(2):
                            f = 2 * b + j
                            for k in range(KC):
                                last = mm(o[:, j * T:(j + 1) * T], w[:, k, f * P:(f + 1) * P],
                                          hT[:, k, 0:T], k == 0, k == KC - 1)
                        last.then_inc(bank_full, 1)
                else:
                    for t in range(2):
                        tokens(f"t2{c}{t}", w, t, 512 if c < 8 else 72)
                release(("w_in", c))
            pe.wait_ge(l2_in, L2_DMAS * 16)
            o = claim("rel")
            mm(o[0:8, 0:2 * T - 1], relb[0:NBUCKET, :], hot[0:NBUCKET, :]).then_inc(bank_full, 1)
            for n in range(2):
                for t in range(2):
                    pe.wait_ge(aqk_ready, 2 * n + t + 1)
                    o = claim(f"aT{n}{t}")
                    src = (aq, ak)[n]
                    for b in range(4):
                        last = turn(o[:, b * P:(b + 1) * P], src[:, t, b * P:(b + 1) * P])
                    last.then_inc(bank_full, 1)
            o = claim("ikT")
            for t in range(2):
                pe.wait_ge(ik_ready, t + 1)
                last = turn(o[:, t * P:(t + 1) * P], ikd[:, t, :])
            last.then_inc(bank_full, 1)
            pe.wait_ge(*moved("ikT"))
            for b in range(2):
                pe.wait_ge(*moved(f"f27{b}"))
            for i in range(2):
                for b in range(4):
                    o = claim(f"ix{i}{b}")
                    j = b % 2
                    for n in range(2):
                        last = mm(o[:, n * T:(n + 1) * T],
                                  iqT[j * HD:(j + 1) * HD, 2 * (b // 2) + n, i * P:(i + 1) * P],
                                  ikT[j * HD:(j + 1) * HD, :])
                    last.then_inc(bank_full, 1)
            for n in range(len(LEVELS) + 1):
                if n < len(LEVELS):
                    pe.wait_ge(ql_ready, n + 1)
                    pe.wait_ge(kl_ready, n + 1)
                for t in range(2):
                    o = claim(f"lev{n}{t}")
                    for h in range(4):
                        qs, ks = (ql, kl) if n < len(LEVELS) else (rqT, rkT)
                        last = mm(o[:, h * P:(h + 1) * P], ks[:, h, t * P:(t + 1) * P], qs[:, h, t * P:(t + 1) * P])
                    last.then_inc(bank_full, 1)
            pe.wait_ge(ql_ready, len(LEVELS) + 1)
            pe.wait_ge(kl_ready, len(LEVELS) + 1)
            o = claim("across")
            for h in range(4):
                last = mm(o[:, h * P:(h + 1) * P], kl[:, h, 0:P], ql[:, h, P:T])
            last.then_inc(bank_full, 1)
            pe.wait_ge(*moved("across"))
            for t in range(2):
                pe.wait_ge(*moved(f"t22{t}"))
                pe.wait_ge(*moved(f"t26{t}"))
                pe.wait_ge(*moved(f"aT0{t}"))
                pe.wait_ge(*moved(f"aT1{t}"))
            for t in range(2):
                o = claim(f"ro{t}")
                for h in range(4):
                    oh = o[:, h * P:(h + 1) * P]
                    last = mm(oh, amat[:, t, h, :], rv[:, t, h * P:(h + 1) * P], True, t == 0)
                    if t == 1:
                        last = mm(oh, across[:, h, :], rv[:, 0, h * P:(h + 1) * P], False, True)
                last.then_inc(bank_full, 1)
            for i in range(2):
                for b in range(4):
                    o = claim(f"lg2{i}{b}")
                    j = b % 2
                    for n in range(2):
                        blk = 2 * (b // 2) + n
                        last = mm(o[:, n * T:(n + 1) * T], aqT[j * HD:(j + 1) * HD, blk, i * P:(i + 1) * P],
                                  akT[j * HD:(j + 1) * HD, blk, :])
                    last.then_inc(bank_full, 1)
                pe.wait_ge(e2_ready, 8 * (i + 1))
                for b in range(4):
                    o = claim(f"eT2{i}{b}")
                    for j in range(2):
                        for c in range(2):
                            last = turn(o[:, (2 * j + c) * P:(2 * j + c + 1) * P], logit[:, 2 * b + j, c * P:(c + 1) * P])
                    last.then_inc(bank_full, 1)
                o = claim(f"att{i}")
                for b in range(4):
                    pe.wait_ge(*moved(f"eT2{i}{b}"))
                    for j in range(2):
                        h = 2 * b + j
                        for c in range(2):
                            last = mm(o[:, h * HD:(h + 1) * HD], eT2[:, b % 4, (2 * j + c) * P:(2 * j + c + 1) * P],
                                      av[:, c, h * HD:(h + 1) * HD], c == 0, c == 1)
                last.then_inc(bank_full, 1)
            for i in range(2):
                pe.wait_ge(mix_ready, 2 + i + 1)
                turn_y(2, mix, i, i)
            gate_rows(2, 0)
            out_project(2, yT2, (2, 3))
            pe.wait_ge(xn_ready, 4)
            turn_x("moe", xn, (0, 1))
            gate_rows(2, 1)
            wait_h("moe")
            o = claim("router")
            for t in range(2):
                for k in range(KC):
                    last = mm(o[:, t * 20:(t + 1) * 20], hT[:, k, t * P:(t + 1) * P], wr[:, k, :], k == 0, k == KC - 1)
            last.then_inc(bank_full, 1)
            base = count[0]
            bank_no["moe"] = base

            def expert(turn_no, j):
                def turn_claim(local):
                    pe.wait_ge(bank_freed[(base + local) % BANKS], turn_no * BODY + (base + local) // BANKS)
                    return psum[:, (base + local) % BANKS, :]

                def slot(piece):
                    i = MOE_LOAD0 + 3 * j + piece
                    pe.wait_ge(w_landed[i % RING], turn_no * (16 * LOADS_PER_TURN // RING) + 16 * (i // RING + 1))
                    return wring[:, i % RING, :, :]

                w1, w3 = slot(0), slot(1)
                for f in range(4):
                    o = turn_claim(8 * j + f)
                    for n, w in enumerate((w1, w3)):
                        for k in range(KC):
                            last = mm(o[:, n * T:(n + 1) * T], w[:, k, f * P:(f + 1) * P], hT[:, k, 0:T],
                                      k == 0, k == KC - 1)
                    last.then_inc(bank_full, 1)
                w2 = slot(2).rearrange("p (f a) n -> p f (a n)", a=2)
                for n in range(2):
                    for t in range(2):
                        o = turn_claim(8 * j + 4 + 2 * n + t)
                        for f in range(4):
                            if n == 0 and t == 0:
                                at = base + 8 * j + f
                                pe.wait_ge(bank_freed[at % BANKS], turn_no * BODY + (at // BANKS + 1))
                            last = mm(o, he[:, j % 2, f, t * P:(t + 1) * P], w2[:, f, n * 512:(n + 1) * 512],
                                      f == 0, f == 3)
                        last.then_inc(bank_full, 1)

            with pe.Fori(0, TURNS) as turn_no:
                for j in range(BODY):
                    expert(turn_no, j)

        def rows_of(vecs):
            return vecs.rearrange("a (k p) -> (a k) p", p=P)

        @block.sync
        def _(sp):
            sp.dma_start(const[:, :], I["const_main"]).then_inc(consts_in, 16)
            for rows, at, src in ((rows1, 40, I["b_mod"][0:1]), (rows1, 88, I["lb_logits_2"]),
                                  (rows2, 0, I["b_mod"][1:2]), (rows2, 48, I["b_ada_2"][0:1])):
                n = src.shape[0] * src.shape[1] // P
                sp.dma_start(rows[at:at + n, :], rows_of(src)).then_inc(rows_in, 16)
            sp.wait_ge(rows_in, ROWS_DMAS * 16)

            def source(key):
                name, c = key
                l = int(name[-1]) if name[-1].isdigit() else 0
                if name.startswith("mod"):
                    m = I["w_mod"][l] if l < 2 else I["w_ada_2"][0]
                    return m[:, c * 512:(c + 1) * 512]
                if name.startswith("out"):
                    m = (I["ev_w_out"], I["od_w_out"], I["w_out_2"])[l][0]
                    return m[:, c * 512:(c + 1) * 512]
                if name.startswith("up"):
                    return I["mlp_w1"][l][:, c * 512:(c + 1) * 512]
                if name.startswith("down"):
                    half, g = c // 4, c % 4
                    return I["mlp_w2"][l][g * D:(g + 1) * D, half * 512:(half + 1) * 512]
                m = {"ev_in": I["ev_w_in"], "od_qkv": I["od_w_qkv"], "w_in": I["w_in_2"]}[name][0]
                return m[:, c * 512:min((c + 1) * 512, m.shape[1])]

            for i, key in enumerate(STREAM):
                if i >= RING:
                    sp.wait_ge(*slot_free[i - RING])
                src = source(key)
                sp.dma_start(wring[:, i % RING, :, 0:src.shape[1]],
                             src.rearrange("(k p) n -> p k n", p=P)).then_inc(w_landed[i % RING], 16)
            base = bank_no["moe"]

            def expert_slot(e, piece):
                if piece < 2:
                    return (I["w1_2"], I["w3_2"])[piece][0, bass.ds(e, 1)].rearrange("a (k p) n -> p (a k) n", p=P)
                return I["w2_2"][0, bass.ds(e, 1)].rearrange("a (f p) n -> p (a f) n", p=P)

            def load_expert(e, piece, local):
                i = MOE_LOAD0 + local
                dst = wring[:, i % RING, :, :]
                if piece == 2:
                    dst = dst.rearrange("p (f a) n -> p f (a n)", a=2)
                sp.dma_start(dst, expert_slot(e, piece)).then_inc(w_landed[i % RING], 16)

            def freed_by(turn_no, q):
                return turn_no * MOE_BANKS + (base + 8 * (q // 3) + (4 if q % 3 < 2 else 8))

            for m in range(RING):
                sp.wait_ge(*slot_free[MOE_LOAD0 + m - RING])
                load_expert(m // 3, m % 3, m)
            with sp.Fori(0, TURNS - 1) as turn_no:
                for q in range(LOADS_PER_TURN):
                    m = q + RING
                    sp.wait_ge(bank_full, freed_by(turn_no, q))
                    load_expert(turn_no * BODY + m // 3, m % 3, m)
            for q in range(LOADS_PER_TURN - RING):
                m = q + RING
                sp.wait_ge(bank_full, freed_by(TURNS - 1, q))
                load_expert((TURNS - 1) * BODY + m // 3, m % 3, m)

        @block.gpsimd
        def _(pool):
            steps = [0]

            def step(ins):
                steps[0] += 1
                ins.then_inc(pool_step, 1)
                pool.wait_ge(pool_step, steps[0])

            step(nc.gpsimd.memset(gkw[0:33, :], 0.0))
            nc.gpsimd.memset(lrT[32:33, :], 1.0).then_inc(gkw_ready, 1)
            pool.dma_start(gkw[0:16, 0:256], I["ev_gla_gk_w"][0, 0]).then_inc(mix0_in, 16)
            pool.dma_start(gkw[16:32, 256:512], I["ev_gla_gk_w"][0, 1]).then_inc(mix0_in, 16)
            pool.dma_start(gkw[32:33, :], I["ev_gla_gk_b"].rearrange("a b c -> a (b c)")).then_inc(mix0_in, 16)
            pool.dma_start(normg, I["ev_gla_norm_g"].to_broadcast([P, P])).then_inc(mix0_in, 16)
            pool.dma_start(theta, I["ev_ret_theta"].rearrange("a b c -> a (b c)").to_broadcast([P, 8])).then_inc(mix0_in, 16)
            pool.dma_start(sinkb, I["od_sink"].to_broadcast([P, 16])).then_inc(sink_in, 16)
            pool.wait_ge(gkw_ready, 1)
            step(nc.gpsimd.memset(half_neg, -0.5))
            roots = [0]

            def inverse_roots(aps):
                for a in aps:
                    roots[0] += 1
                    pool.wait_ge(rate_ready, roots[0])
                    nc.gpsimd.tensor_tensor(a, a, half_neg[:, 0:a.shape[1]], ALU.pow).then_inc(rate_done, 1)

            def norm_vectors(n, s, v):
                pool.wait_ge(s, v)
                l, j = n // 2, n % 2
                pool.dma_start(lnb[:, 0, :], I["ln_g"][l, j:j + 1, :].to_broadcast([P, D])).then_inc(ln_in, 16)
                pool.dma_start(lnb[:, 1, :], I["ln_b"][l, j:j + 1, :].to_broadcast([P, D])).then_inc(ln_in, 16)

            norm_vectors(0, carried_ready, 6)
            inverse_roots([hsum[:, 0:4]] * 8)
            inverse_roots([lnr] * 4)
            norm_vectors(1, x_ready, 4)
            inverse_roots([lnr] * 4)
            norm_vectors(2, x_ready, 8)
            pool.dma_start(rope.rearrange("p a b -> p (a b)"), I["const_rope"]).then_inc(rope_in, 16)
            inverse_roots([lnr] * 2)
            norm_vectors(3, x_ready, 10)
            inverse_roots([lnr] * 2)
            pool.wait_ge(x_ready, 12)
            for dst, src in (
                (relb[0:NBUCKET, :], I["rel_bias_2"]), (hot[0:NBUCKET, :], I["const_buckets"]),
                (qkg[:, 0:HD], I["q_norm_g_2"].to_broadcast([P, HD])), (qkg[:, HD:P], I["k_norm_g_2"].to_broadcast([P, HD])),
                (ikn[:, 0:HD], I["idx_k_norm_g_2"].to_broadcast([P, HD])), (ikn[:, HD:P], I["idx_k_norm_b_2"].to_broadcast([P, HD])),
                (wr[:, :, 0:4], I["w_rg_2"][0].rearrange("(k p) n -> p k n", p=P)),
                (wr[:, :, 4:20], I["w_re_2"][0].rearrange("(k p) n -> p k n", p=P)),
                (brr[:, 0:4], I["b_rg_2"].to_broadcast([P, 4])), (brr[:, 4:20], I["b_re_2"].to_broadcast([P, NEXP])),
            ):
                pool.dma_start(dst, src).then_inc(l2_in, 16)
            inverse_roots([lnr] * 2)
            for b in range(4):
                pool.wait_ge(*moved(f"xTmix2{b}"))
            pool.dma_start(levels, I["const_levels"]).then_inc(lev_in, 16)
            inverse_roots([st8] * 4 + [lnr] * 2)
            pool.wait_ge(bank_full, full("t281"))
            pool.dma_start(rowg[:, 0, :], I["rec_out_g_2"].to_broadcast([P, 512])).then_inc(rowg_in, 16)
            pool.dma_start(rowg[:, 1, :], I["attn_out_g_2"].to_broadcast([P, 512])).then_inc(rowg_in, 16)
            nc.gpsimd.memset(amat, 0.0).then_inc(amat_zero, 1)
            pool.wait_ge(amat_zero, 1)
            pool.wait_ge(*moved("rel"))
            pool.dma_start(rel_scratch, relE[0:8, 0:2 * T - 1]).then_inc(rel_out, 16)
            pool.wait_ge(kln_ready, 1)
            for n in range(len(LEVELS) + 1):
                pool.wait_ge(edec_ready, n + 1)
                if n > 0:
                    pool.wait_ge(bank_full, full(f"lev{n - 1}1"))
                nc.gpsimd.tensor_tensor(kl, rkT, edec, ALU.mult).then_inc(kl_ready, 1)
            pool.wait_ge(rel_out, 16)

            def bias_tile(i):
                pool.dma_start(biasT, bass.AP(tensor=rel_scratch.tensor, offset=i * P,
                                              ap=[[1, P], [2 * T - 1, 8], [1, T]])).then_inc(rel_in, 16)

            pool.wait_ge(*moved("across"))
            bias_tile(0)
            inverse_roots([st8[:, 0:4]] * 2)
            pool.wait_ge(bias_used, 1)
            bias_tile(1)
            inverse_roots([st8] * 2)
            inverse_roots([lnr] * 2)

        @block.scalar
        def _(act):
            steps = [0]

            def step(ins):
                steps[0] += 1
                ins.then_inc(act_step, 1)
                act.wait_ge(act_step, steps[0])

            counts = {}

            def signal(ins, s):
                counts[s.name] = counts.get(s.name, 0) + 1
                ins.then_inc(s, 1)
                act.wait_ge(s, counts[s.name])

            def free(ins, name):
                ins.then_inc(freed(name), 1)
                act.wait_ge(*moved(name))

            def f(o, a, func, **kw):
                return nc.scalar.activation(o, a, func, **kw)

            for at, src in ((0, I["c"]), (8, I["c_ctx"].rearrange("(a d) -> a d", a=1)), (16, I["c_2"]),
                            (24, I["norm1_g_2"]), (32, I["norm2_g_2"])):
                act.dma_start(rows1[at:at + KC, :], rows_of(src)).then_inc(rows_in, 16)
            act.dma_start(xres[:, 0:2, :], I["ctx"][0].rearrange("(t p) d -> p t d", p=P)).then_inc(x_in, 16)
            act.dma_start(xres[:, 2:4, :], I["x"][0].rearrange("(t p) d -> p t d", p=P)).then_inc(x_in, 16)

            act.wait_ge(bank_full, full("cols"))
            free(f(cols[:, :], bank("cols")[:, 0:192], ACT.Copy), "cols")
            act.wait_ge(*moved("cols"))
            signal(f(csilu[:, :], cols[:, 0:24], ACT.Silu), csilu_ready)
            act.wait_ge(mix0_in, 80)
            step(f(theta, theta, ACT.Exp))
            signal(f(theta, theta, ACT.Ln, scale=-1.0, bias=1.0), theta_exp)

            def modulate(stage):
                s = stages.index(stage)
                l, half = s // 2, s % 2
                act.wait_ge(modc_ready, MODC_DONE[stage])
                wide = s < 3
                for b in range(0, 8 if wide else 4, 2):
                    n = f"xT{stage}{b}"
                    act.wait_ge(bank_full, full(n))
                    for j in range(2):
                        k, v, at = (b, 1 - j, j * T) if wide else (2 * b + j, 0, 0)
                        last = f(hT[:, k, at:at + T], bank(n)[:, j * T:(j + 1) * T], ACT.Identity,
                                 bias=modc[:, l, 24 * half + k, v:v + 1], scale=modc[:, l, 24 * half + 8 + k, v:v + 1])
                    free(last, n)

            def move(name, dst, src=None, func=ACT.Copy, **kw):
                act.wait_ge(bank_full, full(name))
                free(f(dst, bank(name) if src is None else src, func, **kw), name)

            def turned(l, t, n):
                dst = (yT, yT1, yT2)[l]
                for b in range(2):
                    name = f"yT{l}{t}{b}"
                    act.wait_ge(bank_full, full(name))
                    move(name, dst[:, 4 * b:4 * b + 4, n * P:(n + 1) * P], bank(name).rearrange("p (b n) -> p b n", b=4))

            def mods(name, c):
                for l, m in BESIDE[name][c]:
                    V = vectors(l)
                    move(f"mod{l}_{m}", modc[:, l, 4 * m:4 * m + 4, 0:V],
                         bank(f"mod{l}_{m}")[:, 0:4 * V].rearrange("p (f v) -> p f v", v=V))

            def gates(l, half):
                for c in range(2):
                    for v in ((0, 1) if l == 0 else (1,)):
                        move(f"gate{l}{half}{c}{v}", gate[:, v, c * 512:(c + 1) * 512])

            def relus(l, n):
                for i in range(32):
                    act.wait_ge(bank_full, full(f"up{l}{i}"))
                    signal(f(h1T[:, i, 0:n], bank(f"up{l}{i}")[:, 0:n], ACT.Relu), relu_ready)
                    if i % 4 == 3 and i > 3:
                        mods(f"up{l}", i // 4 - 1)

            for c in range(4):
                move(f"modrow{c}", modrow[0:2, c, :], bank(f"modrow{c}")[0:2, :])
            modulate("mix0")
            for c in range(7):
                if c in (0, 3):
                    for i in range(4):
                        blk = (0 if c == 0 else 2) + (i if i < 2 else i + 2)
                        scaled = (i >= 2) if c == 0 else (i < 2)
                        move(f"qk0{c}{i}", qkT[:, blk, :], func=ACT.Copy, scale=HD ** -0.5 if scaled else 1.0)
                elif c in (2, 5):
                    for t in range(NT):
                        move(f"vg0{c}{t}", gtok[:, t, (c // 3) * 512:(c // 3 + 1) * 512], func=ACT.Silu)
                if c > 0:
                    mods("ev_in", c - 1)

            def decays(name, dst, kind):
                act.wait_ge(bank_full, full(f"cum{name}"))
                src = bank(f"cum{name}").rearrange("p (a n) -> p a n", a=4)
                f(dst[:, 0], src, ACT.Exp)
                free(f(dst[:, 1], src, ACT.Exp, scale=-1.0), f"cum{name}")
                act.wait_ge(bank_full, full(f"dec{name}"))
                src = bank(f"dec{name}")[:, 0:12].rearrange("p (d h c) -> p d h c", d=2, h=2)
                for t in (range(NT) if name == "ret" else (name,)):
                    last = f(dec[:, t, :, 2 * kind:2 * kind + 2, :], src, ACT.Exp)
                free(last, f"dec{name}")

            decays("ret", exp_ret, 0)
            for t in range(NT):
                act.wait_ge(bank_full, full(f"z{t}"))
                if t > 0:
                    act.wait_ge(*moved(f"z{t - 1}"))
                step(f(zlog, bank(f"z{t}"), ACT.Abs))
                step(f(zlog, zlog, ACT.Exp, scale=-1.0))
                signal(f(zlog, zlog, ACT.Ln, bias=1.0), zlog_ready)
                if t > 0:
                    act.wait_ge(kd_ready, t)
                decays(t, exp_gla, 1)
                for dr in range(2):
                    name = f"ktok{t}{dr}"
                    if t > 0:
                        act.wait_ge(bank_full, full(f"kv{t - 1}{0 if t == 3 else 1}"))
                    move(name, ktok[:, 4 * dr:4 * dr + 4, :], bank_of(name, 4))
            for t in range(NT):
                for half in range(2):
                    if t > 0:
                        act.wait_ge(bank_full, full(f"o{t - 1}{half}"))
                    move(f"sc{t}{half}0", amask[:, 4 * half:4 * half + 4, :], bank_of(f"sc{t}{half}0", 4))
                for half in range(2):
                    if t > 0:
                        act.wait_ge(y_ready, 2 * (t - 1) + half + 1)
                    act.wait_ge(bank_full, full(f"o{t}{half}"))
                    signal(f((sqb, la)[half], bank(f"o{t}{half}"), ACT.Square), sq_ready)
            for t in range(NT):
                turned(0, t, t)
            gates(0, 0)
            modulate("mlp0")
            gates(0, 1)
            relus(0, 512)

            modulate("mix1")
            for p in range(2):
                for b in range(2):
                    move(f"q1{p}{b}", q_raw[:, 4 * p + 2 * b:4 * p + 2 * b + 2, :], bank_of(f"q1{p}{b}", 2))
            for p in range(2):
                act.wait_ge(bank_full, full(f"k1{p}"))
                f(kT[:, p, 0:T], bank(f"k1{p}")[:, 0:T], ACT.Copy)
                move(f"k1{p}", k_raw[:, p, :], bank(f"k1{p}")[:, T:2 * T])
            for i in range(2):
                for g in range(4):
                    n = 4 * i + g
                    act.wait_ge(negm_ready, n + 1)
                    if n > 0:
                        act.wait_ge(bank_full, full(f"eT1{(n - 1) // 4}{(n - 1) % 4}3"))
                    for a in range(4):
                        name = f"lg1{i}{g}{a}"
                        act.wait_ge(bank_full, full(name))
                        signal(f(e1[:, a, :], bank(name), ACT.Exp, scale=HD ** -0.5, bias=negm1[:, a:a + 1],
                          accum_out=den1[:, 4 * n + a:4 * n + a + 1]), e_ready)
                        act.wait_ge(e_ready, 4 * n + a + 1)
                        act.sem_inc(freed(name), 1)
                    signal(f(sexp1, sexp1, ACT.Exp), sexp_ready)
                    if n > 0:
                        act.wait_ge(bank_full, full(f"o1{(n - 1) // 4}{(n - 1) % 4}"))
                    for a in (0, 2):
                        move(f"eT1{i}{g}{a}", eT1[:, a, :])
            for i in range(2):
                turned(1, X0 + i, i)
            gates(1, 0)
            modulate("mlp1")
            gates(1, 1)
            relus(1, 256)

            act.wait_ge(lbd_ready, 1)
            signal(f(lbc, lbc, ACT.Sigmoid), lbs_ready)
            modulate("mix2")
            for b in range(2):
                move(f"f20{b}", rqT[:, 2 * b:2 * b + 2, :], bank_of(f"f20{b}", 2), ACT.Silu)
            for b in range(2):
                move(f"f21{b}", rsig[:, 2 * b:2 * b + 2, :], bank_of(f"f21{b}", 2), ACT.Sigmoid)
            for t in range(2):
                move(f"t23{t}", rg[:, t, :], func=ACT.Silu)
            for b in range(2):
                move(f"f27{b}", iqT[:, 2 * b:2 * b + 2, :], bank_of(f"f27{b}", 2))
            act.wait_ge(rfs_ready, 1)
            signal(f(rsig, rsig, ACT.Ln), lf_ready)
            for n in range(2):
                for t in range(2):
                    name = f"aT{n}{t}"
                    move(name, (aqT, akT)[n][:, :, t * P:(t + 1) * P], bank_of(name, 4))
            move("ikT", ikT, bank("ikT")[:, 0:T])
            for i in range(2):
                for b in range(4):
                    n = 4 * i + b
                    act.wait_ge(sc_ready, n + 1)
                    move(f"ix{i}{b}", sc_r[:, :, :], bank_of(f"ix{i}{b}", 2), ACT.Relu, scale=HD ** -0.5)
            for n in range(len(LEVELS) + 1):
                act.wait_ge(diff_ready, n + 1)
                signal(f(edec, edec, ACT.Exp), edec_ready)
            for i in range(2):
                act.wait_ge(neg2_ready, i + 1)
                for h in range(8):
                    signal(f(logit[:, h, :], logit[:, h, :], ACT.Exp, bias=neg2[:, h:h + 1],
                      accum_out=den2[:, h:h + 1]), e2_ready)
                if i == 1:
                    act.wait_ge(bank_full, full("att0"))
                for b in range(4):
                    move(f"eT2{i}{b}", eT2[:, b, :])
            for i in range(2):
                turned(2, i, i)
            gates(2, 0)
            modulate("moe")
            gates(2, 1)
            act.wait_ge(route_ready, 1)
            signal(f(rt_exp, rt_exp, ACT.Exp), route_exp)
            base = bank_no["moe"]
            with act.Fori(0, TURNS) as turn_no:
                for j in range(BODY):
                    for u in range(4):
                        local = 8 * j + u
                        act.wait_ge(bank_full, turn_no * MOE_BANKS + (base + local + 1))
                        prev = base + local - 16
                        act.wait_ge(bank_freed[prev % BANKS], turn_no * BODY + (prev // BANKS + 1))
                        f(sg[:, j % 2, u, :], psum[:, (base + local) % BANKS, 0:T], ACT.Silu).then_inc(sg_ready, 1)
            for t in range(2):
                act.wait_ge(final_ready, t + 1)
                act.dma_start(out[0, t * P:(t + 1) * P, :], xres[:, X0 + t, :]).then_inc(out_done, 16)
            act.wait_ge(out_done, 32)

        @block.vector
        def _(dve):
            steps = [0]
            v_ = nc.vector

            def step(ins):
                steps[0] += 1
                ins.then_inc(dve_step, 1)
                dve.wait_ge(dve_step, steps[0])

            counts = {}

            def signal(ins, s):
                counts[s.name] = counts.get(s.name, 0) + 1
                ins.then_inc(s, 1)
                dve.wait_ge(s, counts[s.name])

            def free(ins, name):
                ins.then_inc(freed(name), 1)
                dve.wait_ge(*moved(name))

            def root(ins, rate):
                ins.then_inc(rate_ready, 1)
                rates.append(rate)
                dve.wait_ge(rate_done, len(rates))

            def ready(name):
                dve.wait_ge(bank_full, full(name))
                return bank(name)

            def move(name, dst, src=None):
                ready(name)
                free(v_.tensor_copy(dst, bank(name) if src is None else src), name)

            def mods(l, c0, c1):
                V = 2 if l < 2 else 1
                for c in range(c0, c1):
                    o = ready(f"mod{l}_{c}")[:, 0:4 * V].rearrange("p (f v) -> p f v", v=V)
                    free(v_.tensor_copy(modc[:, l, 4 * c:4 * c + 4, 0:V], o), f"mod{l}_{c}")

            def sum_mods(name, c):
                for l, m in BESIDE[name][c]:
                    V = vectors(l)
                    n = SUMMED.index((l, m))
                    i = load_no[(f"mod{l}", m)]
                    dve.wait_ge(w_landed[i % RING], 16 * (i // RING + 1))
                    if n >= 2:
                        dve.wait_ge(bank_full, full("mod%d_%d" % SUMMED[n - 2]))
                    for k in range(KC):
                        for v in range(V):
                            acc, w = modsum[:, n % 2, v, :], wring[:, i % RING, k, :]
                            at = (8 * v if l < 2 else 16) + k
                            by = csilu[:, at:at + 1]
                            if k == 0:
                                ins = v_.tensor_scalar(acc, w, by, None, ALU.mult)
                            else:
                                dve.wait_ge(dve_step, steps[0] - (V - 1))
                                ins = v_.scalar_tensor_tensor(acc, w, by, acc, ALU.mult, ALU.add)
                            if k < KC - 1:
                                steps[0] += 1
                                ins.then_inc(dve_step, 1)
                            else:
                                ins.then_inc(mod_summed, 1)
                                if v == 0 and V == 2:
                                    dve.wait_ge(dve_step, steps[0])

            def finish_mod(l, c0, c1):
                V = 2 if l < 2 else 1
                for c in range(c0, c1):
                    dve.wait_ge(*moved(f"mod{l}_{c}"))
                at = (40, 96, 144)[l]
                raw = modc[:, l, 4 * c0:4 * c1, 0:V]
                ins = v_.tensor_tensor(raw, raw, cols[:, at + 4 * c0:at + 4 * c1].unsqueeze(2)
                                       .to_broadcast([P, 4 * (c1 - c0), V]), ALU.add)
                for half in ((0,) if c1 == 4 else (1,) if c0 == 4 else (0, 1)):
                    step(ins)
                    scales = modc[:, l, 24 * half + 8:24 * half + 16, 0:V]
                    ins = v_.tensor_scalar(scales, scales, 1.0, None, ALU.add)
                    if l == 2:
                        step(ins)
                        gain = cols[:, 24 + 8 * half:32 + 8 * half].unsqueeze(2)
                        ins = v_.tensor_tensor(scales, scales, gain, ALU.mult)
                signal(ins, modc_ready)

            def modulate(stage):
                s = stages.index(stage)
                l, half = s // 2, s % 2
                wide = s < 3
                for b in range(1, 8 if wide else 4, 2):
                    n = f"xT{stage}{b}"
                    ready(n)
                    for j in range(2):
                        k, v, at = (b, 1 - j, j * T) if wide else (2 * b + j, 0, 0)
                        last = v_.tensor_scalar(hT[:, k, at:at + T], bank(n)[:, j * T:(j + 1) * T],
                                                modc[:, l, 24 * half + 8 + k, v:v + 1],
                                                modc[:, l, 24 * half + k, v:v + 1], ALU.mult, ALU.add)
                    free(last, n)

            def residual(l, prefix, half_no, tiles, alpha=ALPHA):
                cs = slice(half_no * 512, (half_no + 1) * 512)
                for t in tiles:
                    name = f"{prefix}{half_no}{t}"
                    ready(name)
                    gv = 0 if t < X0 else 1
                    for v in ((0, 1) if l == 0 else (1,)):
                        dve.wait_ge(*moved(f"gate{l}{0 if prefix.startswith('out') else 1}{half_no}{v}"))
                    free(v_.tensor_tensor(ubuf, bank(name), gate[:, gv, cs], ALU.mult), name)
                    dve.wait_ge(*moved(name))
                    step(v_.scalar_tensor_tensor(xres[:, t, cs], xres[:, t, cs], alpha, ubuf, ALU.mult, ALU.add))

            def residual_norm(l, prefix, t):
                for half in ((0, 1) if prefix == "out" else (1,)):
                    residual(l, f"{prefix}{l}", half, (t,))
                layer_norm(2 * l + (prefix == "down"), (t,))

            def layer_norm(n, tiles):
                dve.wait_ge(ln_in, 32 * (n + 1))
                for t in tiles:
                    x = xres[:, t, :]
                    for c in range(2):
                        step(v_.bn_stats(lnstat[:, c, :], x[:, c * 512:(c + 1) * 512]))
                    step(v_.bn_aggr(lnagg, lnstat.rearrange("p a b -> p (a b)")))
                    root(v_.tensor_scalar(lnr, lnagg[:, 1:2], LN_EPS, None, ALU.add), lnr)
                    step(v_.tensor_scalar(x, x, lnagg[:, 0:1], lnr, ALU.subtract, ALU.mult))
                    step(v_.tensor_tensor(x, x, lnb[:, 0, :], ALU.mult))
                    signal(v_.tensor_tensor(x, x, lnb[:, 1, :], ALU.add), x_ready)
                    tiles_done[0] += 1
                    dve.wait_ge(x_ready, tiles_done[0])

            tiles_done = [0]

            def head_rate(src, heads, out_rate, scratch, width, eps=RMS_EPS):
                step(v_.tensor_tensor(scratch, src, src, ALU.mult))
                step(v_.tensor_reduce(out_rate, scratch.rearrange("p (h d) -> p h d", h=heads), AX.X, ALU.add))
                root(v_.tensor_scalar(out_rate, out_rate, 1.0 / width, eps, ALU.mult, ALU.add), out_rate)

            def mlp(l, tiles):
                n = len(tiles) * P
                for i in range(32):
                    name = f"up{l}{i}"
                    dve.wait_ge(relu_ready, 32 * l + i + 1)
                    h = h1T[:, i, 0:n]
                    free(v_.tensor_tensor(h, h, bank(name)[:, 0:n], ALU.mult), name)
                    if i % 4 == 3:
                        sum_mods(f"up{l}", i // 4)
                finish_mod(l + 1, 0, 12)
                residual(l, f"down{l}", 0, tiles)
                for t in tiles:
                    residual_norm(l, "down", t)

            mods(0, 0, 4)
            finish_mod(0, 0, 4)
            modulate("mix0")
            dve.wait_ge(theta_exp, 1)
            for dr in range(2):
                last = v_.tensor_scalar(la_ret[:, dr * 256:(dr + 1) * 256].rearrange("p (h d) -> p h d", h=4),
                                        theta[:, 4 * dr:4 * dr + 4].unsqueeze(2).to_broadcast([P, 4, HD]),
                                        16.0, None, ALU.mult)
            signal(last, laret_ready)
            for c in range(6):
                for t in (range(NT) if c in (1, 4) else ()):
                    move(f"vg0{c}{t}", vtok[:, t, (c // 3) * 512:(c // 3 + 1) * 512])
                sum_mods("ev_in", c)
            dve.wait_ge(mix0_in, 80)
            free(v_.tensor_copy(lrT[0:32, :], ready("lr0")[0:32, :]), "lr0")
            heads = lambda a: a.rearrange("p (h n) -> p h n", h=4)

            def decay_of(t, dr, which):
                return dec[:, t, dr, :, which:which + 1].to_broadcast([P, 4, P])

            def enter(dr, t):
                signal(v_.tensor_tensor(heads(carried[:, CARRY[(dr, t)], :]), heads(carried[:, roll[dr], :]),
                                 decay_of(t, dr, 0), ALU.mult), carried_ready)
                carried_no[0] += 1
                dve.wait_ge(carried_ready, carried_no[0])

            def added(dr, t, slot):
                name = f"kv{t}{dr}"
                dst = carried[:, slot, :] if slot is not None else la
                free(v_.tensor_tensor(heads(dst), heads(ready(name)), decay_of(t, dr, 1), ALU.mult), name)
                dve.wait_ge(*moved(name))
                return dst

            def pass_tile(dr, t, add):
                r = carried[:, roll[dr], :]
                step(v_.tensor_tensor(heads(r), heads(r), decay_of(t, dr, 2), ALU.mult))
                step(v_.tensor_tensor(r, r, add, ALU.add))

            def states(t):
                dve.wait_ge(*moved(f"dec{t}"))
                held = CARRY[(1, 3)]
                if t == 0:
                    added(0, 0, roll[0])
                    added(1, 0, held)
                elif t == 1:
                    enter(0, 1)
                    pass_tile(0, 1, added(0, 1, None))
                    added(1, 1, roll[1])
                    enter(1, 0)
                    pass_tile(1, 0, carried[:, held, :])
                elif t == 2:
                    enter(0, 2)
                    pass_tile(0, 2, added(0, 2, None))
                else:
                    enter(1, 3)
                    pass_tile(1, 3, added(1, 3, None))
                    enter(0, 3)
                    enter(1, 2)

            carried_no = [0]

            for t in range(NT):
                z = ready(f"z{t}")
                if t > 0:
                    dve.wait_ge(*moved(f"dec{t - 1}"))
                dve.wait_ge(zlog_ready, t + 1)
                free(v_.scalar_tensor_tensor(la, z, 0.0, zlog, ALU.min, ALU.subtract), f"z{t}")
                if t == 0:
                    dve.wait_ge(*moved("cumret"))
                    dve.wait_ge(*moved("decret"))
                    for c in (0, 3):
                        for i in range(4):
                            dve.wait_ge(*moved(f"qk0{c}{i}"))
                dve.wait_ge(*moved(f"cum{t}"))
                ts = slice(t * P, (t + 1) * P)
                for kind, ex in ((0, exp_ret), (1, exp_gla)):
                    for dst, blk, sign in ((qd, 0, 0), (kd, 4, 1)):
                        src = qkT[:, blk + 2 * kind:blk + 2 * kind + 2, ts]
                        for dr in range(2):
                            last = v_.tensor_tensor(dst[:, 4 * dr + 2 * kind:4 * dr + 2 * kind + 2, ts], src,
                                                    ex[:, sign, 2 * dr:2 * dr + 2, :], ALU.mult)
                signal(last, kd_ready)
                states(t)

            def keep(name, dst, mask, n=4):
                ready(name)
                free(v_.copy_predicated(dst, mask.bitcast(I32).unsqueeze(1).to_broadcast([P, n, P]),
                                   bank_of(name, n)), name)

            dve.wait_ge(mix0_in, 80)
            finish_mod(0, 4, 12)
            for c in (2, 5):
                for t in range(NT):
                    dve.wait_ge(*moved(f"vg0{c}{t}"))
            for t in range(NT):
                for half in range(2):
                    dve.wait_ge(*moved(f"sc{t}{half}0"))
                    keep(f"sc{t}{half}1", amask[:, 4 * half:4 * half + 4, :], cst("win1"))
                for half in range(2):
                    o = ready(f"o{t}{half}")
                    rate = hsum[:, 0:4]
                    sqf = sq.rearrange("p a b -> p (a b)")
                    dve.wait_ge(sq_ready, 2 * t + half + 1)
                    step(v_.tensor_reduce(rate, (sqb, la)[half].rearrange("p (h d) -> p h d", h=4), AX.X, ALU.add))
                    root(v_.tensor_scalar(rate, rate, 1.0 / P, RMS_EPS, ALU.mult, ALU.add), rate)
                    free(v_.tensor_tensor(sqf.rearrange("p (h d) -> p h d", h=4), o.rearrange("p (h d) -> p h d", h=4),
                                          rate.unsqueeze(2).to_broadcast([P, 4, P]), ALU.mult), f"o{t}{half}")
                    dve.wait_ge(*moved(f"o{t}{half}"))
                    step(v_.tensor_tensor(sq[:, 2:4], sq[:, 2:4], normg.unsqueeze(1).to_broadcast([P, 2, P]), ALU.mult))
                    gs = gtok[:, t, :].rearrange("p (h j d) -> p h j d", j=2, d=P)[:, :, half, :]
                    signal(v_.tensor_tensor(gs, gs, sq, ALU.mult), y_ready)
            for t in range(NT):
                residual_norm(0, "out", t)
            modulate("mlp0")
            mlp(0, range(NT))

            modulate("mix1")
            for t in range(NT):
                move(f"v1{t}", v1[:, t, :], bank(f"v1{t}")[:, 0:T])
            dve.wait_ge(rope_in, 16)
            cos = rope[:, 0:1, :].to_broadcast([P, 2, T])
            sin = rope[:, 1:2, :].to_broadcast([P, 2, T])
            for b in range(5):
                o = ready(f"rot{b}")
                src = q_raw[:, 2 * b:2 * b + 2, :] if b < 4 else k_raw
                dst = qT[:, 2 * b:2 * b + 2, :] if b < 4 else kT[:, :, T:2 * T]
                rt3 = rope_t.rearrange("p (a n) -> p a n", a=2)
                free(v_.tensor_tensor(rt3, bank_of(f"rot{b}", 2), sin, ALU.mult), f"rot{b}")
                for n in ([f"q1{b // 2}{b % 2}"] if b < 4 else ["k10", "k11"]):
                    dve.wait_ge(*moved(n))
                step(v_.tensor_tensor(src, src, cos, ALU.mult))
                dve.wait_ge(*moved(f"rot{b}"))
                signal(v_.tensor_tensor(dst, src, rt3, ALU.add), roped)
            dve.wait_ge(roped, 5)
            signal(v_.tensor_copy(kTx[0:HD], kT[HD:P]), roped)
            signal(v_.tensor_copy(kTx[HD:P], kT[0:HD]), roped)
            dve.wait_ge(sink_in, 16)
            for i in range(2):
                for g in range(4):
                    n = 4 * i + g
                    for a in range(4):
                        step(v_.tensor_reduce(mx1[:, a:a + 1], ready(f"lg1{i}{g}{a}"), AX.X, ALU.max))
                    step(v_.scalar_tensor_tensor(mx1, mx1, HD ** -0.5, sinkb[:, 4 * g:4 * g + 4], ALU.mult, ALU.max))
                    step(v_.tensor_tensor(sexp1, sinkb[:, 4 * g:4 * g + 4], mx1, ALU.subtract))
                    signal(v_.tensor_scalar(negm1, mx1, -1.0, None, ALU.mult), negm_ready)
                    if n > 0:
                        dve.wait_ge(bank_full, full(f"o1{(n - 1) // 4}{(n - 1) % 4}"))
                    for a in (1, 3):
                        move(f"eT1{i}{g}{a}", eT1[:, a, :])
                    dve.wait_ge(sexp_ready, n + 1)
                    den = den1[:, 4 * n:4 * n + 4]
                    step(v_.tensor_tensor(den, den, sexp1, ALU.add))
                    step(v_.reciprocal(den, den))
                    name = f"o1{i}{g}"
                    o = ready(name)[:, 0:T].rearrange("p (h d) -> p h d", h=4)
                    free(v_.tensor_tensor(y1[:, i, g * T:(g + 1) * T].rearrange("p (h d) -> p h d", h=4), o,
                                     den.unsqueeze(2).to_broadcast([P, 4, HD]), ALU.mult), name)
            for t in (2, 3):
                residual_norm(1, "out", t)
            modulate("mlp1")
            mlp(1, (2, 3))

            def rms_rows(tiles=(0, 1)):
                for t in tiles:
                    x = xres[:, X0 + t, :]
                    step(v_.tensor_tensor_reduce(out=xn[:, t, :], in0=x, in1=x, scale=1.0, scalar=0.0, op0=ALU.mult,
                                                 op1=ALU.add, accum_out=lnr))
                    root(v_.tensor_scalar(lnr, lnr, 1.0 / D, RMS_EPS, ALU.mult, ALU.add), lnr)
                    signal(v_.tensor_scalar(xn[:, t, :], x, lnr, None, ALU.mult), xn_ready)

            step(v_.tensor_tensor(lbc, cols[:, 88:92], cols[:, 92:96], ALU.subtract))
            signal(v_.tensor_copy(olb, lbc), lbd_ready)
            rms_rows()
            modulate("mix2")
            dve.wait_ge(lbs_ready, 1)
            step(v_.tensor_scalar(olb, lbc, -1.0, 1.0, ALU.mult, ALU.add))
            step(v_.tensor_scalar(mod3[:, 0:4], olb, -1.0, None, ALU.mult))
            for b in range(2):
                dve.wait_ge(*moved(f"f20{b}"))
                dve.wait_ge(*moved(f"f21{b}"))
            for h in range(4):
                last = v_.tensor_scalar(rkT[:, h, :], rsig[:, h, :], mod3[:, h:h + 1], olb[:, h:h + 1], ALU.mult, ALU.add)
            signal(last, kln_ready)
            dve.wait_ge(kln_ready, 1)
            for h in range(4):
                last = v_.tensor_scalar(rsig[:, h, :], rsig[:, h, :], olb[:, h:h + 1], lbc[:, h:h + 1], ALU.mult, ALU.add)
            signal(last, rfs_ready)
            for t in range(2):
                move(f"t22{t}", rv[:, t, :])
            dve.wait_ge(l2_in, 160)
            for n in range(2):
                for t in range(2):
                    dst = (aq, ak)[n][:, t, :]
                    name = f"t2{4 + n}{t}"
                    o = ready(name)
                    if n == 0 and t == 0:
                        dve.wait_ge(lev_in, 16)
                    free(v_.tensor_copy(dst, o), name)
                    dve.wait_ge(*moved(name))
                    head_rate(dst, 8, st8, sq2, HD)
                    d3 = dst.rearrange("p (h d) -> p h d", h=8)
                    step(v_.tensor_tensor(d3, d3, st8.unsqueeze(2).to_broadcast([P, 8, HD]), ALU.mult))
                    signal(v_.tensor_tensor(d3, d3, qkg[:, n * HD:(n + 1) * HD].unsqueeze(1).to_broadcast([P, 8, HD]),
                                     ALU.mult), aqk_ready)
            for t in range(2):
                move(f"t26{t}", av[:, t, :])
            for t in range(2):
                name = f"t28{t}"
                o = ready(name)
                step(v_.bn_stats(ik_st, o[:, 0:HD]))
                step(v_.bn_aggr(ik_ag, ik_st))
                root(v_.tensor_scalar(lnr, ik_ag[:, 1:2], RMS_EPS, None, ALU.add), lnr)
                step(v_.tensor_scalar(ikd[:, t, 0:HD], o[:, 0:HD], ik_ag[:, 0:1], lnr, ALU.subtract, ALU.mult))
                step(v_.tensor_tensor(ikd[:, t, 0:HD], ikd[:, t, 0:HD], ikn[:, 0:HD], ALU.mult))
                step(v_.tensor_tensor(ikd[:, t, 0:HD], ikd[:, t, 0:HD], ikn[:, HD:P], ALU.add))
                free(v_.tensor_scalar(iwt[:, t, :], o[:, HD:HD + 8], 8.0 ** -0.5, None, ALU.mult), name)
                dve.wait_ge(*moved(name))
                signal(v_.tensor_copy(ikd[:, t, HD:P], ikd[:, t, 0:HD]), ik_ready)
            free(v_.tensor_copy(relE[0:8, 0:2 * T - 1], ready("rel")[0:8, 0:2 * T - 1]), "rel")
            dve.wait_ge(lf_ready, 1)
            step(v_.tensor_tensor_scan(rb.rearrange("p a b -> p (a b)"), levels[:, len(LEVELS) * P:],
                                       rsig.rearrange("p a b -> p (a b)"), 0.0, ALU.mult, ALU.add))
            dve.sem_inc(sc_ready, 1)
            for i in range(2):
                for b in range(4):
                    dve.wait_ge(*moved(f"ix{i}{b}"))
                    for j in range(2):
                        head = 4 * (b // 2) + 2 * j + b % 2
                        w = iwt[:, i, head:head + 1]
                        if b == 0 and j == 0:
                            last = v_.tensor_scalar(score[:, i, :], sc_r[:, j, :], w, None, ALU.mult)
                        else:
                            last = v_.scalar_tensor_tensor(score[:, i, :], sc_r[:, j, :], w, score[:, i, :],
                                                           ALU.mult, ALU.add)
                        if j == 0:
                            step(last)
                        else:
                            signal(last, sc_ready)
                            dve.wait_ge(sc_ready, 4 * i + b + 2)
            for i in range(2):
                if i == 0:
                    v_.memset(score[0:64, 0, 64:T], INADMISSIBLE)
                    step(v_.memset(score[64:P, 0, P:T], INADMISSIBLE))
                else:
                    step(v_.memset(score[0:64, 1, 192:T], INADMISSIBLE))
                cur = score[:, i, :]
                for r in range(8):
                    step(v_.max(max8, cur))
                    step(v_.match_replace(work[:, i, :], max8, cur, TAKEN))
                    cur = work[:, i, :]
                step(v_.tensor_scalar(negsel[:, i, :], work[:, i, :], TAKEN, 1.0, ALU.is_equal, ALU.subtract))
            dve.wait_ge(amat_zero, 1)
            flat = rb.rearrange("p a b -> p (a b)")
            eflat = edec.rearrange("p a b -> p (a b)")
            for n in range(len(LEVELS) + 1):
                if n > 0:
                    dve.wait_ge(ql_ready, n)
                    dve.wait_ge(kl_ready, n)
                if n < len(LEVELS):
                    L = LEVELS[n]
                    s4 = flat.rearrange("p (b h n) -> p b h n", h=2, n=L)
                    d4 = eflat.rearrange("p (b h n) -> p b h n", h=2, n=L)
                    mid = s4[:, :, 0, L - 1:L].to_broadcast([P, 4 * T // (2 * L), L])
                    v_.tensor_tensor(d4[:, :, 0, :], mid, s4[:, :, 0, :], ALU.subtract)
                    signal(v_.tensor_tensor(d4[:, :, 1, :], s4[:, :, 1, :], mid, ALU.subtract), diff_ready)
                else:
                    v_.tensor_tensor(edec[:, :, 0:P], rb[:, :, P - 1:P].to_broadcast([P, 4, P]), rb[:, :, 0:P], ALU.subtract)
                    signal(v_.tensor_copy(edec[:, :, P:T], rb[:, :, P:T]), diff_ready)
                dve.wait_ge(edec_ready, n + 1)
                if n > 0:
                    dve.wait_ge(bank_full, full(f"lev{n - 1}1"))
                signal(v_.tensor_tensor(ql, rqT, edec, ALU.mult), ql_ready)
                for t in range(2):
                    if n < len(LEVELS):
                        keep(f"lev{n}{t}", amat[:, t], levels[:, n * P:(n + 1) * P])
            for t in range(2):
                keep(f"lev{len(LEVELS)}{t}", amat[:, t], ident)
            move("across", across, bank_of("across", 4))
            dve.wait_ge(rowg_in, 32)
            for t in range(2):
                dve.wait_ge(*moved(f"t23{t}"))
            for t in range(2):
                name = f"ro{t}"
                o = ready(name)
                m = mix[:, t, 0:512]
                m3 = m.rearrange("p (h d) -> p h d", h=4)
                free(v_.tensor_copy(m, o), name)
                dve.wait_ge(*moved(name))
                head_rate(m, 4, st8[:, 0:4], ubuf3, P)
                step(v_.tensor_tensor(m3, m3, st8[:, 0:4].unsqueeze(2).to_broadcast([P, 4, P]), ALU.mult))
                step(v_.tensor_tensor(m, m, rowg[:, 0, :], ALU.mult))
                signal(v_.tensor_tensor(m, m, rg[:, t, :], ALU.mult), mix_ready)
            for i in range(2):
                dve.wait_ge(rel_in, 16 * (i + 1))
                if i == 1:
                    dve.wait_ge(bank_full, full("eT203"))
                signal(v_.scalar_tensor_tensor(logit, negsel[:, i, :].unsqueeze(1).to_broadcast([P, 8, T]), -NEG,
                                        biasT[:, :, ::-1], ALU.mult, ALU.add), bias_used)
                dve.wait_ge(bias_used, i + 1)
                for b in range(4):
                    name = f"lg2{i}{b}"
                    ready(name)
                    pair = logit.rearrange("p (m n j) k -> p m n j k", n=2, j=2)[:, b // 2, :, b % 2, :]
                    free(v_.scalar_tensor_tensor(pair, bank_of(name, 2), HD ** -0.5, pair, ALU.mult, ALU.add), name)
                dve.wait_ge(*moved(f"lg2{i}3"))
                step(v_.tensor_reduce(mx2, logit, AX.X, ALU.max))
                signal(v_.tensor_scalar(neg2, mx2, -1.0, None, ALU.mult), neg2_ready)
                dve.wait_ge(e2_ready, 8 * (i + 1))
                step(v_.reciprocal(mx2, den2))
                name = f"att{i}"
                o = ready(name)
                m = mix[:, i, 512:D]
                m3 = m.rearrange("p (h d) -> p h d", h=8)
                free(v_.tensor_tensor(m3, o.rearrange("p (h d) -> p h d", h=8), mx2.unsqueeze(2).to_broadcast([P, 8, HD]),
                                 ALU.mult), name)
                dve.wait_ge(*moved(name))
                head_rate(m, 8, st8, ubuf3, HD)
                step(v_.tensor_tensor(m3, m3, st8.unsqueeze(2).to_broadcast([P, 8, HD]), ALU.mult))
                signal(v_.tensor_tensor(m, m, rowg[:, 1, :], ALU.mult), mix_ready)
            for t in range(2):
                for half in range(2):
                    residual(2, "out2", half, (X0 + t,), alpha=1.0)
                rms_rows((t,))
            modulate("moe")
            o = ready("router")
            free(v_.tensor_tensor(lg, o[:, 0:40].rearrange("p (t e) -> p t e", t=2),
                             brr.unsqueeze(1).to_broadcast([P, 2, 20]), ALU.add), "router")
            dve.wait_ge(*moved("router"))
            pick = cst("pick")
            four = lambda a: a.unsqueeze(1).to_broadcast([P, 2, 4])
            each = lambda a: a.unsqueeze(2).to_broadcast([P, 2, 4])

            def first_largest(vals, top, hot):
                step(v_.tensor_reduce(top, vals, AX.X, ALU.max))
                step(v_.tensor_tensor(hot, vals, each(top), ALU.is_equal))
                step(v_.tensor_tensor(hot, hot, four(pick), ALU.mult))
                step(v_.tensor_reduce(rt_m, hot, AX.X, ALU.max))
                step(v_.tensor_tensor(hot, hot, each(rt_m), ALU.is_equal))

            first_largest(lg[:, :, 0:4], rt_g, rt_hg)
            prod = rt_p.rearrange("p (t g e) -> p t g e", t=2, g=4)
            e4 = lg[:, :, 4:20].rearrange("p t (g e) -> p t g e", g=4)
            for t in range(2):
                step(v_.tensor_tensor(prod[:, t], e4[:, t], rt_hg[:, t].unsqueeze(2).to_broadcast([P, 4, 4]), ALU.mult))
                step(v_.tensor_reduce(rt_e[:, t], prod[:, t].rearrange("p g e -> p e g"), AX.X, ALU.add))
            first_largest(rt_e, rt_1, rt_h1)
            step(v_.scalar_tensor_tensor(rt_e2, rt_h1, INADMISSIBLE, rt_e, ALU.mult, ALU.add))
            first_largest(rt_e2, rt_2, rt_h2)
            rt_x4 = rt_exp.rearrange("p (t e) -> p t e", t=2)
            step(v_.tensor_tensor(rt_x4[:, :, 0:4], lg[:, :, 0:4], each(rt_g), ALU.subtract))
            signal(v_.tensor_tensor(rt_x4[:, :, 4], rt_2, rt_1, ALU.subtract), route_ready)
            dve.wait_ge(route_exp, 1)
            step(v_.tensor_reduce(rt_g, rt_x4[:, :, 0:4], AX.X, ALU.add))
            step(v_.reciprocal(rt_g, rt_g))
            step(v_.tensor_scalar(rt_1, rt_x4[:, :, 4], 1.0, None, ALU.add))
            step(v_.reciprocal(rt_1, rt_1))
            step(v_.tensor_tensor(rt_1, rt_1, rt_g, ALU.mult))
            step(v_.tensor_tensor(rt_2, rt_1, rt_x4[:, :, 4], ALU.mult))
            step(v_.tensor_tensor(rt_h1, rt_h1, each(rt_1), ALU.mult))
            step(v_.tensor_tensor(rt_h2, rt_h2, each(rt_2), ALU.mult))
            step(v_.tensor_tensor(rt_h1, rt_h1, rt_h2, ALU.add))
            c4 = comb.rearrange("p t (g e) -> p t g e", g=4)
            for t in range(2):
                step(v_.tensor_tensor(c4[:, t], rt_h1[:, t].unsqueeze(1).to_broadcast([P, 4, 4]),
                                      rt_hg[:, t].unsqueeze(2).to_broadcast([P, 4, 4]), ALU.mult))
            for q in range(4):
                signal(v_.memset(yacc[:, q % 2, (q // 2) * 512:(q // 2 + 1) * 512], 0.0), yacc_step)
            base = bank_no["moe"]
            with dve.Fori(0, TURNS) as turn_no:
                for j in range(BODY):
                    for u in range(4):
                        b = (base + 8 * j + u) % BANKS
                        dve.wait_ge(sg_ready, turn_no * (4 * BODY) + (4 * j + u + 1))
                        dve.wait_ge(bank_full, turn_no * MOE_BANKS + (base + 8 * (j - 1)))
                        v_.tensor_tensor(he[:, j % 2, u, :], psum[:, b, T:2 * T], sg[:, j % 2, u, :],
                                         ALU.mult).then_inc(bank_freed[b], 1)
                    for q in range(4):
                        i = base + 8 * j + 4 + q
                        n, t = q // 2, q % 2
                        y = yacc[:, t, n * 512:(n + 1) * 512]
                        dve.wait_ge(bank_full, turn_no * MOE_BANKS + (i + 1))
                        dve.wait_ge(yacc_step, turn_no * (4 * BODY) + (4 * j + q + 1))
                        step_bank = psum[:, i % BANKS, :]
                        v_.scalar_tensor_tensor(y, step_bank, comb[:, t, bass.ds(turn_no * BODY + j, 1)], y,
                                                ALU.mult, ALU.add).then_inc(yacc_step, 1)
                        dve.wait_ge(yacc_step, turn_no * (4 * BODY) + (4 * j + q + 5))
                        dve.sem_inc(bank_freed[i % BANKS], 1)
            for c in range(2):
                dve.wait_ge(*moved(f"gate21{c}1"))
            for t in range(2):
                step(v_.tensor_tensor(yacc[:, t, :], yacc[:, t, :], gate[:, 1, :], ALU.mult))
                step(v_.tensor_tensor(xres[:, X0 + t, :], xres[:, X0 + t, :], yacc[:, t, :], ALU.add))
            for t in range(2):
                signal(v_.tensor_copy(junk, const[:, 0:1]), final_ready)


_INS = ["x", "c", "ctx", "c_ctx", "w_mod", "b_mod", "ln_g", "ln_b", "mlp_w1", "mlp_w2", "ev_w_in", "ev_ret_theta",
        "ev_gla_gk_w", "ev_gla_gk_b", "ev_gla_norm_g", "ev_w_out", "od_w_qkv", "od_sink", "od_w_out", "c_2",
        "w_ada_2", "b_ada_2", "norm1_g_2", "norm2_g_2", "w_in_2", "lb_logits_2", "rec_out_g_2", "q_norm_g_2",
        "k_norm_g_2", "idx_k_norm_g_2", "idx_k_norm_b_2", "attn_out_g_2", "rel_bias_2", "w_out_2", "w_rg_2",
        "b_rg_2", "w_re_2", "b_re_2", "w1_2", "w3_2", "w2_2"]


def kernel(**inputs):
    import numpy as _np
    import concourse.bacc as _bacc
    from concourse import mybir as _mybir
    from concourse.bass_utils import run_bass_kernel_spmd as _run

    nc = _bacc.Bacc("TRN2", target_bir_lowering=False, num_devices=1)
    arrays, aps = {}, {}
    for name, a in {**{n: inputs[n] for n in _INS}, **shape_constants()}.items():
        a = _np.ascontiguousarray(a)
        arrays[f"in_{name}"] = a
        aps[name] = nc.dram_tensor(f"in_{name}", a.shape, _mybir.dt.from_np(a.dtype), kind="ExternalInput").ap()
    out = nc.dram_tensor("out_x", (1, T, D), F32, kind="ExternalOutput").ap()
    build(nc, aps, out)
    r = _run(nc, [arrays], core_ids=[0])
    return r.results[0]["out_x"]
```

```python
from contextlib import ExitStack

import numpy as np

import concourse.bass as bass
from concourse import mybir

ALU = mybir.AluOpType
ACT = mybir.ActivationFunctionType
AX = mybir.AxisListType
F32 = mybir.dt.float32
I32 = mybir.dt.int32

P = 128
D = 1024
KC = D // P
T = 256
NT = 4
X0 = 2
DFF = 4 * D
ALPHA = 4.0 ** 0.25
LN_EPS = 1e-5
RMS_EPS = 1e-6
RING = 4
BANKS = 8
HD = 64
NEXP = 16
BODY = 4
NEG = -1.0e30
INADMISSIBLE = -2.0e38
TAKEN = -3.0e38
NBUCKET = 32
MIDREF = P // 2


CONST_COLS = {}


def _place(names):
    at = 0
    for name, width in names:
        CONST_COLS[name] = (at, at + width)
        at += width
    return at


CONST_W = _place([("ident", P), ("cum_f", P), ("cum_b", P), ("dec_f", 3), ("dec_b", 3), ("perm", P),
                  ("win0", P), ("win1", P), ("pick", 4),
                  ("ones", 1)])
LEVELS = [64, 32, 16, 8, 4, 2, 1]
LEVEL_W = P * len(LEVELS) + 4 * T


def shape_constants():
    c = np.zeros((P, CONST_W), np.float32)
    r, t = np.arange(P)[:, None], np.arange(P)[None, :]

    def put(name, value):
        a, b = CONST_COLS[name]
        c[:, a:b] = value

    put("ident", r == t)
    first_f, first_b = (r < MIDREF), (r >= MIDREF)
    put("cum_f", ((r <= t) * 1.0 - first_f) / 16.0)
    put("cum_b", ((r >= t) * 1.0 - first_b) / 16.0)
    put("dec_f", np.concatenate([first_f, ~first_f, np.ones((P, 1))], 1) / 16.0)
    put("dec_b", np.concatenate([first_b, ~first_b, np.ones((P, 1))], 1) / 16.0)
    d = np.arange(P) % 32
    perm = np.zeros((P, P))
    for m in range(P):
        if m % 32 < 16:
            perm[m + 16, m] = -1.0
        else:
            perm[m - 16, m] = 1.0
    put("perm", perm)
    inv = (10000.0 ** (-np.arange(0, 32, 2) / 32.0)).astype(np.float32)
    tok = np.arange(T)
    pos = np.where((np.arange(P)[:, None] % 64) < 32, tok[None, :] // 64, tok[None, :] % 64).astype(np.float32)
    ang = (pos * inv[d % 16][:, None]).astype(np.float32)
    rope = np.concatenate([np.cos(ang.astype(np.float64)), np.sin(ang.astype(np.float64))], 1).astype(np.float32)
    put("win0", np.where(t > r, NEG, 0.0))
    put("win1", np.where(r > t, NEG, 0.0))
    put("pick", np.array([[4.0, 3.0, 2.0, 1.0]]))
    put("ones", 1.0)
    lv = np.zeros((P, LEVEL_W), np.float32)
    for n, size in enumerate(LEVELS):
        same = (r // (2 * size)) == (t // (2 * size))
        lv[:, n * P:(n + 1) * P] = same & (r % (2 * size) < size) & (t % (2 * size) >= size)
    go = np.ones(4 * T)
    go[::P] = 0.0
    lv[:, len(LEVELS) * P:] = go
    rel = (T - 1) - np.arange(2 * T - 1)
    n = np.abs(rel)
    large = 8 + np.floor(np.log2(np.maximum(n, 1) / 8.0) * 2 + 1e-9).astype(int)
    bucket = np.where(rel > 0, 16, 0) + np.where(n < 8, n, np.minimum(large, 15))
    hot = (bucket[None, :] == np.arange(NBUCKET)[:, None]).astype(np.float32)
    return {"const_main": c, "const_rope": rope, "const_levels": lv, "const_buckets": hot}


def _deal(chunks, counts):
    chunks = list(chunks)
    return [[chunks.pop(0) for _ in range(n)] for n in counts]


BESIDE = {
    "ev_in": _deal([(0, c) for c in range(4, 12)], (1, 2, 1, 2, 1, 1, 0)),
    "up0": _deal([(1, c) for c in range(12)] + [(2, c) for c in range(2)], (2, 2, 2, 2, 2, 2, 2, 0)),
    "up1": _deal([(2, c) for c in range(2, 12)], (2, 1, 1, 2, 1, 2, 1, 0)),
}
SUMMED = [m for name in ("ev_in", "up0", "up1") for group in BESIDE[name] for m in group]


def due(name, c, f):
    group = BESIDE[name][c - 1] if c > 0 else []
    return group[f // 2] if f in (0, 2) and f // 2 < len(group) else None


def vectors(l):
    return 2 if l < 2 else 1


W_IN_FIRST = (0, 3, 1, 8, 7)
W_IN_BESIDE = (4, 5, 2, 6)


def weight_stream():
    def part(name, lo, hi):
        return [(name, c) for c in range(lo, hi)]

    def with_mods(name, n):
        s = []
        for c in range(n):
            s += [(name, c)] + [(f"mod{l}", m) for l, m in BESIDE[name][c]]
        return s

    return (part("mod0", 0, 4) + with_mods("ev_in", 7) + part("out0", 0, 2)
            + with_mods("up0", 8) + part("down0", 0, 8) + part("od_qkv", 0, 3)
            + part("out1", 0, 2) + with_mods("up1", 8) + part("down1", 0, 8)
            + [("w_in", c) for c in W_IN_FIRST + W_IN_BESIDE] + part("out2", 0, 2))


def build(nc, I, out):
    STREAM = weight_stream()
    load_no = {key: n for n, key in enumerate(STREAM)}
    MOE_LOAD0 = len(STREAM)
    LOADS_PER_TURN = 3 * BODY
    TURNS = NEXP // BODY

    with ExitStack() as ctx:
        def sb(name, shape, dt=F32):
            return ctx.enter_context(nc.sbuf_tensor(name, shape, dt))

        def sem(name):
            return ctx.enter_context(nc.semaphore(name))

        psum = ctx.enter_context(nc.psum_tensor("psum", [P, BANKS, 512], F32))
        wring = sb("wring", [P, RING, KC, 512])
        xres = sb("xres", [P, NT, D])
        hT = sb("hT", [P, KC, 512])
        big = sb("big", [P, 16384])
        gate = sb("gate", [P, 2, D])
        lnb = sb("lnb", [P, 2, D])
        tmp = sb("tmp", [P, 22 * 256])
        const = sb("const", [P, CONST_W])
        cols = sb("cols", [P, 192])
        csilu = sb("csilu", [P, 24])
        modc = sb("modc", [P, 3, 6 * KC, 2])
        small = sb("small", [P, 592])

        def cst(name, rows=P):
            a, b = CONST_COLS[name]
            return const[0:rows, a:b]

        ident = cst("ident")

        def region(base, at, *shape):
            n = int(np.prod(shape))
            v = base[:, at:at + n]
            if len(shape) == 1:
                return v
            names = "abcd"[:len(shape)]
            return v.rearrange(f"p ({' '.join(names)}) -> p {' '.join(names)}",
                               **{names[i]: shape[i] for i in range(1, len(shape))})

        CARRY = {(0, 1): 0, (0, 2): 1, (0, 3): 2, (1, 0): 3, (1, 3): 4, (1, 2): 5}
        qkT = region(big, 0, 8, 512)
        vtok = region(big, 4096, NT, D)
        gtok = region(big, 8192, NT, D)
        qd = region(big, 12288, 8, 512)
        kd = hT
        yT = region(big, 0, KC, 512)
        h1T = region(big, 0, 32, 512)
        rows1 = region(big, 0, P)
        rows2 = region(big, P, P)
        exp_ret = region(tmp, 0, 2, 4, P)
        exp_gla = region(tmp, 1024, 2, 4, P)
        amask = region(tmp, 0, 8, P)
        sq = region(tmp, 1024, 4, P)
        sqb = region(tmp, 1536, 512)
        la = region(tmp, 2048, 512)
        modrow = region(tmp, 0, 4, 512)
        modsum = region(tmp, 2560, 2, 2, 512)
        carried = region(tmp, 2560, 6, 512)
        las = (carried[:, CARRY[(0, 1)], :], carried[:, CARRY[(1, 0)], :], carried[:, CARRY[(0, 2)], :], la)
        roll = {0: CARRY[(0, 3)], 1: CARRY[(1, 2)]}
        ktok = region(lnb[:, :, :].rearrange("p a b -> p (a b)"), 0, 8, P)
        passing = region(lnb[:, :, :].rearrange("p a b -> p (a b)"), 1536, 512)
        gkw = region(gate[:, :, :].rearrange("p a b -> p (a b)"), 0, 512)
        la_ret = region(gate[:, :, :].rearrange("p a b -> p (a b)"), 512, 512)
        normg = region(gate[:, :, :].rearrange("p a b -> p (a b)"), 1024, P)
        theta = region(gate[:, :, :].rearrange("p a b -> p (a b)"), 1152, 8)
        dec = region(gate[:, :, :].rearrange("p a b -> p (a b)"), 1160, NT, 2, 4, 3)
        lrT = region(gate[:, :, :].rearrange("p a b -> p (a b)"), 1280, 512)
        q_raw = region(big, 0, 8, T)
        k_raw = region(big, 2048, 2, T)
        qT = region(big, 2560, 8, T)
        kT = region(big, 4608, 2, 512)
        kTx = region(big, 14848, 2, 512)
        v1 = region(big, 5632, NT, T)
        rope = region(big, 14336, 2, T)
        e1 = region(big, 6656, 4, 512)
        rope_t = region(big, 6656, 512)
        eT1 = region(big, 8704, 4, 512)
        y1 = region(big, 12288, 2, D)
        yT1 = region(big, 0, KC, T)
        sinkb = region(small, 0, 16)
        mx1 = region(small, 16, 4)
        negm1 = region(small, 576, 2, 4)
        den1 = region(small, 24, 32)
        sexp1 = region(small, 584, 2, 4)
        lnstat = region(small, 64, 2, 6)
        lnagg = region(small, 76, 2)
        lnr = region(small, 78, 1)
        hsum = region(small, 80, 8)
        rqT = region(big, 0, 4, T)
        rkT = region(big, 1024, 4, T)
        rb = region(big, 2048, 4, T)
        rsig = region(big, 3072, 4, T)
        rv = region(big, 4096, 2, 512)
        rg = region(big, 5120, 2, 512)
        aq = region(big, 6144, 2, 512)
        ak = region(big, 7168, 2, 512)
        av = region(big, 8192, 2, 512)
        iqT = region(big, 9216, 4, T)
        aqT = region(big, 10240, 4, T)
        akT = region(big, 11264, 4, T)
        mix = region(big, 12288, 2, D)
        ikd = region(big, 14336, 2, P)
        ikT = region(big, 14592, T)
        score = region(big, 14848, 2, T)
        work = region(big, 15360, 2, T)
        ikn = region(big, 15872, P)
        qkg = region(big, 16000, P)
        iwt = region(big, 16128, 2, 8)
        levels = region(tmp, 0, LEVEL_W)
        sc_r = region(tmp, 1920, 2, T)
        edec = region(tmp, 2432, 4, T)
        ql = region(tmp, 3456, 4, T)
        kl = region(tmp, 4480, 4, T)
        edecs = (edec, rsig)
        qls = (ql, region(lnb[:, :, :].rearrange("p a b -> p (a b)"), 0, 4, T))
        kls = (kl, region(lnb[:, :, :].rearrange("p a b -> p (a b)"), 1024, 4, T))
        amat = region(big, 13312, 2, 4, P)
        across = region(hT[:, :, :].rearrange("p a b -> p (a b)"), 1024, 4, P)
        rowg = region(hT[:, :, :].rearrange("p a b -> p (a b)"), 1536, 2, 512)
        relE = region(big, 12288, 512)
        relb = region(small, 520, 8)
        hot = region(big, 14848, 2 * T - 1)
        biasT = region(tmp, 0, 8, T)
        logits = (region(tmp, 2048, 8, T), region(big, 6144, 8, T))
        eT2 = region(big, 2048, 4, 512)
        yT2 = region(big, 0, KC, T)
        negsel = work
        sq2 = region(gate[:, :, :].rearrange("p a b -> p (a b)"), 0, 512)
        ubuf = region(tmp, 5120, 512)
        ubuf3 = region(big, 14848, 512)
        junk = region(small, 575, 1)
        half_neg = region(small, 528, 8)
        lbc = region(small, 96, 4)
        olb = region(small, 100, 4)
        mod3 = region(small, 104, 8)
        st8 = region(small, 112, 8)
        max8 = region(small, 120, 8)
        mx2 = region(small, 128, 8)
        neg2 = region(small, 536, 2, 8)
        den2 = region(small, 552, 2, 8)
        ik_st = region(small, 152, 6)
        ik_ag = region(small, 158, 2)
        xn = region(tmp, 0, 2, D)
        wr = region(small, 176, KC, 20)
        brr = region(small, 336, 20)
        lg = region(small, 356, 2, 20)
        comb = region(small, 396, 2, NEXP)
        rt_p = region(small, 428, 32)
        rt_g = region(small, 460, 2)
        rt_m = region(small, 462, 2)
        rt_1 = region(small, 464, 2)
        rt_2 = region(small, 466, 2)
        rt_hg = region(small, 468, 2, 4)
        rt_h1 = region(small, 476, 2, 4)
        rt_h2 = region(small, 484, 2, 4)
        rt_e = region(small, 492, 2, 4)
        rt_e2 = region(small, 500, 2, 4)
        rt_exp = region(small, 508, 10)
        sg = region(big, 2048, 2, 4, T)
        he = region(big, 4096, 2, 4, T)
        yacc = region(big, 8192, 2, D)

        rel_scratch = nc.dram_tensor("rel_scratch", [8, 2 * T - 1], F32, kind="Internal").ap()

        w_landed = [sem(f"w_landed{s}") for s in range(RING)]
        w_used = sem("w_used")
        bank_full = sem("bank_full")
        bank_freed = [sem(f"bank_freed{b}") for b in range(BANKS)]
        consts_in = sem("consts_in")
        rows_in = sem("rows_in")
        x_in = sem("x_in")
        mix0_in = sem("mix0_in")
        ln_in = sem("ln_in")
        sink_in = sem("sink_in")
        rope_in = sem("rope_in")
        rate_ready = sem("rate_ready")
        rate_done = sem("rate_done")
        bias_used = sem("bias_used")
        relu_ready = sem("relu_ready")
        l2_in = sem("l2_in")
        lev_in = sem("lev_in")
        rowg_in = sem("rowg_in")
        rel_out = sem("rel_out")
        rel_in = sem("rel_in")
        out_done = sem("out_done")
        act_step = sem("act_step")
        dve_step = sem("dve_step")
        pool_step = sem("pool_step")
        csilu_ready = sem("csilu_ready")
        modc_ready = sem("modc_ready")
        gkw_ready = sem("gkw_ready")
        laret_ready = sem("laret_ready")
        theta_exp = sem("theta_exp")
        zlog_ready = sem("zlog_ready")
        kd_ready = sem("kd_ready")
        carried_ready = sem("carried_ready")
        y_ready = sem("y_ready")
        mod_summed = sem("mod_summed")
        sq_ready = sem("sq_ready")
        x_ready = sem("x_ready")
        roped = sem("roped")
        negm_ready = sem("negm_ready")
        e_ready = sem("e_ready")
        xn_ready = sem("xn_ready")
        lf_ready = sem("lf_ready")
        aqk_ready = sem("aqk_ready")
        ik_ready = sem("ik_ready")
        diff_ready = sem("diff_ready")
        edec_ready = sem("edec_ready")
        ql_ready = sem("ql_ready")
        kl_ready = sem("kl_ready")
        neg2_ready = sem("neg2_ready")
        e2_ready = sem("e2_ready")
        mix_ready = sem("mix_ready")
        final_ready = sem("final_ready")
        amat_zero = sem("amat_zero")
        kln_ready = sem("kln_ready")
        rfs_ready = sem("rfs_ready")
        sexp_ready = sem("sexp_ready")
        sc_ready = sem("sc_ready")
        lbd_ready = sem("lbd_ready")
        lbs_ready = sem("lbs_ready")
        yacc_step = sem("yacc_step")
        sg_ready = sem("sg_ready")
        route_ready = sem("route_ready")
        route_exp = sem("route_exp")

        rates = []
        slot_free = {}
        ROWS_DMAS = 9
        L2_DMAS = 10
        bank_no = {}
        MOE_BANKS = 8 * BODY

        def full(name):
            return bank_no[name] + 1

        def bank(name):
            return psum[:, bank_no[name] % BANKS, :]

        def freed(name):
            return bank_freed[bank_no[name] % BANKS]

        def moved(name):
            return freed(name), bank_no[name] // BANKS + 1

        def bank_of(name, n):
            return bank(name).rearrange("p (a n) -> p a n", a=n)

        stages = ["mix0", "mlp0", "mix1", "mlp1", "mix2", "moe"]
        MODC_DONE = {"mix0": 1, "mlp0": 2, "mix1": 3, "mlp1": 3, "mix2": 4, "moe": 4}

        block = ctx.enter_context(nc.Block())

        @block.tensor
        def _(pe):
            count, uses = [0], [0]

            def claim(name):
                i = count[0]
                count[0] += 1
                assert name not in bank_no
                bank_no[name] = i
                if i >= BANKS:
                    pe.wait_ge(bank_freed[i % BANKS], i // BANKS)
                return psum[:, i % BANKS, :]

            def weights(key):
                i = load_no[key]
                pe.wait_ge(w_landed[i % RING], 16 * (i // RING + 1))
                return wring[:, i % RING, :, :]

            def mm(o, a, b, first=True, last=True):
                return nc.tensor.matmul(o, a, b, start=first, stop=last)

            def turn(o, a):
                n = a.shape[0]
                return nc.tensor.transpose(o, a, ident[0:n, 0:n])

            def mod_rows():
                vec = csilu[:, 0:16].rearrange("p (v k) -> p k v", v=2)
                for c in range(4):
                    w = weights(("mod0", c))
                    o = claim(f"modrow{c}")
                    for k in range(KC):
                        last = mm(o[0:2, :], vec[:, k, :], w[:, k, :], k == 0, k == KC - 1)
                    last.then_inc(bank_full, 1)
                    release(("mod0", c))
                for c in range(4):
                    pe.wait_ge(*moved(f"modrow{c}"))
                    o = claim(f"mod0_{c}")
                    for f in range(4):
                        last = turn(o[:, 2 * f:2 * f + 2], modrow[0:2, c, f * P:(f + 1) * P])
                    last.then_inc(bank_full, 1)

            def open_sums(chunk):
                if chunk is None:
                    return []
                l, m = chunk
                V = vectors(l)
                n = SUMMED.index(chunk)
                done = sum(vectors(x) for x, _ in SUMMED[:n + 1])
                slot_free[load_no[(f"mod{l}", m)]] = (mod_summed, done)
                pe.wait_ge(mod_summed, done)
                o = claim(f"mod{l}_{m}")
                return [(o[:, f * V + v:f * V + v + 1], modsum[:, n % 2, v, f * P:(f + 1) * P])
                        for f in range(4) for v in range(V)]

            def take_sum(sums, k):
                if k < len(sums):
                    last = mm(sums[k][0], sums[k][1], cst("ones"))
                    if k == len(sums) - 1:
                        last.then_inc(bank_full, 1)

            def gate_rows(l, half):
                pe.wait_ge(modc_ready, l + 2)
                for c in range(2):
                    for v in ((0, 1) if l == 0 else (1,)):
                        o = claim(f"gate{l}{half}{c}{v}")
                        for j in range(4):
                            col = modc[:, l, 24 * half + 16 + 4 * c + j, 1 - v:2 - v]
                            last = mm(o[:, j * P:(j + 1) * P], col.to_broadcast([P, P]), ident)
                        last.then_inc(bank_full, 1)

            def release(key):
                slot_free[load_no[key]] = (bank_full, count[0])

            def release_on_use(key):
                uses[0] += 1
                slot_free[load_no[key]] = (w_used, uses[0])

            def turn_x(stage, src, tiles):
                n = len(tiles)
                per = 4 // n
                for b in range(KC // per):
                    o = claim(f"xT{stage}{b}")
                    for j in range(per):
                        k = b * per + j
                        for t in range(n):
                            last = turn(o[:, (j * n + t) * P:(j * n + t + 1) * P], src[:, tiles[t], k * P:(k + 1) * P])
                    last.then_inc(bank_full, 1)

            def wait_h(stage):
                for b in range(8 if stage in ("mix0", "mlp0", "mix1") else 4):
                    pe.wait_ge(*moved(f"xT{stage}{b}"))

            def features(name, w, f, lo, hi, chunk=None):
                sums = open_sums(chunk)
                o = claim(name)
                for k in range(KC):
                    take_sum(sums, k)
                    last = mm(o[:, 0:hi - lo], w[:, k, f * P:(f + 1) * P], hT[:, k, lo:hi], k == 0, k == KC - 1)
                last.then_inc(bank_full, 1)

            def tokens(name, w, t, width=512, at=0, chunk=None):
                sums = open_sums(chunk)
                o = claim(name)
                for k in range(KC):
                    take_sum(sums, k)
                    last = mm(o[:, 0:width], hT[:, k, t * P:(t + 1) * P], w[:, k, at:at + width], k == 0, k == KC - 1)
                last.then_inc(bank_full, 1)

            def out_project(l, y, tiles):
                for n, t in enumerate(tiles):
                    pe.wait_ge(*moved(f"yT{l}{t if l < 2 else n}0"))
                    pe.wait_ge(*moved(f"yT{l}{t if l < 2 else n}1"))
                    for c in range(2):
                        w = weights((f"out{l}", c))
                        o = claim(f"out{l}{c}{t}")
                        for k in range(KC):
                            last = mm(o, y[:, k, n * P:(n + 1) * P], w[:, k, :], k == 0, k == KC - 1)
                        last.then_inc(bank_full, 1)
                        if t == tiles[-1]:
                            release((f"out{l}", c))

            def turn_y(l, src, t, n):
                for b in range(2):
                    o = claim(f"yT{l}{t}{b}")
                    for j in range(4):
                        k = 4 * b + j
                        last = turn(o[:, j * P:(j + 1) * P], src[:, n, k * P:(k + 1) * P])
                    last.then_inc(bank_full, 1)

            def mlp(l, tiles):
                lo = 0
                n = len(tiles) * P
                for c in range(8):
                    w = weights((f"up{l}", c))
                    for f in range(4):
                        features(f"up{l}{4 * c + f}", w, f, lo, lo + n, due(f"up{l}", c, f))
                    release((f"up{l}", c))
                for half in range(2):
                    outs = [claim(f"down{l}{half}{t}") for t in tiles]
                    for g in range(4):
                        w = weights((f"down{l}", 4 * half + g))
                        if half == 0 and g == 0:
                            pe.wait_ge(*moved(f"up{l}31"))
                        for i, t in enumerate(tiles):
                            for c in range(KC):
                                last = mm(outs[i], h1T[:, g * KC + c, i * P:(i + 1) * P], w[:, c, :],
                                          g == 0 and c == 0, g == 3 and c == KC - 1)
                            if g == 3:
                                last.then_inc(bank_full, 1)
                        if g < 3:
                            last.then_inc(w_used, 1)
                            release_on_use((f"down{l}", 4 * half + g))
                    release((f"down{l}", 4 * half + 3))

            pe.wait_ge(consts_in, 16)
            pe.wait_ge(rows_in, ROWS_DMAS * 16)
            o = claim("cols")
            turn(o[:, 0:96], rows1[0:96, :])
            turn(o[:, 96:192], rows2[0:96, :]).then_inc(bank_full, 1)
            pe.wait_ge(csilu_ready, 1)

            mod_rows()
            pe.wait_ge(x_in, 32)
            turn_x("mix0", xres, range(4))
            wait_h("mix0")
            for c in range(7):
                w = weights(("ev_in", c))
                if c in (0, 3):
                    for f in range(4):
                        features(f"qk0{c}{f}", w, f, 0, 512, due("ev_in", c, f))
                elif c < 6:
                    for t in range(NT):
                        tokens(f"vg0{c}{t}", w, t, chunk=due("ev_in", c, t))
                else:
                    sums = open_sums(due("ev_in", c, 0))
                    o = claim("lr0")
                    for k in range(KC):
                        take_sum(sums, k)
                        last = mm(o[0:32, :], w[:, k, 0:32], hT[:, k, :], k == 0, k == KC - 1)
                    last.then_inc(bank_full, 1)
                release(("ev_in", c))
            pe.wait_ge(laret_ready, 1)

            def decays(name, src):
                o = claim(f"cum{name}")
                for dr, (cum, dc) in enumerate((("cum_f", "dec_f"), ("cum_b", "dec_b"))):
                    for hp in range(2):
                        a = src[:, dr * 256 + hp * P:dr * 256 + (hp + 1) * P]
                        last = mm(o[:, (2 * dr + hp) * P:(2 * dr + hp + 1) * P], a, cst(cum))
                last.then_inc(bank_full, 1)
                o = claim(f"dec{name}")
                for dr, (cum, dc) in enumerate((("cum_f", "dec_f"), ("cum_b", "dec_b"))):
                    for hp in range(2):
                        a = src[:, dr * 256 + hp * P:dr * 256 + (hp + 1) * P]
                        last = mm(o[:, (2 * dr + hp) * 3:(2 * dr + hp + 1) * 3], a, cst(dc))
                last.then_inc(bank_full, 1)

            decays("ret", la_ret)
            pe.wait_ge(*moved("lr0"))
            pe.wait_ge(gkw_ready, 1)

            for t in range(NT):
                o = claim(f"z{t}")
                mm(o, lrT[0:33, t * P:(t + 1) * P], gkw[0:33, :]).then_inc(bank_full, 1)

            def gated_decays(t):
                pe.wait_ge(*moved(f"z{t}"))
                decays(t, las[t])

            gated_decays(0)
            for t in range(NT):
                if t + 1 < NT:
                    gated_decays(t + 1)
                pe.wait_ge(kd_ready, t + 1)
                for dr in range(2):
                    o = claim(f"ktok{t}{dr}")
                    for hp in range(4):
                        last = turn(o[:, hp * P:(hp + 1) * P], kd[:, 4 * dr + hp, t * P:(t + 1) * P])
                    last.then_inc(bank_full, 1)
                pe.wait_ge(*moved(f"vg01{t}"))
                pe.wait_ge(*moved(f"vg04{t}"))
                for dr in range(2):
                    pe.wait_ge(*moved(f"ktok{t}{dr}"))
                for dr in range(2):
                    if (dr, t) in ((0, 3), (1, 2)):
                        continue
                    o = claim(f"kv{t}{dr}")
                    for hp in range(4):
                        for j in range(2):
                            last = mm(o[j * HD:(j + 1) * HD, hp * P:(hp + 1) * P],
                                      ktok[:, 4 * dr + hp, j * HD:(j + 1) * HD],
                                      vtok[:, t, (2 * hp + j) * P:(2 * hp + j + 1) * P])
                    last.then_inc(bank_full, 1)
            pe.wait_ge(carried_ready, 6)
            for t in range(NT):
                for half in range(2):
                    for dr in range(2):
                        o = claim(f"sc{t}{half}{dr}")
                        for hp in range(4):
                            h, j = hp, half
                            ks = kd[j * HD:(j + 1) * HD, 4 * dr + hp, t * P:(t + 1) * P]
                            qs = qd[j * HD:(j + 1) * HD, 4 * dr + hp, t * P:(t + 1) * P]
                            last = mm(o[:, h * P:(h + 1) * P], ks, qs)
                        last.then_inc(bank_full, 1)
                for half in range(2):
                    pe.wait_ge(*moved(f"sc{t}{half}1"))
                    o = claim(f"o{t}{half}")
                    for hp in range(4):
                        h, j = hp, half
                        oh = o[:, h * P:(h + 1) * P]
                        seeds = [s for s in (0, 1) if (s, t) != (0, 0) and (s, t) != (1, 1)]
                        mm(oh, amask[:, 4 * half + h, :], vtok[:, t, (2 * hp + j) * P:(2 * hp + j + 1) * P], True, False)
                        for s in seeds:
                            last = mm(oh, qd[j * HD:(j + 1) * HD, 4 * s + hp, t * P:(t + 1) * P],
                                      carried[j * HD:(j + 1) * HD, CARRY[(s, t)], hp * P:(hp + 1) * P],
                                      False, s == seeds[-1])
                    last.then_inc(bank_full, 1)
            for t in range(NT):
                pe.wait_ge(y_ready, 2 * (t + 1))
                turn_y(0, gtok, t, t)
            gate_rows(0, 0)
            out_project(0, yT, range(NT))
            pe.wait_ge(x_ready, 4)
            turn_x("mlp0", xres, range(4))
            gate_rows(0, 1)
            wait_h("mlp0")
            mlp(0, range(4))

            pe.wait_ge(x_ready, 8)
            turn_x("mix1", xres, range(4))
            wait_h("mix1")
            for p in range(2):
                w = weights(("od_qkv", p))
                for b in range(2):
                    o = claim(f"q1{p}{b}")
                    for j in range(2):
                        a = 2 * b + j
                        for k in range(KC):
                            last = mm(o[:, j * T:(j + 1) * T], w[:, k, a * P:(a + 1) * P], hT[:, k, T:2 * T], k == 0, k == KC - 1)
                    last.then_inc(bank_full, 1)
                release(("od_qkv", p))
            w = weights(("od_qkv", 2))
            for p in range(2):
                features(f"k1{p}", w, p, 0, 512)
            for t in range(NT):
                tokens(f"v1{t}", w, t, T, T)
            release(("od_qkv", 2))
            for b in range(5):
                for n in ([f"q1{b // 2}{b % 2}"] if b < 4 else ["k10", "k11"]):
                    pe.wait_ge(*moved(n))
                o = claim(f"rot{b}")
                src = q_raw[:, 2 * b:2 * b + 2, :] if b < 4 else k_raw
                mm(o, cst("perm"), src).then_inc(bank_full, 1)
            pe.wait_ge(roped, 7)
            for t in range(NT):
                pe.wait_ge(*moved(f"v1{t}"))

            def window_logits(i, g):
                for a in range(4):
                    o = claim(f"lg1{i}{g}{a}")
                    j = a % 2
                    keys = kT if j == g % 2 else kTx
                    mm(o, qT[j * HD:(j + 1) * HD, 2 * g + a // 2, i * P:(i + 1) * P],
                       keys[j * HD:(j + 1) * HD, g // 2, :], True, False)
                    far = T + P * (1 - i)
                    mm(o[:, far:far + P], ident, cst(f"win{i}"), False, True).then_inc(bank_full, 1)

            window_logits(0, 0)
            for n in range(8):
                i, g = divmod(n, 4)
                if n < 7:
                    window_logits(*divmod(n + 1, 4))
                for a in range(4):
                    pe.wait_ge(e_ready, 4 * n + a + 1)
                    o = claim(f"eT1{i}{g}{a}")
                    for c in range(4):
                        last = turn(o[:, c * P:(c + 1) * P], e1[:, a, c * P:(c + 1) * P])
                    last.then_inc(bank_full, 1)
                o1 = claim(f"o1{i}{g}")
                for a in range(4):
                    pe.wait_ge(*moved(f"eT1{i}{g}{a}"))
                    for c in range(4):
                        last = mm(o1[:, a * HD:(a + 1) * HD], eT1[:, a, c * P:(c + 1) * P],
                                  v1[:, c, g * HD:(g + 1) * HD], c == 0, c == 3)
                last.then_inc(bank_full, 1)
            for i in range(2):
                pe.wait_ge(*moved(f"o1{i}3"))
                turn_y(1, y1, X0 + i, i)
            gate_rows(1, 0)
            out_project(1, yT1, (2, 3))
            pe.wait_ge(x_ready, 10)
            turn_x("mlp1", xres, (2, 3))
            gate_rows(1, 1)
            wait_h("mlp1")
            mlp(1, (2, 3))

            pe.wait_ge(xn_ready, 2)
            turn_x("mix2", xn, (0, 1))
            wait_h("mix2")

            def third(c):
                w = weights(("w_in", c))
                if c in (0, 1, 7):
                    for b in range(2):
                        o = claim(f"f2{c}{b}")
                        for j in range(2):
                            f = 2 * b + j
                            for k in range(KC):
                                last = mm(o[:, j * T:(j + 1) * T], w[:, k, f * P:(f + 1) * P],
                                          hT[:, k, 0:T], k == 0, k == KC - 1)
                        last.then_inc(bank_full, 1)
                else:
                    for t in range(2):
                        tokens(f"t2{c}{t}", w, t, 512 if c < 8 else 72)
                release(("w_in", c))

            for c in W_IN_FIRST:
                third(c)
            pe.wait_ge(l2_in, L2_DMAS * 16)
            o = claim("rel")
            mm(o[0:8, 0:2 * T - 1], relb[0:NBUCKET, :], hot[0:NBUCKET, :]).then_inc(bank_full, 1)
            o = claim("ikT")
            for t in range(2):
                pe.wait_ge(ik_ready, t + 1)
                last = turn(o[:, t * P:(t + 1) * P], ikd[:, t, :])
            last.then_inc(bank_full, 1)
            pe.wait_ge(*moved("ikT"))
            for b in range(2):
                pe.wait_ge(*moved(f"f27{b}"))

            def index_products(i, pair):
                for b in pair:
                    o = claim(f"ix{i}{b}")
                    j = b % 2
                    for n in range(2):
                        last = mm(o[:, n * T:(n + 1) * T],
                                  iqT[j * HD:(j + 1) * HD, 2 * (b // 2) + n, i * P:(i + 1) * P],
                                  ikT[j * HD:(j + 1) * HD, :])
                    last.then_inc(bank_full, 1)

            def turn_heads():
                for n in range(2):
                    for t in range(2):
                        pe.wait_ge(aqk_ready, 2 * n + t + 1)
                        o = claim(f"aT{n}{t}")
                        for b in range(4):
                            last = turn(o[:, b * P:(b + 1) * P], (aq, ak)[n][:, t, b * P:(b + 1) * P])
                        last.then_inc(bank_full, 1)

            for n in range(len(LEVELS) + 1):
                if n < 4:
                    index_products(n // 2, (0, 1) if n % 2 == 0 else (2, 3))
                    third(W_IN_BESIDE[n])
                elif n == 4:
                    turn_heads()
                if n < len(LEVELS):
                    pe.wait_ge(ql_ready, n + 1)
                    pe.wait_ge(kl_ready, n + 1)
                for t in range(2):
                    o = claim(f"lev{n}{t}")
                    for h in range(4):
                        qs, ks = (qls[n % 2], kls[n % 2]) if n < len(LEVELS) else (rqT, rkT)
                        last = mm(o[:, h * P:(h + 1) * P], ks[:, h, t * P:(t + 1) * P], qs[:, h, t * P:(t + 1) * P])
                    last.then_inc(bank_full, 1)
            pe.wait_ge(ql_ready, len(LEVELS) + 1)
            pe.wait_ge(kl_ready, len(LEVELS) + 1)
            o = claim("across")
            for h in range(4):
                last = mm(o[:, h * P:(h + 1) * P], kls[len(LEVELS) % 2][:, h, 0:P], qls[len(LEVELS) % 2][:, h, P:T])
            last.then_inc(bank_full, 1)
            pe.wait_ge(*moved("across"))
            for t in range(2):
                pe.wait_ge(*moved(f"t22{t}"))
                pe.wait_ge(*moved(f"t26{t}"))
                pe.wait_ge(*moved(f"aT0{t}"))
                pe.wait_ge(*moved(f"aT1{t}"))
            for t in range(2):
                o = claim(f"ro{t}")
                for h in range(4):
                    oh = o[:, h * P:(h + 1) * P]
                    last = mm(oh, amat[:, t, h, :], rv[:, t, h * P:(h + 1) * P], True, t == 0)
                    if t == 1:
                        last = mm(oh, across[:, h, :], rv[:, 0, h * P:(h + 1) * P], False, True)
                last.then_inc(bank_full, 1)
            for i in range(2):
                for b in range(4):
                    o = claim(f"lg2{i}{b}")
                    j = b % 2
                    for n in range(2):
                        blk = 2 * (b // 2) + n
                        last = mm(o[:, n * T:(n + 1) * T], aqT[j * HD:(j + 1) * HD, blk, i * P:(i + 1) * P],
                                  akT[j * HD:(j + 1) * HD, blk, :])
                    last.then_inc(bank_full, 1)
            for i in range(2):
                pe.wait_ge(e2_ready, 8 * (i + 1))
                for b in range(4):
                    o = claim(f"eT2{i}{b}")
                    for j in range(2):
                        for c in range(2):
                            last = turn(o[:, (2 * j + c) * P:(2 * j + c + 1) * P], logits[i][:, 2 * b + j, c * P:(c + 1) * P])
                    last.then_inc(bank_full, 1)
                o = claim(f"att{i}")
                for b in range(4):
                    pe.wait_ge(*moved(f"eT2{i}{b}"))
                    for j in range(2):
                        h = 2 * b + j
                        for c in range(2):
                            last = mm(o[:, h * HD:(h + 1) * HD], eT2[:, b % 4, (2 * j + c) * P:(2 * j + c + 1) * P],
                                      av[:, c, h * HD:(h + 1) * HD], c == 0, c == 1)
                last.then_inc(bank_full, 1)
            for i in range(2):
                pe.wait_ge(mix_ready, 2 + i + 1)
                turn_y(2, mix, i, i)
            gate_rows(2, 0)
            out_project(2, yT2, (2, 3))
            pe.wait_ge(xn_ready, 4)
            turn_x("moe", xn, (0, 1))
            gate_rows(2, 1)
            wait_h("moe")
            o = claim("router")
            for t in range(2):
                for k in range(KC):
                    last = mm(o[:, t * 20:(t + 1) * 20], hT[:, k, t * P:(t + 1) * P], wr[:, k, :], k == 0, k == KC - 1)
            last.then_inc(bank_full, 1)
            base = count[0]
            bank_no["moe"] = base

            def expert(turn_no, j):
                def turn_claim(local):
                    pe.wait_ge(bank_freed[(base + local) % BANKS], turn_no * BODY + (base + local) // BANKS)
                    return psum[:, (base + local) % BANKS, :]

                def slot(piece):
                    i = MOE_LOAD0 + 3 * j + piece
                    pe.wait_ge(w_landed[i % RING], turn_no * (16 * LOADS_PER_TURN // RING) + 16 * (i // RING + 1))
                    return wring[:, i % RING, :, :]

                w1, w3 = slot(0), slot(1)
                for f in range(4):
                    o = turn_claim(8 * j + f)
                    for n, w in enumerate((w1, w3)):
                        for k in range(KC):
                            last = mm(o[:, n * T:(n + 1) * T], w[:, k, f * P:(f + 1) * P], hT[:, k, 0:T],
                                      k == 0, k == KC - 1)
                    last.then_inc(bank_full, 1)
                w2 = slot(2).rearrange("p (f a) n -> p f (a n)", a=2)
                for n in range(2):
                    for t in range(2):
                        o = turn_claim(8 * j + 4 + 2 * n + t)
                        for f in range(4):
                            if n == 0 and t == 0:
                                at = base + 8 * j + f
                                pe.wait_ge(bank_freed[at % BANKS], turn_no * BODY + (at // BANKS + 1))
                            last = mm(o, he[:, j % 2, f, t * P:(t + 1) * P], w2[:, f, n * 512:(n + 1) * 512],
                                      f == 0, f == 3)
                        last.then_inc(bank_full, 1)

            with pe.Fori(0, TURNS) as turn_no:
                for j in range(BODY):
                    expert(turn_no, j)

        def rows_of(vecs):
            return vecs.rearrange("a (k p) -> (a k) p", p=P)

        @block.sync
        def _(sp):
            sp.dma_start(const[:, :], I["const_main"]).then_inc(consts_in, 16)
            for rows, at, src in ((rows1, 40, I["b_mod"][0:1]), (rows1, 88, I["lb_logits_2"]),
                                  (rows2, 0, I["b_mod"][1:2]), (rows2, 48, I["b_ada_2"][0:1])):
                n = src.shape[0] * src.shape[1] // P
                sp.dma_start(rows[at:at + n, :], rows_of(src)).then_inc(rows_in, 16)

            def source(key):
                name, c = key
                l = int(name[-1]) if name[-1].isdigit() else 0
                if name.startswith("mod"):
                    m = I["w_mod"][l] if l < 2 else I["w_ada_2"][0]
                    return m[:, c * 512:(c + 1) * 512]
                if name.startswith("out"):
                    m = (I["ev_w_out"], I["od_w_out"], I["w_out_2"])[l][0]
                    return m[:, c * 512:(c + 1) * 512]
                if name.startswith("up"):
                    return I["mlp_w1"][l][:, c * 512:(c + 1) * 512]
                if name.startswith("down"):
                    half, g = c // 4, c % 4
                    return I["mlp_w2"][l][g * D:(g + 1) * D, half * 512:(half + 1) * 512]
                m = {"ev_in": I["ev_w_in"], "od_qkv": I["od_w_qkv"], "w_in": I["w_in_2"]}[name][0]
                return m[:, c * 512:min((c + 1) * 512, m.shape[1])]

            for i, key in enumerate(STREAM):
                if i >= RING:
                    sp.wait_ge(*slot_free[i - RING])
                src = source(key)
                sp.dma_start(wring[:, i % RING, :, 0:src.shape[1]],
                             src.rearrange("(k p) n -> p k n", p=P)).then_inc(w_landed[i % RING], 16)
            base = bank_no["moe"]

            def expert_slot(e, piece):
                if piece < 2:
                    return (I["w1_2"], I["w3_2"])[piece][0, bass.ds(e, 1)].rearrange("a (k p) n -> p (a k) n", p=P)
                return I["w2_2"][0, bass.ds(e, 1)].rearrange("a (f p) n -> p (a f) n", p=P)

            def load_expert(e, piece, local):
                i = MOE_LOAD0 + local
                dst = wring[:, i % RING, :, :]
                if piece == 2:
                    dst = dst.rearrange("p (f a) n -> p f (a n)", a=2)
                sp.dma_start(dst, expert_slot(e, piece)).then_inc(w_landed[i % RING], 16)

            def freed_by(turn_no, q):
                return turn_no * MOE_BANKS + (base + 8 * (q // 3) + (4 if q % 3 < 2 else 8))

            for m in range(RING):
                sp.wait_ge(*slot_free[MOE_LOAD0 + m - RING])
                load_expert(m // 3, m % 3, m)
            with sp.Fori(0, TURNS - 1) as turn_no:
                for q in range(LOADS_PER_TURN):
                    m = q + RING
                    sp.wait_ge(bank_full, freed_by(turn_no, q))
                    load_expert(turn_no * BODY + m // 3, m % 3, m)
            for q in range(LOADS_PER_TURN - RING):
                m = q + RING
                sp.wait_ge(bank_full, freed_by(TURNS - 1, q))
                load_expert((TURNS - 1) * BODY + m // 3, m % 3, m)

        @block.gpsimd
        def _(pool):
            steps = [0]

            def step(ins):
                steps[0] += 1
                ins.then_inc(pool_step, 1)
                pool.wait_ge(pool_step, steps[0])

            step(nc.gpsimd.memset(gkw[0:33, :], 0.0))
            nc.gpsimd.memset(lrT[32:33, :], 1.0).then_inc(gkw_ready, 1)
            pool.dma_start(gkw[0:16, 0:256], I["ev_gla_gk_w"][0, 0]).then_inc(mix0_in, 16)
            pool.dma_start(gkw[16:32, 256:512], I["ev_gla_gk_w"][0, 1]).then_inc(mix0_in, 16)
            pool.dma_start(gkw[32:33, :], I["ev_gla_gk_b"].rearrange("a b c -> a (b c)")).then_inc(mix0_in, 16)
            pool.dma_start(normg, I["ev_gla_norm_g"].to_broadcast([P, P])).then_inc(mix0_in, 16)
            pool.dma_start(theta, I["ev_ret_theta"].rearrange("a b c -> a (b c)").to_broadcast([P, 8])).then_inc(mix0_in, 16)
            pool.dma_start(sinkb, I["od_sink"].to_broadcast([P, 16])).then_inc(sink_in, 16)
            pool.wait_ge(gkw_ready, 1)
            step(nc.gpsimd.memset(half_neg, -0.5))
            roots = [0]

            def inverse_roots(aps):
                for a in aps:
                    roots[0] += 1
                    pool.wait_ge(rate_ready, roots[0])
                    nc.gpsimd.tensor_tensor(a, a, half_neg[:, 0:a.shape[1]], ALU.pow).then_inc(rate_done, 1)

            def norm_vectors(n, s, v):
                pool.wait_ge(s, v)
                l, j = n // 2, n % 2
                pool.dma_start(lnb[:, 0, :], I["ln_g"][l, j:j + 1, :].to_broadcast([P, D])).then_inc(ln_in, 16)
                pool.dma_start(lnb[:, 1, :], I["ln_b"][l, j:j + 1, :].to_broadcast([P, D])).then_inc(ln_in, 16)

            norm_vectors(0, carried_ready, 6)
            inverse_roots([hsum] * 4)
            inverse_roots([lnr] * 4)
            norm_vectors(1, x_ready, 4)
            inverse_roots([lnr] * 4)
            norm_vectors(2, x_ready, 8)
            pool.dma_start(rope.rearrange("p a b -> p (a b)"), I["const_rope"]).then_inc(rope_in, 16)
            inverse_roots([lnr] * 2)
            norm_vectors(3, x_ready, 10)
            inverse_roots([lnr] * 2)
            inverse_roots([lnr] * 2)
            pool.wait_ge(x_ready, 12)
            for dst, src in (
                (relb[0:NBUCKET, :], I["rel_bias_2"]), (hot[0:NBUCKET, :], I["const_buckets"]),
                (qkg[:, 0:HD], I["q_norm_g_2"].to_broadcast([P, HD])), (qkg[:, HD:P], I["k_norm_g_2"].to_broadcast([P, HD])),
                (ikn[:, 0:HD], I["idx_k_norm_g_2"].to_broadcast([P, HD])), (ikn[:, HD:P], I["idx_k_norm_b_2"].to_broadcast([P, HD])),
                (wr[:, :, 0:4], I["w_rg_2"][0].rearrange("(k p) n -> p k n", p=P)),
                (wr[:, :, 4:20], I["w_re_2"][0].rearrange("(k p) n -> p k n", p=P)),
                (brr[:, 0:4], I["b_rg_2"].to_broadcast([P, 4])), (brr[:, 4:20], I["b_re_2"].to_broadcast([P, NEXP])),
            ):
                pool.dma_start(dst, src).then_inc(l2_in, 16)
            for b in range(4):
                pool.wait_ge(*moved(f"xTmix2{b}"))
            pool.dma_start(levels, I["const_levels"]).then_inc(lev_in, 16)
            nc.gpsimd.memset(amat, 0.0).then_inc(amat_zero, 1)
            pool.wait_ge(amat_zero, 1)
            inverse_roots([lnr] * 2)
            pool.wait_ge(*moved("rel"))
            pool.dma_start(rel_scratch, relE[0:8, 0:2 * T - 1]).then_inc(rel_out, 16)
            pool.wait_ge(kln_ready, 1)
            for n in range(len(LEVELS) + 1):
                pool.wait_ge(edec_ready, n + 1)
                if n > 1:
                    pool.wait_ge(bank_full, full(f"lev{n - 2}1"))
                nc.gpsimd.tensor_tensor(kls[n % 2], rkT, edecs[n % 2], ALU.mult).then_inc(kl_ready, 1)
                if n < 2:
                    pool.wait_ge(kl_ready, n + 1)
                    inverse_roots([st8] * 2)
            pool.wait_ge(bank_full, full("t261"))
            pool.dma_start(rowg[:, 0, :], I["rec_out_g_2"].to_broadcast([P, 512])).then_inc(rowg_in, 16)
            pool.dma_start(rowg[:, 1, :], I["attn_out_g_2"].to_broadcast([P, 512])).then_inc(rowg_in, 16)
            pool.wait_ge(rel_out, 16)

            def bias_tile(i):
                pool.dma_start(biasT, bass.AP(tensor=rel_scratch.tensor, offset=i * P,
                                              ap=[[1, P], [2 * T - 1, 8], [1, T]])).then_inc(rel_in, 16)

            pool.wait_ge(*moved("across"))
            bias_tile(0)
            inverse_roots([st8[:, 0:4]])
            pool.wait_ge(bias_used, 1)
            bias_tile(1)
            inverse_roots([st8[:, 0:4]])
            inverse_roots([st8] * 2)
            inverse_roots([lnr] * 2)

        @block.scalar
        def _(act):
            steps = [0]

            def step(ins):
                steps[0] += 1
                ins.then_inc(act_step, 1)
                act.wait_ge(act_step, steps[0])

            counts = {}

            def signal(ins, s):
                counts[s.name] = counts.get(s.name, 0) + 1
                ins.then_inc(s, 1)
                act.wait_ge(s, counts[s.name])

            def free(ins, name):
                ins.then_inc(freed(name), 1)
                act.wait_ge(*moved(name))

            def f(o, a, func, **kw):
                return nc.scalar.activation(o, a, func, **kw)

            for at, src in ((0, I["c"]), (8, I["c_ctx"].rearrange("(a d) -> a d", a=1)), (16, I["c_2"]),
                            (24, I["norm1_g_2"]), (32, I["norm2_g_2"])):
                act.dma_start(rows1[at:at + KC, :], rows_of(src)).then_inc(rows_in, 16)

            act.wait_ge(bank_full, full("cols"))
            free(f(cols[:, :], bank("cols")[:, 0:192], ACT.Copy), "cols")
            act.wait_ge(*moved("cols"))
            signal(f(csilu[:, :], cols[:, 0:24], ACT.Silu), csilu_ready)
            act.dma_start(xres[:, 0:2, :], I["ctx"][0].rearrange("(t p) d -> p t d", p=P)).then_inc(x_in, 16)
            act.dma_start(xres[:, 2:4, :], I["x"][0].rearrange("(t p) d -> p t d", p=P)).then_inc(x_in, 16)
            act.wait_ge(mix0_in, 80)
            step(f(theta, theta, ACT.Exp))
            signal(f(theta, theta, ACT.Ln, scale=-1.0, bias=1.0), theta_exp)

            def modulate(stage):
                s = stages.index(stage)
                l, half = s // 2, s % 2
                act.wait_ge(modc_ready, MODC_DONE[stage])
                wide = s < 3
                for b in range(0, 8 if wide else 4, 2):
                    n = f"xT{stage}{b}"
                    act.wait_ge(bank_full, full(n))
                    for j in range(2):
                        k, v, at = (b, 1 - j, j * T) if wide else (2 * b + j, 0, 0)
                        last = f(hT[:, k, at:at + T], bank(n)[:, j * T:(j + 1) * T], ACT.Identity,
                                 bias=modc[:, l, 24 * half + k, v:v + 1], scale=modc[:, l, 24 * half + 8 + k, v:v + 1])
                    free(last, n)

            def move(name, dst, src=None, func=ACT.Copy, **kw):
                act.wait_ge(bank_full, full(name))
                free(f(dst, bank(name) if src is None else src, func, **kw), name)

            def turned(l, t, n):
                dst = (yT, yT1, yT2)[l]
                for b in range(2):
                    name = f"yT{l}{t}{b}"
                    act.wait_ge(bank_full, full(name))
                    move(name, dst[:, 4 * b:4 * b + 4, n * P:(n + 1) * P], bank(name).rearrange("p (b n) -> p b n", b=4))

            def mods(chunk):
                if chunk is not None:
                    l, m = chunk
                    V = vectors(l)
                    move(f"mod{l}_{m}", modc[:, l, 4 * m:4 * m + 4, 0:V],
                         bank(f"mod{l}_{m}")[:, 0:4 * V].rearrange("p (f v) -> p f v", v=V))

            def gates(l, half):
                for c in range(2):
                    for v in ((0, 1) if l == 0 else (1,)):
                        move(f"gate{l}{half}{c}{v}", gate[:, v, c * 512:(c + 1) * 512])

            def relus(l, n):
                for i in range(32):
                    mods(due(f"up{l}", i // 4, i % 4))
                    act.wait_ge(bank_full, full(f"up{l}{i}"))
                    signal(f(h1T[:, i, 0:n], bank(f"up{l}{i}")[:, 0:n], ACT.Relu), relu_ready)

            for c in range(4):
                move(f"modrow{c}", modrow[0:2, c, :], bank(f"modrow{c}")[0:2, :])
            modulate("mix0")
            for c in range(7):
                for i in range(4):
                    mods(due("ev_in", c, i))
                    if c in (0, 3):
                        blk = (0 if c == 0 else 2) + (i if i < 2 else i + 2)
                        scaled = (i >= 2) if c == 0 else (i < 2)
                        move(f"qk0{c}{i}", qkT[:, blk, :], func=ACT.Copy, scale=HD ** -0.5 if scaled else 1.0)
                    elif c in (2, 5):
                        move(f"vg0{c}{i}", gtok[:, i, (c // 3) * 512:(c // 3 + 1) * 512], func=ACT.Silu)

            def decays(name, dst, kind):
                act.wait_ge(bank_full, full(f"cum{name}"))
                src = bank(f"cum{name}").rearrange("p (a n) -> p a n", a=4)
                f(dst[:, 0], src, ACT.Exp)
                free(f(dst[:, 1], src, ACT.Exp, scale=-1.0), f"cum{name}")
                act.wait_ge(bank_full, full(f"dec{name}"))
                src = bank(f"dec{name}")[:, 0:12].rearrange("p (d h c) -> p d h c", d=2, h=2)
                for t in (range(NT) if name == "ret" else (name,)):
                    last = f(dec[:, t, :, 2 * kind:2 * kind + 2, :], src, ACT.Exp)
                free(last, f"dec{name}")

            decays("ret", exp_ret, 0)
            for t in range(NT):
                act.wait_ge(bank_full, full(f"z{t}"))
                step(f(las[t], bank(f"z{t}"), ACT.Abs))
            for t in range(NT):
                step(f(las[t], las[t], ACT.Exp, scale=-1.0))
            for t in range(NT):
                signal(f(las[t], las[t], ACT.Ln, bias=1.0), zlog_ready)

            def gated_decays(t):
                if t > 0:
                    act.wait_ge(kd_ready, t)
                decays(t, exp_gla, 1)

            gated_decays(0)
            for t in range(NT):
                if t + 1 < NT:
                    gated_decays(t + 1)
                for dr in range(2):
                    name = f"ktok{t}{dr}"
                    if t > 0:
                        act.wait_ge(bank_full, full(f"kv{t - 1}{0 if t == 3 else 1}"))
                    move(name, ktok[:, 4 * dr:4 * dr + 4, :], bank_of(name, 4))
            def forward_scores(t):
                for half in range(2):
                    if t > 0:
                        act.wait_ge(bank_full, full(f"o{t - 1}{half}"))
                    move(f"sc{t}{half}0", amask[:, 4 * half:4 * half + 4, :], bank_of(f"sc{t}{half}0", 4))

            forward_scores(0)
            for t in range(NT):
                if t + 1 < NT:
                    forward_scores(t + 1)
                for half in range(2):
                    if t > 0:
                        act.wait_ge(y_ready, 2 * (t - 1) + half + 1)
                    act.wait_ge(bank_full, full(f"o{t}{half}"))
                    signal(f((sqb, la)[half], bank(f"o{t}{half}"), ACT.Square), sq_ready)
            for t in range(NT):
                turned(0, t, t)
            gates(0, 0)
            modulate("mlp0")
            gates(0, 1)
            relus(0, 512)

            modulate("mix1")
            for p in range(2):
                for b in range(2):
                    move(f"q1{p}{b}", q_raw[:, 4 * p + 2 * b:4 * p + 2 * b + 2, :], bank_of(f"q1{p}{b}", 2))
            for p in range(2):
                act.wait_ge(bank_full, full(f"k1{p}"))
                f(kT[:, p, 0:T], bank(f"k1{p}")[:, 0:T], ACT.Copy)
                move(f"k1{p}", k_raw[:, p, :], bank(f"k1{p}")[:, T:2 * T])
            for i in range(2):
                for g in range(4):
                    n = 4 * i + g
                    act.wait_ge(negm_ready, n + 1)
                    if n > 0:
                        act.wait_ge(bank_full, full(f"eT1{(n - 1) // 4}{(n - 1) % 4}3"))
                    for a in range(4):
                        name = f"lg1{i}{g}{a}"
                        act.wait_ge(bank_full, full(name))
                        signal(f(e1[:, a, :], bank(name), ACT.Exp, scale=HD ** -0.5, bias=negm1[:, n % 2, a:a + 1],
                          accum_out=den1[:, 4 * n + a:4 * n + a + 1]), e_ready)
                        act.wait_ge(e_ready, 4 * n + a + 1)
                        act.sem_inc(freed(name), 1)
                    signal(f(sexp1[:, n % 2, :], sexp1[:, n % 2, :], ACT.Exp), sexp_ready)
                    if n > 0:
                        act.wait_ge(bank_full, full(f"o1{(n - 1) // 4}{(n - 1) % 4}"))
                    for a in (0, 2):
                        move(f"eT1{i}{g}{a}", eT1[:, a, :])
            for i in range(2):
                turned(1, X0 + i, i)
            gates(1, 0)
            modulate("mlp1")
            gates(1, 1)
            relus(1, 256)

            act.wait_ge(lbd_ready, 1)
            signal(f(lbc, lbc, ACT.Sigmoid), lbs_ready)
            modulate("mix2")
            for b in range(2):
                move(f"f20{b}", rqT[:, 2 * b:2 * b + 2, :], bank_of(f"f20{b}", 2), ACT.Silu)
            for t in range(2):
                move(f"t23{t}", rg[:, t, :], func=ACT.Silu)
            for b in range(2):
                move(f"f21{b}", rsig[:, 2 * b:2 * b + 2, :], bank_of(f"f21{b}", 2), ACT.Sigmoid)
            act.wait_ge(rfs_ready, 1)
            signal(f(rsig, rsig, ACT.Ln), lf_ready)
            for b in range(2):
                move(f"f27{b}", iqT[:, 2 * b:2 * b + 2, :], bank_of(f"f27{b}", 2))
            move("ikT", ikT, bank("ikT")[:, 0:T])
            for n in range(len(LEVELS) + 1):
                act.wait_ge(diff_ready, n + 1)
                signal(f(edecs[n % 2], edecs[n % 2], ACT.Exp), edec_ready)
                for m in ((2 * n, 2 * n + 1) if n < 4 else ()):
                    act.wait_ge(sc_ready, m + 1)
                    move(f"ix{m // 4}{m % 4}", sc_r[:, :, :], bank_of(f"ix{m // 4}{m % 4}", 2), ACT.Relu, scale=HD ** -0.5)
                for m in (range(4) if n == 4 else ()):
                    name = f"aT{m // 2}{m % 2}"
                    move(name, (aqT, akT)[m // 2][:, :, (m % 2) * P:(m % 2 + 1) * P], bank_of(name, 4))
            for i in range(2):
                act.wait_ge(neg2_ready, i + 1)
                for h in range(8):
                    signal(f(logits[i][:, h, :], logits[i][:, h, :], ACT.Exp, bias=neg2[:, i, h:h + 1],
                      accum_out=den2[:, i, h:h + 1]), e2_ready)
                if i == 1:
                    act.wait_ge(bank_full, full("att0"))
                for b in range(4):
                    move(f"eT2{i}{b}", eT2[:, b, :])
            for i in range(2):
                turned(2, i, i)
            gates(2, 0)
            modulate("moe")
            gates(2, 1)
            act.wait_ge(route_ready, 1)
            signal(f(rt_exp, rt_exp, ACT.Exp), route_exp)
            base = bank_no["moe"]
            with act.Fori(0, TURNS) as turn_no:
                for j in range(BODY):
                    for u in range(4):
                        local = 8 * j + u
                        act.wait_ge(bank_full, turn_no * MOE_BANKS + (base + local + 1))
                        prev = base + local - 16
                        act.wait_ge(bank_freed[prev % BANKS], turn_no * BODY + (prev // BANKS + 1))
                        f(sg[:, j % 2, u, :], psum[:, (base + local) % BANKS, 0:T], ACT.Silu).then_inc(sg_ready, 1)
            for t in range(2):
                act.wait_ge(final_ready, t + 1)
                act.dma_start(out[0, t * P:(t + 1) * P, :], xres[:, X0 + t, :]).then_inc(out_done, 16)
            act.wait_ge(out_done, 32)

        @block.vector
        def _(dve):
            steps = [0]
            v_ = nc.vector

            def step(ins):
                steps[0] += 1
                ins.then_inc(dve_step, 1)
                dve.wait_ge(dve_step, steps[0])

            counts = {}

            def signal(ins, s):
                counts[s.name] = counts.get(s.name, 0) + 1
                ins.then_inc(s, 1)
                dve.wait_ge(s, counts[s.name])

            def free(ins, name):
                ins.then_inc(freed(name), 1)
                dve.wait_ge(*moved(name))

            def root(ins, rate):
                ins.then_inc(rate_ready, 1)
                rates.append(rate)
                dve.wait_ge(rate_done, len(rates))

            def ready(name):
                dve.wait_ge(bank_full, full(name))
                return bank(name)

            def move(name, dst, src=None):
                ready(name)
                free(v_.tensor_copy(dst, bank(name) if src is None else src), name)

            def mods(l, c0, c1):
                V = 2 if l < 2 else 1
                for c in range(c0, c1):
                    o = ready(f"mod{l}_{c}")[:, 0:4 * V].rearrange("p (f v) -> p f v", v=V)
                    free(v_.tensor_copy(modc[:, l, 4 * c:4 * c + 4, 0:V], o), f"mod{l}_{c}")

            def sum_mods(name, c, j):
                for l, m in BESIDE[name][c][j:j + 1]:
                    V = vectors(l)
                    n = SUMMED.index((l, m))
                    i = load_no[(f"mod{l}", m)]
                    dve.wait_ge(w_landed[i % RING], 16 * (i // RING + 1))
                    if n >= 2:
                        dve.wait_ge(bank_full, full("mod%d_%d" % SUMMED[n - 2]))
                    for k in range(KC):
                        for v in range(V):
                            acc, w = modsum[:, n % 2, v, :], wring[:, i % RING, k, :]
                            at = (8 * v if l < 2 else 16) + k
                            by = csilu[:, at:at + 1]
                            if k == 0:
                                ins = v_.tensor_scalar(acc, w, by, None, ALU.mult)
                            else:
                                dve.wait_ge(dve_step, steps[0] - (V - 1))
                                ins = v_.scalar_tensor_tensor(acc, w, by, acc, ALU.mult, ALU.add)
                            if k < KC - 1:
                                steps[0] += 1
                                ins.then_inc(dve_step, 1)
                            else:
                                ins.then_inc(mod_summed, 1)
                                if v == 0 and V == 2:
                                    dve.wait_ge(dve_step, steps[0])

            def finish_mod(l, c0, c1):
                V = 2 if l < 2 else 1
                for c in range(c0, c1):
                    dve.wait_ge(*moved(f"mod{l}_{c}"))
                at = (40, 96, 144)[l]
                raw = modc[:, l, 4 * c0:4 * c1, 0:V]
                ins = v_.tensor_tensor(raw, raw, cols[:, at + 4 * c0:at + 4 * c1].unsqueeze(2)
                                       .to_broadcast([P, 4 * (c1 - c0), V]), ALU.add)
                for half in ((0,) if c1 == 4 else (1,) if c0 == 4 else (0, 1)):
                    step(ins)
                    scales = modc[:, l, 24 * half + 8:24 * half + 16, 0:V]
                    ins = v_.tensor_scalar(scales, scales, 1.0, None, ALU.add)
                    if l == 2:
                        step(ins)
                        gain = cols[:, 24 + 8 * half:32 + 8 * half].unsqueeze(2)
                        ins = v_.tensor_tensor(scales, scales, gain, ALU.mult)
                signal(ins, modc_ready)

            def modulate(stage):
                s = stages.index(stage)
                l, half = s // 2, s % 2
                wide = s < 3
                for b in range(1, 8 if wide else 4, 2):
                    n = f"xT{stage}{b}"
                    ready(n)
                    for j in range(2):
                        k, v, at = (b, 1 - j, j * T) if wide else (2 * b + j, 0, 0)
                        last = v_.tensor_scalar(hT[:, k, at:at + T], bank(n)[:, j * T:(j + 1) * T],
                                                modc[:, l, 24 * half + 8 + k, v:v + 1],
                                                modc[:, l, 24 * half + k, v:v + 1], ALU.mult, ALU.add)
                    free(last, n)

            def residual(l, prefix, half_no, tiles, alpha=ALPHA):
                cs = slice(half_no * 512, (half_no + 1) * 512)
                for t in tiles:
                    name = f"{prefix}{half_no}{t}"
                    ready(name)
                    gv = 0 if t < X0 else 1
                    for v in ((0, 1) if l == 0 else (1,)):
                        dve.wait_ge(*moved(f"gate{l}{0 if prefix.startswith('out') else 1}{half_no}{v}"))
                    free(v_.tensor_tensor(ubuf, bank(name), gate[:, gv, cs], ALU.mult), name)
                    dve.wait_ge(*moved(name))
                    step(v_.scalar_tensor_tensor(xres[:, t, cs], xres[:, t, cs], alpha, ubuf, ALU.mult, ALU.add))

            def residual_norm(l, prefix, t):
                for half in ((0, 1) if prefix == "out" else (1,)):
                    residual(l, f"{prefix}{l}", half, (t,))
                layer_norm(2 * l + (prefix == "down"), (t,))

            def layer_norm(n, tiles):
                dve.wait_ge(ln_in, 32 * (n + 1))
                for t in tiles:
                    x = xres[:, t, :]
                    for c in range(2):
                        step(v_.bn_stats(lnstat[:, c, :], x[:, c * 512:(c + 1) * 512]))
                    step(v_.bn_aggr(lnagg, lnstat.rearrange("p a b -> p (a b)")))
                    v_.tensor_scalar(lnr, lnagg[:, 1:2], LN_EPS, None, ALU.add).then_inc(rate_ready, 1)
                    rates.append(lnr)
                    step(v_.scalar_tensor_tensor(x, x, lnagg[:, 0:1], lnb[:, 0, :], ALU.subtract, ALU.mult))
                    dve.wait_ge(rate_done, len(rates))
                    signal(v_.scalar_tensor_tensor(x, x, lnr, lnb[:, 1, :], ALU.mult, ALU.add), x_ready)
                    tiles_done[0] += 1
                    dve.wait_ge(x_ready, tiles_done[0])

            tiles_done = [0]

            def head_rate(src, heads, out_rate, scratch, width, eps=RMS_EPS):
                step(v_.tensor_tensor(scratch, src, src, ALU.mult))
                step(v_.tensor_reduce(out_rate, scratch.rearrange("p (h d) -> p h d", h=heads), AX.X, ALU.add))
                root(v_.tensor_scalar(out_rate, out_rate, 1.0 / width, eps, ALU.mult, ALU.add), out_rate)

            def rms_row(t):
                x = xres[:, X0 + t, :]
                step(v_.tensor_tensor_reduce(out=xn[:, t, :], in0=x, in1=x, scale=1.0, scalar=0.0, op0=ALU.mult,
                                             op1=ALU.add, accum_out=lnr))
                root(v_.tensor_scalar(lnr, lnr, 1.0 / D, RMS_EPS, ALU.mult, ALU.add), lnr)
                signal(v_.tensor_scalar(xn[:, t, :], x, lnr, None, ALU.mult), xn_ready)

            def mlp(l, tiles):
                n = len(tiles) * P
                for i in range(32):
                    name = f"up{l}{i}"
                    dve.wait_ge(relu_ready, 32 * l + i + 1)
                    h = h1T[:, i, 0:n]
                    free(v_.tensor_tensor(h, h, bank(name)[:, 0:n], ALU.mult), name)
                    if i % 2 == 1:
                        sum_mods(f"up{l}", i // 4, i % 4 // 2)
                finish_mod(l + 1, 0, 12)
                residual(l, f"down{l}", 0, tiles)
                for t in tiles:
                    residual_norm(l, "down", t)
                    if l == 1:
                        rms_row(t - X0)

            mods(0, 0, 4)
            finish_mod(0, 0, 4)
            modulate("mix0")
            dve.wait_ge(theta_exp, 1)
            for dr in range(2):
                last = v_.tensor_scalar(la_ret[:, dr * 256:(dr + 1) * 256].rearrange("p (h d) -> p h d", h=4),
                                        theta[:, 4 * dr:4 * dr + 4].unsqueeze(2).to_broadcast([P, 4, HD]),
                                        16.0, None, ALU.mult)
            signal(last, laret_ready)
            for c in range(6):
                for t in range(NT):
                    if c in (1, 4):
                        move(f"vg0{c}{t}", vtok[:, t, (c // 3) * 512:(c // 3 + 1) * 512])
                    if t % 2 == 1:
                        sum_mods("ev_in", c, t // 2)
            dve.wait_ge(mix0_in, 80)
            free(v_.tensor_copy(lrT[0:32, :], ready("lr0")[0:32, :]), "lr0")
            heads = lambda a: a.rearrange("p (h n) -> p h n", h=4)

            def decay_of(t, dr, which):
                return dec[:, t, dr, :, which:which + 1].to_broadcast([P, 4, P])

            def enter(dr, t):
                signal(v_.tensor_tensor(heads(carried[:, CARRY[(dr, t)], :]), heads(carried[:, roll[dr], :]),
                                 decay_of(t, dr, 0), ALU.mult), carried_ready)
                carried_no[0] += 1
                dve.wait_ge(carried_ready, carried_no[0])

            def added(dr, t, slot):
                name = f"kv{t}{dr}"
                dst = carried[:, slot, :] if slot is not None else passing
                free(v_.tensor_tensor(heads(dst), heads(ready(name)), decay_of(t, dr, 1), ALU.mult), name)
                dve.wait_ge(*moved(name))
                return dst

            def pass_tile(dr, t, add):
                r = carried[:, roll[dr], :]
                step(v_.tensor_tensor(heads(r), heads(r), decay_of(t, dr, 2), ALU.mult))
                step(v_.tensor_tensor(r, r, add, ALU.add))

            def states(t):
                dve.wait_ge(*moved(f"dec{t}"))
                held = CARRY[(1, 3)]
                if t == 0:
                    added(0, 0, roll[0])
                    added(1, 0, held)
                elif t == 1:
                    enter(0, 1)
                    pass_tile(0, 1, added(0, 1, None))
                    added(1, 1, roll[1])
                    enter(1, 0)
                    pass_tile(1, 0, carried[:, held, :])
                elif t == 2:
                    enter(0, 2)
                    pass_tile(0, 2, added(0, 2, None))
                else:
                    enter(1, 3)
                    pass_tile(1, 3, added(1, 3, None))
                    enter(0, 3)
                    enter(1, 2)

            carried_no = [0]

            def log_gates(t):
                z = ready(f"z{t}")
                dve.wait_ge(zlog_ready, t + 1)
                free(v_.scalar_tensor_tensor(las[t], z, 0.0, las[t], ALU.min, ALU.subtract), f"z{t}")

            for t in range(NT):
                log_gates(t)
            dve.wait_ge(*moved("cumret"))
            dve.wait_ge(*moved("decret"))
            for c in (0, 3):
                for i in range(4):
                    dve.wait_ge(*moved(f"qk0{c}{i}"))

            def decayed(t):
                dve.wait_ge(*moved(f"cum{t}"))
                ts = slice(t * P, (t + 1) * P)
                for kind, ex in ((0, exp_ret), (1, exp_gla)):
                    for dst, blk, sign in ((qd, 0, 0), (kd, 4, 1)):
                        src = qkT[:, blk + 2 * kind:blk + 2 * kind + 2, ts]
                        for dr in range(2):
                            last = v_.tensor_tensor(dst[:, 4 * dr + 2 * kind:4 * dr + 2 * kind + 2, ts], src,
                                                    ex[:, sign, 2 * dr:2 * dr + 2, :], ALU.mult)
                signal(last, kd_ready)

            decayed(0)
            for t in range(NT):
                if t + 1 < NT:
                    decayed(t + 1)
                states(t)

            def keep(name, dst, mask, n=4):
                ready(name)
                free(v_.copy_predicated(dst, mask.bitcast(I32).unsqueeze(1).to_broadcast([P, n, P]),
                                   bank_of(name, n)), name)

            dve.wait_ge(mix0_in, 80)
            finish_mod(0, 4, 12)
            for c in (2, 5):
                for t in range(NT):
                    dve.wait_ge(*moved(f"vg0{c}{t}"))

            def backward_scores(t):
                for half in range(2):
                    dve.wait_ge(*moved(f"sc{t}{half}0"))
                    keep(f"sc{t}{half}1", amask[:, 4 * half:4 * half + 4, :], cst("win1"))

            backward_scores(0)
            for t in range(NT):
                if t + 1 < NT:
                    backward_scores(t + 1)
                for half in range(2):
                    dve.wait_ge(sq_ready, 2 * t + half + 1)
                    step(v_.tensor_reduce(hsum[:, 4 * half:4 * half + 4],
                                          (sqb, la)[half].rearrange("p (h d) -> p h d", h=4), AX.X, ALU.add))
                root(v_.tensor_scalar(hsum, hsum, 1.0 / P, RMS_EPS, ALU.mult, ALU.add), hsum)
                for half in range(2):
                    o = ready(f"o{t}{half}").rearrange("p (h d) -> p h d", h=4)
                    rate = hsum[:, 4 * half:4 * half + 4].unsqueeze(2).to_broadcast([P, 4, P])
                    free(v_.tensor_tensor(sq, o, rate, ALU.mult), f"o{t}{half}")
                    dve.wait_ge(*moved(f"o{t}{half}"))
                    step(v_.tensor_tensor(sq[:, 2:4], sq[:, 2:4], normg.unsqueeze(1).to_broadcast([P, 2, P]), ALU.mult))
                    gs = gtok[:, t, :].rearrange("p (h j d) -> p h j d", j=2, d=P)[:, :, half, :]
                    signal(v_.tensor_tensor(gs, gs, sq, ALU.mult), y_ready)
            for t in range(NT):
                residual_norm(0, "out", t)
            modulate("mlp0")
            mlp(0, range(NT))

            modulate("mix1")
            for t in range(NT):
                move(f"v1{t}", v1[:, t, :], bank(f"v1{t}")[:, 0:T])
            dve.wait_ge(rope_in, 16)
            cos = rope[:, 0:1, :].to_broadcast([P, 2, T])
            sin = rope[:, 1:2, :].to_broadcast([P, 2, T])
            for b in range(5):
                o = ready(f"rot{b}")
                src = q_raw[:, 2 * b:2 * b + 2, :] if b < 4 else k_raw
                dst = qT[:, 2 * b:2 * b + 2, :] if b < 4 else kT[:, :, T:2 * T]
                rt3 = rope_t.rearrange("p (a n) -> p a n", a=2)
                free(v_.tensor_tensor(rt3, bank_of(f"rot{b}", 2), sin, ALU.mult), f"rot{b}")
                for n in ([f"q1{b // 2}{b % 2}"] if b < 4 else ["k10", "k11"]):
                    dve.wait_ge(*moved(n))
                step(v_.tensor_tensor(src, src, cos, ALU.mult))
                dve.wait_ge(*moved(f"rot{b}"))
                signal(v_.tensor_tensor(dst, src, rt3, ALU.add), roped)
            dve.wait_ge(roped, 5)
            signal(v_.tensor_copy(kTx[0:HD], kT[HD:P]), roped)
            signal(v_.tensor_copy(kTx[HD:P], kT[0:HD]), roped)
            dve.wait_ge(sink_in, 16)

            def maxima(n):
                i, g = divmod(n, 4)
                for a in range(4):
                    step(v_.tensor_reduce(mx1[:, a:a + 1], ready(f"lg1{i}{g}{a}"), AX.X, ALU.max))
                step(v_.scalar_tensor_tensor(mx1, mx1, HD ** -0.5, sinkb[:, 4 * g:4 * g + 4], ALU.mult, ALU.max))
                step(v_.tensor_tensor(sexp1[:, n % 2, :], sinkb[:, 4 * g:4 * g + 4], mx1, ALU.subtract))
                signal(v_.tensor_scalar(negm1[:, n % 2, :], mx1, -1.0, None, ALU.mult), negm_ready)

            maxima(0)
            for i in range(2):
                for g in range(4):
                    n = 4 * i + g
                    if n < 7:
                        maxima(n + 1)
                    if n > 0:
                        dve.wait_ge(bank_full, full(f"o1{(n - 1) // 4}{(n - 1) % 4}"))
                    for a in (1, 3):
                        move(f"eT1{i}{g}{a}", eT1[:, a, :])
                    dve.wait_ge(sexp_ready, n + 1)
                    den = den1[:, 4 * n:4 * n + 4]
                    step(v_.tensor_tensor(den, den, sexp1[:, n % 2, :], ALU.add))
                    step(v_.reciprocal(den, den))
                    name = f"o1{i}{g}"
                    o = ready(name)[:, 0:T].rearrange("p (h d) -> p h d", h=4)
                    free(v_.tensor_tensor(y1[:, i, g * T:(g + 1) * T].rearrange("p (h d) -> p h d", h=4), o,
                                     den.unsqueeze(2).to_broadcast([P, 4, HD]), ALU.mult), name)
            for t in (2, 3):
                residual_norm(1, "out", t)
            modulate("mlp1")
            mlp(1, (2, 3))

            step(v_.tensor_tensor(lbc, cols[:, 88:92], cols[:, 92:96], ALU.subtract))
            signal(v_.tensor_copy(olb, lbc), lbd_ready)
            modulate("mix2")
            dve.wait_ge(lbs_ready, 1)
            step(v_.tensor_scalar(olb, lbc, -1.0, 1.0, ALU.mult, ALU.add))
            step(v_.tensor_scalar(mod3[:, 0:4], olb, -1.0, None, ALU.mult))
            for b in range(2):
                dve.wait_ge(*moved(f"f20{b}"))
                dve.wait_ge(*moved(f"f21{b}"))
            for h in range(4):
                last = v_.tensor_scalar(rkT[:, h, :], rsig[:, h, :], mod3[:, h:h + 1], olb[:, h:h + 1], ALU.mult, ALU.add)
            signal(last, kln_ready)
            dve.wait_ge(kln_ready, 1)
            for h in range(4):
                last = v_.tensor_scalar(rsig[:, h, :], rsig[:, h, :], olb[:, h:h + 1], lbc[:, h:h + 1], ALU.mult, ALU.add)
            signal(last, rfs_ready)
            dve.wait_ge(l2_in, 160)
            for t in range(2):
                name = f"t28{t}"
                o = ready(name)
                step(v_.bn_stats(ik_st, o[:, 0:HD]))
                step(v_.bn_aggr(ik_ag, ik_st))
                root(v_.tensor_scalar(lnr, ik_ag[:, 1:2], RMS_EPS, None, ALU.add), lnr)
                step(v_.tensor_scalar(ikd[:, t, 0:HD], o[:, 0:HD], ik_ag[:, 0:1], lnr, ALU.subtract, ALU.mult))
                step(v_.tensor_tensor(ikd[:, t, 0:HD], ikd[:, t, 0:HD], ikn[:, 0:HD], ALU.mult))
                step(v_.tensor_tensor(ikd[:, t, 0:HD], ikd[:, t, 0:HD], ikn[:, HD:P], ALU.add))
                free(v_.tensor_scalar(iwt[:, t, :], o[:, HD:HD + 8], 8.0 ** -0.5, None, ALU.mult), name)
                dve.wait_ge(*moved(name))
                signal(v_.tensor_copy(ikd[:, t, HD:P], ikd[:, t, 0:HD]), ik_ready)
            free(v_.tensor_copy(relE[0:8, 0:2 * T - 1], ready("rel")[0:8, 0:2 * T - 1]), "rel")
            dve.wait_ge(lev_in, 16)
            dve.wait_ge(lf_ready, 1)
            step(v_.tensor_tensor_scan(rb.rearrange("p a b -> p (a b)"), levels[:, len(LEVELS) * P:],
                                       rsig.rearrange("p a b -> p (a b)"), 0.0, ALU.mult, ALU.add))
            dve.sem_inc(sc_ready, 1)

            def index_scores(i, pairs):
                for b in pairs:
                    dve.wait_ge(*moved(f"ix{i}{b}"))
                    for j in range(2):
                        head = 4 * (b // 2) + 2 * j + b % 2
                        w = iwt[:, i, head:head + 1]
                        if b == 0 and j == 0:
                            last = v_.tensor_scalar(score[:, i, :], sc_r[:, j, :], w, None, ALU.mult)
                        else:
                            last = v_.scalar_tensor_tensor(score[:, i, :], sc_r[:, j, :], w, score[:, i, :],
                                                           ALU.mult, ALU.add)
                        if j == 0:
                            step(last)
                        else:
                            signal(last, sc_ready)
                            dve.wait_ge(sc_ready, 4 * i + b + 2)

            def top_keys(i, rounds):
                for r in rounds:
                    if r == 0:
                        if i == 0:
                            v_.memset(score[0:64, 0, 64:T], INADMISSIBLE)
                            step(v_.memset(score[64:P, 0, P:T], INADMISSIBLE))
                        else:
                            step(v_.memset(score[0:64, 1, 192:T], INADMISSIBLE))
                    cur = score[:, i, :] if r == 0 else work[:, i, :]
                    step(v_.max(max8, cur))
                    step(v_.match_replace(work[:, i, :], max8, cur, TAKEN))
                if rounds[-1] == 7:
                    step(v_.tensor_scalar(negsel[:, i, :], work[:, i, :], TAKEN, 1.0, ALU.is_equal, ALU.subtract))

            def head_norms(n):
                for t in range(2):
                    dst = (aq, ak)[n][:, t, :]
                    name = f"t2{4 + n}{t}"
                    free(v_.tensor_copy(dst, ready(name)), name)
                    dve.wait_ge(*moved(name))
                    head_rate(dst, 8, st8, sq2, HD)
                    d3 = dst.rearrange("p (h d) -> p h d", h=8)
                    step(v_.tensor_tensor(d3, d3, st8.unsqueeze(2).to_broadcast([P, 8, HD]), ALU.mult))
                    signal(v_.tensor_tensor(d3, d3, qkg[:, n * HD:(n + 1) * HD].unsqueeze(1).to_broadcast([P, 8, HD]),
                                            ALU.mult), aqk_ready)

            def keep_level(n):
                for t in range(2):
                    keep(f"lev{n}{t}", amat[:, t], levels[:, n * P:(n + 1) * P])

            dve.wait_ge(amat_zero, 1)
            flat = rb.rearrange("p a b -> p (a b)")
            for n in range(len(LEVELS) + 1):
                ed = edecs[n % 2]
                eflat = ed.rearrange("p a b -> p (a b)")
                if n > 1:
                    dve.wait_ge(kl_ready, n - 1)
                if n < len(LEVELS):
                    L = LEVELS[n]
                    s4 = flat.rearrange("p (b h n) -> p b h n", h=2, n=L)
                    d4 = eflat.rearrange("p (b h n) -> p b h n", h=2, n=L)
                    mid = s4[:, :, 0, L - 1:L].to_broadcast([P, 4 * T // (2 * L), L])
                    v_.tensor_tensor(d4[:, :, 0, :], mid, s4[:, :, 0, :], ALU.subtract)
                    signal(v_.tensor_tensor(d4[:, :, 1, :], s4[:, :, 1, :], mid, ALU.subtract), diff_ready)
                else:
                    v_.tensor_tensor(ed[:, :, 0:P], rb[:, :, P - 1:P].to_broadcast([P, 4, P]), rb[:, :, 0:P], ALU.subtract)
                    signal(v_.tensor_copy(ed[:, :, P:T], rb[:, :, P:T]), diff_ready)
                if n < 4:
                    index_scores(n // 2, (0, 1) if n % 2 == 0 else (2, 3))
                if n in (2, 3):
                    top_keys(0, range(3 * (n - 2), 3 * (n - 1)))
                elif n == 4:
                    top_keys(0, range(6, 8))
                elif n > 4:
                    top_keys(1, range(3 * (n - 5), min(8, 3 * (n - 4))))
                dve.wait_ge(edec_ready, n + 1)
                if n > 1:
                    dve.wait_ge(bank_full, full(f"lev{n - 2}1"))
                signal(v_.tensor_tensor(qls[n % 2], rqT, ed, ALU.mult), ql_ready)
                if n > 0:
                    keep_level(n - 1)
                if n < 2:
                    head_norms(n)
                elif n < 4:
                    for t in range(2):
                        move(f"t2{W_IN_BESIDE[n]}{t}", (rv, av)[n - 2][:, t, :])
            for t in range(2):
                keep(f"lev{len(LEVELS)}{t}", amat[:, t], ident)
            move("across", across, bank_of("across", 4))
            dve.wait_ge(rowg_in, 32)
            for t in range(2):
                dve.wait_ge(*moved(f"t23{t}"))

            def recurrent_out(t):
                name = f"ro{t}"
                o = ready(name)
                m = mix[:, t, 0:512]
                m3 = m.rearrange("p (h d) -> p h d", h=4)
                free(v_.tensor_copy(m, o), name)
                dve.wait_ge(*moved(name))
                head_rate(m, 4, st8[:, 0:4], ubuf3, P)
                step(v_.tensor_tensor(m3, m3, st8[:, 0:4].unsqueeze(2).to_broadcast([P, 4, P]), ALU.mult))
                step(v_.tensor_tensor(m, m, rowg[:, 0, :], ALU.mult))
                signal(v_.tensor_tensor(m, m, rg[:, t, :], ALU.mult), mix_ready)

            def masked_logits(i):
                logit = logits[i]
                dve.wait_ge(rel_in, 16 * (i + 1))
                if i == 1:
                    dve.wait_ge(bank_full, full("across"))
                signal(v_.scalar_tensor_tensor(logit, negsel[:, i, :].unsqueeze(1).to_broadcast([P, 8, T]), -NEG,
                                               biasT[:, :, ::-1], ALU.mult, ALU.add), bias_used)
                for b in range(4):
                    name = f"lg2{i}{b}"
                    ready(name)
                    pair = logit.rearrange("p (m n j) k -> p m n j k", n=2, j=2)[:, b // 2, :, b % 2, :]
                    free(v_.scalar_tensor_tensor(pair, bank_of(name, 2), HD ** -0.5, pair, ALU.mult, ALU.add), name)
                dve.wait_ge(*moved(f"lg2{i}3"))
                step(v_.tensor_reduce(mx2, logit, AX.X, ALU.max))
                signal(v_.tensor_scalar(neg2[:, i, :], mx2, -1.0, None, ALU.mult), neg2_ready)

            recurrent_out(0)
            masked_logits(0)
            recurrent_out(1)
            masked_logits(1)
            for i in range(2):
                dve.wait_ge(e2_ready, 8 * (i + 1))
                step(v_.reciprocal(den2[:, i, :], den2[:, i, :]))
                name = f"att{i}"
                o = ready(name)
                m = mix[:, i, 512:D]
                m3 = m.rearrange("p (h d) -> p h d", h=8)
                free(v_.tensor_tensor(m3, o.rearrange("p (h d) -> p h d", h=8),
                                      den2[:, i, :].unsqueeze(2).to_broadcast([P, 8, HD]), ALU.mult), name)
                dve.wait_ge(*moved(name))
                head_rate(m, 8, st8, ubuf3, HD)
                step(v_.tensor_tensor(m3, m3, st8.unsqueeze(2).to_broadcast([P, 8, HD]), ALU.mult))
                signal(v_.tensor_tensor(m, m, rowg[:, 1, :], ALU.mult), mix_ready)
            for t in range(2):
                for half in range(2):
                    residual(2, "out2", half, (X0 + t,), alpha=1.0)
                rms_row(t)
            modulate("moe")
            o = ready("router")
            free(v_.tensor_tensor(lg, o[:, 0:40].rearrange("p (t e) -> p t e", t=2),
                             brr.unsqueeze(1).to_broadcast([P, 2, 20]), ALU.add), "router")
            dve.wait_ge(*moved("router"))
            pick = cst("pick")
            four = lambda a: a.unsqueeze(1).to_broadcast([P, 2, 4])
            each = lambda a: a.unsqueeze(2).to_broadcast([P, 2, 4])

            def first_largest(vals, top, hot):
                step(v_.tensor_reduce(top, vals, AX.X, ALU.max))
                step(v_.tensor_tensor(hot, vals, each(top), ALU.is_equal))
                step(v_.tensor_tensor(hot, hot, four(pick), ALU.mult))
                step(v_.tensor_reduce(rt_m, hot, AX.X, ALU.max))
                step(v_.tensor_tensor(hot, hot, each(rt_m), ALU.is_equal))

            first_largest(lg[:, :, 0:4], rt_g, rt_hg)
            prod = rt_p.rearrange("p (t g e) -> p t g e", t=2, g=4)
            e4 = lg[:, :, 4:20].rearrange("p t (g e) -> p t g e", g=4)
            for t in range(2):
                step(v_.tensor_tensor(prod[:, t], e4[:, t], rt_hg[:, t].unsqueeze(2).to_broadcast([P, 4, 4]), ALU.mult))
                step(v_.tensor_reduce(rt_e[:, t], prod[:, t].rearrange("p g e -> p e g"), AX.X, ALU.add))
            first_largest(rt_e, rt_1, rt_h1)
            step(v_.scalar_tensor_tensor(rt_e2, rt_h1, INADMISSIBLE, rt_e, ALU.mult, ALU.add))
            first_largest(rt_e2, rt_2, rt_h2)
            rt_x4 = rt_exp.rearrange("p (t e) -> p t e", t=2)
            step(v_.tensor_tensor(rt_x4[:, :, 0:4], lg[:, :, 0:4], each(rt_g), ALU.subtract))
            signal(v_.tensor_tensor(rt_x4[:, :, 4], rt_2, rt_1, ALU.subtract), route_ready)
            dve.wait_ge(route_exp, 1)
            step(v_.tensor_reduce(rt_g, rt_x4[:, :, 0:4], AX.X, ALU.add))
            step(v_.reciprocal(rt_g, rt_g))
            step(v_.tensor_scalar(rt_1, rt_x4[:, :, 4], 1.0, None, ALU.add))
            step(v_.reciprocal(rt_1, rt_1))
            step(v_.tensor_tensor(rt_1, rt_1, rt_g, ALU.mult))
            step(v_.tensor_tensor(rt_2, rt_1, rt_x4[:, :, 4], ALU.mult))
            step(v_.tensor_tensor(rt_h1, rt_h1, each(rt_1), ALU.mult))
            step(v_.tensor_tensor(rt_h2, rt_h2, each(rt_2), ALU.mult))
            step(v_.tensor_tensor(rt_h1, rt_h1, rt_h2, ALU.add))
            c4 = comb.rearrange("p t (g e) -> p t g e", g=4)
            for t in range(2):
                step(v_.tensor_tensor(c4[:, t], rt_h1[:, t].unsqueeze(1).to_broadcast([P, 4, 4]),
                                      rt_hg[:, t].unsqueeze(2).to_broadcast([P, 4, 4]), ALU.mult))
            for q in range(4):
                signal(v_.memset(yacc[:, q % 2, (q // 2) * 512:(q // 2 + 1) * 512], 0.0), yacc_step)
            base = bank_no["moe"]
            with dve.Fori(0, TURNS) as turn_no:
                for j in range(BODY):
                    for u in range(4):
                        b = (base + 8 * j + u) % BANKS
                        dve.wait_ge(sg_ready, turn_no * (4 * BODY) + (4 * j + u + 1))
                        dve.wait_ge(bank_full, turn_no * MOE_BANKS + (base + 8 * (j - 1)))
                        v_.tensor_tensor(he[:, j % 2, u, :], psum[:, b, T:2 * T], sg[:, j % 2, u, :],
                                         ALU.mult).then_inc(bank_freed[b], 1)
                    for q in range(4):
                        i = base + 8 * j + 4 + q
                        n, t = q // 2, q % 2
                        y = yacc[:, t, n * 512:(n + 1) * 512]
                        dve.wait_ge(bank_full, turn_no * MOE_BANKS + (i + 1))
                        dve.wait_ge(yacc_step, turn_no * (4 * BODY) + (4 * j + q + 1))
                        step_bank = psum[:, i % BANKS, :]
                        v_.scalar_tensor_tensor(y, step_bank, comb[:, t, bass.ds(turn_no * BODY + j, 1)], y,
                                                ALU.mult, ALU.add).then_inc(yacc_step, 1)
                        dve.wait_ge(yacc_step, turn_no * (4 * BODY) + (4 * j + q + 5))
                        dve.sem_inc(bank_freed[i % BANKS], 1)
            for c in range(2):
                dve.wait_ge(*moved(f"gate21{c}1"))
            for t in range(2):
                step(v_.tensor_tensor(yacc[:, t, :], yacc[:, t, :], gate[:, 1, :], ALU.mult))
                step(v_.tensor_tensor(xres[:, X0 + t, :], xres[:, X0 + t, :], yacc[:, t, :], ALU.add))
            for t in range(2):
                signal(v_.tensor_copy(junk, const[:, 0:1]), final_ready)


_INS = ["x", "c", "ctx", "c_ctx", "w_mod", "b_mod", "ln_g", "ln_b", "mlp_w1", "mlp_w2", "ev_w_in", "ev_ret_theta",
        "ev_gla_gk_w", "ev_gla_gk_b", "ev_gla_norm_g", "ev_w_out", "od_w_qkv", "od_sink", "od_w_out", "c_2",
        "w_ada_2", "b_ada_2", "norm1_g_2", "norm2_g_2", "w_in_2", "lb_logits_2", "rec_out_g_2", "q_norm_g_2",
        "k_norm_g_2", "idx_k_norm_g_2", "idx_k_norm_b_2", "attn_out_g_2", "rel_bias_2", "w_out_2", "w_rg_2",
        "b_rg_2", "w_re_2", "b_re_2", "w1_2", "w3_2", "w2_2"]


def kernel(**inputs):
    import numpy as _np
    import concourse.bacc as _bacc
    from concourse import mybir as _mybir
    from concourse.bass_utils import run_bass_kernel_spmd as _run

    nc = _bacc.Bacc("TRN2", target_bir_lowering=False, num_devices=1)
    arrays, aps = {}, {}
    for name, a in {**{n: inputs[n] for n in _INS}, **shape_constants()}.items():
        a = _np.ascontiguousarray(a)
        arrays[f"in_{name}"] = a
        aps[name] = nc.dram_tensor(f"in_{name}", a.shape, _mybir.dt.from_np(a.dtype), kind="ExternalInput").ap()
    out = nc.dram_tensor("out_x", (1, T, D), F32, kind="ExternalOutput").ap()
    build(nc, aps, out)
    r = _run(nc, [arrays], core_ids=[0])
    return r.results[0]["out_x"]
```
